# Optimizing a Trainium2 kernel written in Bass

```python
import math
import jax, jax.numpy as jnp
from jax import lax
import numpy as np

D_MODEL = 1024
BATCH = 1
SEQ = 256
DEPTH = 1
DEC_BATCH = 8
DEC_SEQ = 1
PAST_LEN = 2048
PAGE_SIZE = 128

N_META = 16
D_MIX = 2 * D_MODEL
D_SSM = D_MIX // 2
D_CONF = D_MIX - D_SSM
SSD_HEAD_DIM = 64
SSD_HEADS = D_SSM // SSD_HEAD_DIM
SSD_GROUPS = 2
SSD_STATE = 128
SSD_CONV = 4
SSD_CONV_DIM = D_SSM + 2 * SSD_GROUPS * SSD_STATE
CHUNK = 128
CONF_WIDTH = 31
N_EXPERTS = 32
TOP_K = 4
D_FF = D_MODEL
SWIGLU_LIMIT = 7.0
SWIGLU_ALPHA = 1.702
MOE_BLOCK = 128
EPS = 1e-5
D_IN_PROJ = D_SSM + SSD_CONV_DIM + SSD_HEADS + 2 * D_CONF

kernel_name = 'hymba_ssd_conformer_moe_step'

F32 = jnp.float32

def rmsnorm(x, g):
    xf = x.astype(F32)
    r = xf * lax.rsqrt(jnp.mean(xf * xf, axis=-1, keepdims=True) + EPS)
    return (r * g.astype(F32)).astype(x.dtype)

def layernorm(x, g, b):
    xf = x.astype(F32)
    mu = jnp.mean(xf, axis=-1, keepdims=True)
    var = jnp.mean(jnp.square(xf - mu), axis=-1, keepdims=True)
    return ((xf - mu) * lax.rsqrt(var + EPS) * g.astype(F32) + b.astype(F32)).astype(x.dtype)

def causal_dwconv(seq, hist, w, b):
    full = jnp.concatenate([hist.astype(seq.dtype), seq], axis=1)
    k = w.shape[0]
    out = lax.conv_general_dilated(full, w[:, None, :].astype(seq.dtype), (1,), 'VALID',
                                   dimension_numbers=('NWC', 'WIO', 'NWC'),
                                   feature_group_count=seq.shape[-1])
    return out + b.astype(seq.dtype), full[:, full.shape[1] - (k - 1):]

def ssd_chunked(x, dt, a, bm, cm, h0, front_pad):
    b, length, n_heads, p = x.shape
    g, n = bm.shape[2], bm.shape[3]
    r = n_heads // g
    total = length + front_pad
    q = min(CHUNK, total)
    end_pad = (-total) % q
    nc = (total + end_pad) // q

    def pad(t):
        return jnp.pad(t.astype(F32), [(0, 0), (front_pad, end_pad)] + [(0, 0)] * (t.ndim - 2))

    x = pad(x).reshape(b, nc, q, g, r, p)
    dt = pad(dt).reshape(b, nc, q, g, r)
    bm = pad(bm).reshape(b, nc, q, g, n)
    cm = pad(cm).reshape(b, nc, q, g, n)
    a_cum = jnp.cumsum(dt * a.astype(F32).reshape(g, r), axis=2)
    xdt = x * dt[..., None]
    causal = jnp.tril(jnp.ones((q, q), dtype=bool))[:, :, None, None]
    seg = a_cum[:, :, :, None] - a_cum[:, :, None, :]
    decay_ls = jnp.exp(jnp.where(causal, seg, -jnp.inf))
    cb = jnp.einsum('bclgn,bcsgn->bclsg', cm, bm)
    y_diag = jnp.einsum('bclsg,bclsgr,bcsgrp->bclgrp', cb, decay_ls, xdt)
    decay_to_end = jnp.exp(a_cum[:, :, -1:] - a_cum)
    chunk_states = jnp.einsum('bcsgn,bcsgr,bcsgrp->bcgrpn', bm, decay_to_end, xdt)
    chunk_decay = jnp.exp(a_cum[:, :, -1])

    def step(h, inp):
        s, d = inp
        return d[..., None, None] * h + s, h

    h_final, h_enter = lax.scan(step, h0.astype(F32).reshape(b, g, r, p, n),
                                (jnp.moveaxis(chunk_states, 1, 0), jnp.moveaxis(chunk_decay, 1, 0)))
    h_enter = jnp.moveaxis(h_enter, 0, 1)
    y_off = jnp.einsum('bclgn,bcgrpn,bclgr->bclgrp', cm, h_enter, jnp.exp(a_cum))
    y = (y_diag + y_off).reshape(b, nc * q, n_heads, p)[:, front_pad:front_pad + length]
    return y, h_final.reshape(b, n_heads, p, n)

def mixer_groups(u, ssm0, ssd_hist, conf_hist, front_pad, w_in, conv_ssd_w, conv_ssd_b, dt_bias,
                 a_log, d_skip, g_ssd_norm, conv_conf_w, conv_conf_b, ln_conf_g, ln_conf_b, w_out):
    b, length, _ = u.shape
    proj = u @ w_in
    z, xbc, dt_raw, glu_in = jnp.split(
        proj, [D_SSM, D_SSM + SSD_CONV_DIM, D_SSM + SSD_CONV_DIM + SSD_HEADS], axis=-1)
    xbc, ssd_hist_new = causal_dwconv(xbc, ssd_hist, conv_ssd_w, conv_ssd_b)
    xbc = jax.nn.silu(xbc)
    xs, bm, cm = jnp.split(xbc, [D_SSM, D_SSM + SSD_GROUPS * SSD_STATE], axis=-1)
    xs = xs.reshape(b, length, SSD_HEADS, SSD_HEAD_DIM)
    bm = bm.reshape(b, length, SSD_GROUPS, SSD_STATE)
    cm = cm.reshape(b, length, SSD_GROUPS, SSD_STATE)
    dt = jax.nn.softplus(dt_raw.astype(F32) + dt_bias.astype(F32))
    a = -jnp.exp(a_log.astype(F32))
    y, ssm_new = ssd_chunked(xs, dt, a, bm, cm, ssm0, front_pad)
    y = y + xs.astype(F32) * d_skip.astype(F32)[:, None]
    grp = (b, length, SSD_GROUPS, D_SSM // SSD_GROUPS)
    y = y.reshape(grp) * jax.nn.silu(z.astype(F32)).reshape(grp)
    y = rmsnorm(y, g_ssd_norm.reshape(SSD_GROUPS, -1)).reshape(b, length, D_SSM).astype(u.dtype)
    val, gate = jnp.split(glu_in, 2, axis=-1)
    c = val * jax.nn.sigmoid(gate)
    c, conf_hist_new = causal_dwconv(c, conf_hist, conv_conf_w, conv_conf_b)
    c = jax.nn.silu(layernorm(c, ln_conf_g, ln_conf_b))
    out = jnp.concatenate([y, c], axis=-1) @ w_out
    return out, ssm_new.astype(ssm0.dtype), ssd_hist_new, conf_hist_new

def moe_ffn(u, w_router, b_router, w_gate, b_gate, w_up, b_up, w_down, b_down):
    lead = u.shape[:-1]
    xf = u.reshape(-1, D_MODEL)
    t = xf.shape[0]
    logits = (xf @ w_router + b_router).astype(F32)
    top_val, top_idx = lax.top_k(logits, TOP_K)
    gates = jax.nn.softmax(top_val, axis=-1).astype(u.dtype)
    n_assign = t * TOP_K
    e_flat = top_idx.reshape(-1)
    tok_flat = jnp.arange(n_assign, dtype=jnp.int32) // TOP_K
    g_flat = gates.reshape(-1)
    counts = jnp.bincount(e_flat, length=N_EXPERTS)
    padded = (counts + MOE_BLOCK - 1) // MOE_BLOCK * MOE_BLOCK
    pad_end = jnp.cumsum(padded)
    pad_start = pad_end - padded
    raw_start = jnp.cumsum(counts) - counts
    order = jnp.argsort(e_flat)
    e_sorted = e_flat[order]
    dest = pad_start[e_sorted] + jnp.arange(n_assign) - raw_start[e_sorted]
    n_blocks = -(-n_assign // MOE_BLOCK) + N_EXPERTS
    rows = n_blocks * MOE_BLOCK
    buf_tok = jnp.full((rows,), t, dtype=jnp.int32).at[dest].set(tok_flat[order])
    buf_gate = jnp.zeros((rows,), u.dtype).at[dest].set(g_flat[order])
    block_expert = jnp.minimum(
        jnp.searchsorted(pad_end, jnp.arange(n_blocks) * MOE_BLOCK, side='right'), N_EXPERTS - 1)
    xb = jnp.concatenate([xf, jnp.zeros((1, D_MODEL), xf.dtype)], axis=0)[buf_tok]
    xb = xb.reshape(n_blocks, MOE_BLOCK, D_MODEL)

    def expert_rows(args):
        xblk, e = args
        gt = jnp.minimum(xblk @ w_gate[e] + b_gate[e], SWIGLU_LIMIT)
        up = jnp.clip(xblk @ w_up[e] + b_up[e], -SWIGLU_LIMIT, SWIGLU_LIMIT)
        hdn = (up + 1.0) * gt * jax.nn.sigmoid(gt * SWIGLU_ALPHA)
        return hdn @ w_down[e] + b_down[e]

    yb = lax.map(expert_rows, (xb, block_expert)).reshape(rows, D_MODEL)
    out = jnp.zeros((t + 1, D_MODEL), u.dtype).at[buf_tok].add(yb * buf_gate[:, None])[:t]
    return out.reshape(*lead, D_MODEL)

def decoder_layer(h, ssm0, ssd_hist, conf_hist, front_pad, g_mix, g_ffn, mix_w, moe_w):
    mixed, ssm_new, ssd_new, conf_new = mixer_groups(rmsnorm(h, g_mix), ssm0, ssd_hist, conf_hist,
                                                     front_pad, *mix_w)
    h = h + mixed
    h = h + moe_ffn(rmsnorm(h, g_ffn), *moe_w)
    return h, ssm_new, ssd_new, conf_new

def setup_inputs(seed: int = 0) -> dict:
    key = jax.random.key(seed)
    ks = jax.random.split(key, 32)
    nrm = jax.random.normal
    dt0 = jnp.exp(jax.random.uniform(ks[10], (DEPTH, SSD_HEADS), minval=math.log(1e-3), maxval=math.log(1e-1)))
    return {
        'x_prompt': nrm(ks[0], (BATCH, SEQ, D_MODEL), F32),
        'x_sample': nrm(ks[1], (DEC_BATCH, DEC_SEQ, D_MODEL), F32),
        'state_ssm': 0.5 * nrm(ks[2], (DEPTH, DEC_BATCH, SSD_HEADS, SSD_HEAD_DIM, SSD_STATE), F32),
        'state_ssd_conv': nrm(ks[3], (DEPTH, DEC_BATCH, SSD_CONV - 1, SSD_CONV_DIM), F32),
        'state_conf_conv': 0.5 * nrm(ks[4], (DEPTH, DEC_BATCH, CONF_WIDTH - 1, D_CONF), F32),
        'meta_tokens': nrm(ks[5], (N_META, D_MODEL), F32),
        'g_mix': 1.0 + 0.02 * nrm(ks[6], (DEPTH, D_MODEL), F32),
        'w_in': nrm(ks[7], (DEPTH, D_MODEL, D_IN_PROJ), F32) * D_MODEL ** -0.5,
        'conv_ssd_w': nrm(ks[8], (DEPTH, SSD_CONV, SSD_CONV_DIM), F32) * SSD_CONV ** -0.5,
        'conv_ssd_b': 0.02 * nrm(ks[9], (DEPTH, SSD_CONV_DIM), F32),
        'dt_bias': dt0 + jnp.log(-jnp.expm1(-dt0)),
        'a_log': jnp.log(jax.random.uniform(ks[11], (DEPTH, SSD_HEADS), minval=1.0, maxval=16.0)),
        'd_skip': 1.0 + 0.1 * nrm(ks[12], (DEPTH, SSD_HEADS), F32),
        'g_ssd_norm': 1.0 + 0.02 * nrm(ks[13], (DEPTH, D_SSM), F32),
        'conv_conf_w': nrm(ks[14], (DEPTH, CONF_WIDTH, D_CONF), F32) * CONF_WIDTH ** -0.5,
        'conv_conf_b': 0.02 * nrm(ks[15], (DEPTH, D_CONF), F32),
        'ln_conf_g': 1.0 + 0.02 * nrm(ks[16], (DEPTH, D_CONF), F32),
        'ln_conf_b': 0.02 * nrm(ks[17], (DEPTH, D_CONF), F32),
        'w_out': nrm(ks[18], (DEPTH, D_MIX, D_MODEL), F32) * D_MIX ** -0.5,
        'g_ffn': 1.0 + 0.02 * nrm(ks[19], (DEPTH, D_MODEL), F32),
        'w_router': nrm(ks[20], (DEPTH, D_MODEL, N_EXPERTS), F32) * D_MODEL ** -0.5,
        'b_router': 0.01 * nrm(ks[21], (DEPTH, N_EXPERTS), F32),
        'w_gate': nrm(ks[22], (DEPTH, N_EXPERTS, D_MODEL, D_FF), F32) * D_MODEL ** -0.5,
        'b_gate': 0.02 * nrm(ks[23], (DEPTH, N_EXPERTS, D_FF), F32),
        'w_up': nrm(ks[24], (DEPTH, N_EXPERTS, D_MODEL, D_FF), F32) * D_MODEL ** -0.5,
        'b_up': 0.02 * nrm(ks[25], (DEPTH, N_EXPERTS, D_FF), F32),
        'w_down': nrm(ks[26], (DEPTH, N_EXPERTS, D_FF, D_MODEL), F32) * D_FF ** -0.5,
        'b_down': 0.02 * nrm(ks[27], (DEPTH, N_EXPERTS, D_MODEL), F32),
        'g_final': 1.0 + 0.02 * nrm(ks[28], (D_MODEL,), F32),
    }

def reference(x_prompt, x_sample, state_ssm, state_ssd_conv, state_conf_conv, meta_tokens, g_mix,
              w_in, conv_ssd_w, conv_ssd_b, dt_bias, a_log, d_skip, g_ssd_norm, conv_conf_w,
              conv_conf_b, ln_conf_g, ln_conf_b, w_out, g_ffn, w_router, b_router, w_gate, b_gate,
              w_up, b_up, w_down, b_down, g_final):
    dtype = x_prompt.dtype
    bp = x_prompt.shape[0]
    meta = jnp.broadcast_to(meta_tokens.astype(dtype)[None], (bp, N_META, D_MODEL))
    h_p = jnp.concatenate([meta, x_prompt], axis=1)
    h_s = x_sample
    front_pad = (-N_META) % CHUNK
    ssm_p, ssdc_p, confc_p, ssm_s, ssdc_s, confc_s = [], [], [], [], [], []
    for l in range(DEPTH):
        mix_w = (w_in[l], conv_ssd_w[l], conv_ssd_b[l], dt_bias[l], a_log[l], d_skip[l], g_ssd_norm[l],
                 conv_conf_w[l], conv_conf_b[l], ln_conf_g[l], ln_conf_b[l], w_out[l])
        moe_w = (w_router[l], b_router[l], w_gate[l], b_gate[l], w_up[l], b_up[l], w_down[l], b_down[l])
        ssm0 = jnp.zeros((bp, SSD_HEADS, SSD_HEAD_DIM, SSD_STATE), state_ssm.dtype)
        ssd0 = jnp.zeros((bp, SSD_CONV - 1, SSD_CONV_DIM), dtype)
        conf0 = jnp.zeros((bp, CONF_WIDTH - 1, D_CONF), dtype)
        h_p, s1, s2, s3 = decoder_layer(h_p, ssm0, ssd0, conf0, front_pad, g_mix[l], g_ffn[l], mix_w, moe_w)
        ssm_p.append(s1)
        ssdc_p.append(s2)
        confc_p.append(s3)
        h_s, s1, s2, s3 = decoder_layer(h_s, state_ssm[l], state_ssd_conv[l], state_conf_conv[l], 0,
                                        g_mix[l], g_ffn[l], mix_w, moe_w)
        ssm_s.append(s1)
        ssdc_s.append(s2)
        confc_s.append(s3)
    y_prompt = rmsnorm(h_p, g_final)[:, N_META:]
    y_sample = rmsnorm(h_s, g_final)
    new_ssm_p = jnp.stack(ssm_p, axis=0)
    new_ssdc_p = jnp.stack(ssdc_p, axis=0)
    new_confc_p = jnp.stack(confc_p, axis=0)
    new_ssm_s = jnp.stack(ssm_s, axis=0)
    new_ssdc_s = jnp.stack(ssdc_s, axis=0)
    new_confc_s = jnp.stack(confc_s, axis=0)
    return (y_prompt, y_sample, new_ssm_p, new_ssdc_p, new_confc_p, new_ssm_s, new_ssdc_s, new_confc_s)


_drawn_inputs = setup_inputs


def setup_inputs(seed=0):
    import zlib

    import numpy as np

    out = dict(_drawn_inputs(seed))
    spreads = {}
    factors = {'ln_conf_g': 11.937,
     'b_gate': 7.684,
     'b_up': 23.772,
     'b_down': 7.214,
     'g_final': 7.231,
     'g_ssd_norm': 3.543,
     'ln_conf_b': 10.911,
     'b_router': 11.005,
     'g_ffn': 3.234}
    for name, (base, spread) in spreads.items():
        noise = np.random.default_rng([zlib.crc32(name.encode()), seed]).standard_normal(out[name].shape)
        drawn = base * np.exp(spread * noise) if base else spread * noise
        out[name] = __import__('jax').numpy.asarray(drawn.astype(out[name].dtype))
    for name, factor in factors.items():
        out[name] = (out[name] * factor).astype(out[name].dtype)
    return out
```

```python
from contextlib import ExitStack

import concourse.bass as bass
from concourse import mybir
from concourse.alu_op_type import AluOpType as ALU

F32 = mybir.dt.float32
I32 = mybir.dt.int32
U32 = mybir.dt.uint32
ACT = mybir.ActivationFunctionType
AX = mybir.AxisListType.X

P = 128
D = 1024
KT = D // P
META, SEQ, NB = 16, 256, 8
TP = META + SEQ
T = TP + NB
TN = SEQ + NB
HEADS, HD, NST, GROUPS = 16, 64, 128, 2
HPG = HEADS // GROUPS
XBC = D + 2 * GROUPS * NST
XT_ = XBC // P
CW, SW = 31, 4
NE, TOPK = 32, 4
CAP = 128
HALF = 64
OVER = (TN * TOPK) // (CAP + 1)
EPS = 1e-5
LIMIT, ALPHA = 7.0, 1.702
FAR = 4096.0

COL_Z, COL_X, COL_DT, COL_VAL, COL_GATE = 0, D, D + XBC, D + XBC + HEADS, 2 * D + XBC + HEADS


def build(nc, I, O):
    ctx = ExitStack()
    with ctx:
        def sb(name, n, dt=F32):
            return ctx.enter_context(nc.sbuf_tensor(name, [P, n], dt))

        def sem(name):
            return ctx.enter_context(nc.semaphore(name))

        def view(t, off, *dims):
            n = 1
            for d in dims:
                n *= d
            a = t[:, off:off + n]
            if len(dims) == 1:
                return a
            names = "abc"[:len(dims)]
            return a.rearrange("p (" + " ".join(names) + ") -> p " + " ".join(names),
                               **dict(zip(names, dims)))

        def flat(ap):
            names = " ".join("abcd"[:len(ap.shape) - 1])
            return ap.rearrange(f"p {names} -> p ({names})")

        def bc(ap, axis, n):
            a = ap.unsqueeze(axis)
            s = list(a.shape)
            s[axis] = n
            return a.to_broadcast(s)

        PIECE = 2 * D
        NP = 12
        ring = sb("ring", NP * PIECE)
        extra = sb("extra", 4 * PIECE)
        acts = sb("acts", 3072 + 2240 + 2480 + 3136 + 3360 + 2112)
        small = sb("small", 3480)
        ps = ctx.enter_context(nc.psum_tensor("ps", [P, 8, 512], F32))

        o = 0
        x_tok = view(acts, o, 3, D); o += 3072
        uT = view(acts, o, KT, T); st_off = o; o += 2240
        cbuf = view(acts, o, KT, 30 + T); yT = view(acts, o, KT, TN); o += 2480
        xs_tok = view(acts, o, 3, D); conv = view(acts, o, KT, TN); cstage = view(acts, o + 2112, D); o += 3136
        xa = view(acts, o, XT_, T); hist_x = view(acts, o, XBC); xn = view(acts, o, 3, D); o += 3360
        zT = view(acts, o, KT, TN); hist_c = view(acts, o, 2, D); accT = zT; o += 2112
        csq = view(acts, 3072 + 2240, KT, TN)
        state_in = view(acts, st_off, 2, KT, P)
        t0 = 8 * PIECE
        csmp = view(ring, t0, KT, NB, CW)
        sprod = view(ring, t0, KT, P)
        xsmp = view(ring, t0 + 1984, XT_, NB, SW)
        xraw = view(ring, t0 + 2368, XT_, 3 + T)
        xstage = view(ring, t0 + 5764, XBC)
        xsig = view(ring, t0 + 5764, 6, T)
        s0 = t0 + 2368
        Mh = view(ring, s0, HPG, P)
        Ce = view(ring, s0 + 1024, HPG, P)
        ysq = view(ring, s0, KT, TN)
        zsig = view(ring, s0, KT, TN)
        xdt = view(ring, s0 + 2112, HEADS, HD)
        xdec = view(ring, s0 + 3136, HEADS, HD)
        hT = view(ring, s0 + 4160, HEADS, HD)
        btok = view(ring, s0 + 5184, GROUPS, NST)
        cbm = view(ring, s0 + 5440, P)

        so = [0]

        def sm(*dims):
            n = 1
            for d in dims:
                n *= d
            v = view(small, so[0], *dims)
            so[0] += n
            return v

        ident, tri, tri_s, ones = sm(P), sm(P), sm(P), sm(P)
        r_ = t0 + 5764
        vrow = view(ring, r_, P)
        vcol = sm(108)
        cwrow, cwcol = view(ring, r_ + 128, 2, P), sm(CW, KT)
        bgrow, bgT = view(ring, r_ + 384, 2, P), sm(NE, KT)
        burow, buT = view(ring, r_ + 640, 2, P), sm(NE, KT)
        wdt, wr = sm(KT, HEADS), sm(KT, NE)
        brt, dtb, aneg, dsk = sm(NE), sm(HEADS), sm(HEADS), sm(KT)
        dtt, dta, dtw, dte, dtd = sm(4, HEADS), sm(4, HEADS), sm(4, HEADS), sm(4, HEADS), sm(4, HEADS)
        acum = sm(2, HEADS)
        dec, cdec = sm(HEADS), sm(HEADS)
        sgt = sm(2, T)
        stat = sm(4, 4)
        sdt, sdec = sm(KT, NB), sm(KT, NB)
        ysum = sm(KT)
        mu = sm(TN)
        assert so[0] <= 3480, so[0]
        gmx, gxb, gsn, gcb = vcol[:, 0:8], vcol[:, 8:20], vcol[:, 20:28], vcol[:, 28:36]
        glg, glb, gff, gxw = vcol[:, 36:44], vcol[:, 44:52], vcol[:, 52:60], vcol[:, 60:108]
        rstd = sgt[:, 0, :][:, 0:TN]
        rstd2 = sgt[:, 1, :][:, 0:TN]

        ge, sig = view(extra, 0, KT, CAP), view(extra, 1024, KT, CAP)
        ue, hdn = view(extra, 2048, KT, CAP), view(extra, 3072, KT, CAP)
        yTs, ys = view(extra, 4096, KT, CAP), view(extra, 5120, D)
        xg = view(extra, 6144, KT, CAP)
        S, Sg = view(extra, 7168, 3, CAP), view(extra, 7552, 3, CAP)
        m0 = 3072
        Pm = view(acts, m0, TN)
        bdn = view(acts, m0 + 264, D)
        gT = view(acts, m0 + 1288, TN)
        iota_f = view(acts, m0 + 1552, P)
        c0 = 5312
        slotp, gates = view(acts, c0, 3, NE + 2), view(acts, c0 + 102, 3, NE + 2)
        logit, top8 = view(acts, c0 + 204, 3, NE), view(acts, c0 + 300, 3, 8)
        topf, topw = view(acts, c0 + 324, 3, TOPK), view(acts, c0 + 336, 3, TOPK)
        eq, mask = view(acts, c0 + 348, TOPK, NE), view(acts, c0 + 476, 3, NE)
        tmp96 = view(acts, c0 + 572, 3, NE)
        cntf, nbo, cum = view(acts, c0 + 668, NE), view(acts, c0 + 700, NE), view(acts, c0 + 732, NE)
        ole, oe, ob = view(acts, c0 + 764, OVER, NE), view(acts, c0 + 1020, OVER + 1), view(acts, c0 + 1029, OVER)
        oslot = view(acts, c0 + 1037, 3)
        topi = view(acts, c0 + 1040, 3, 8).bitcast(U32)
        otab = view(acts, c0 + 1064, OVER + 1).bitcast(I32)
        zero32 = view(acts, c0 + 1073, NE)
        cnti = view(acts, c0 + 1111, NE + 1).bitcast(I32)
        rsum, nmax = view(acts, c0 + 1105, 3), view(acts, c0 + 1108, 3)
        hout = view(acts, 0, 3, D)
        gfin = view(acts, 7792, D)
        hsq = view(acts, 7792 + 1024, D)

        names = ("zeroed consts x_loaded x_tail vec_loaded bias_loaded hist_loaded misc_loaded wdt_loaded "
                 "ssq_ready rms_ready xs_ready vt_done vcol_ready xtr_done uT_ready htr_done hist_ready win_done "
                 "evac_done glu_done pad_ready dt_mm dt_ready dt_exp dt_v xst_tr xst_ready xst_out cst_tr "
                 "cst_ready kept_out conv_done mean_mm mu_ready cent_ready csq_ready var_mm var_ready std_ready "
                 "norm_ready csig_ready conf_ready xpre_ready xsig_ready xa_ready win_used z_sig acum_mm meta_exp "
                 "meta_v xtok_mm xdt_ready cb_mm cb_raw acb_mm d_ready e_ready ce_ready m_ready xdec_ready y_mm "
                 "st_mm y_ready hT_ready hT_tr hT_st hT_out sexp_mm sdec_ready st_in0 st_in1 sbc_mm sh_dec sh_bx "
                 "sh_new sh_prod sy_ready sh_out0 sh_out1 yg_ready ysq_ready yvar_mm yvar_ready ystd_ready "
                 "yn_ready wo_used wo_mm acc_ready h_tr hsq_ready hr_v hstd_ready xn_ready lg_mm nm_ready topexp "
                 "gates_ready pos_mm cnt_ready gt_ready late_loaded g_read xg_done "
                 "ytr_done pt_done sc_done g_ready u_read hdn_ready xg_ready yt_ready y_back p_ready acc_done "
                 "s_ready sg_ready sig_ready piece_used o_tab f_ready f_out f_rd iota_ready").split()
        ev = {n: sem(n) for n in names}
        landed = [sem(f"piece_landed{i}") for i in range(NP)]
        win_landed = [sem(f"win_landed{i}") for i in range(6)]
        wo_landed = [sem(f"wo_landed{i}") for i in range(4)]
        block = ctx.enter_context(nc.Block())

        CHUNKS = [(COL_VAL, "val", 0), (COL_GATE, "gate", 0), (COL_VAL + 512, "val", 4), (COL_GATE + 512, "gate", 4),
                  (COL_X, "xbc", 0), (COL_X + 512, "xbc", 4), (COL_X + 1024, "xbc", 8), (COL_Z, "z", 0), (COL_Z + 512, "z", 4)]
        PLACE = [(ring, 0), (ring, 4096), (ring, 8192), (ring, 12288), (extra, 0), (extra, 4096),
                 (ring, 0), (ring, 4096), (ring, 8192)]
        NC_ = len(CHUNKS)

        def win(c):
            return view(PLACE[c][0], PLACE[c][1], KT, 512)

        def wout(p):
            return view(extra, (p % 4) * PIECE, 2, D)

        def piece(p):
            return view(ring, p * PIECE, 2, D)

        WO_K = [8, 10, 12, 14, 0, 2, 4, 6]
        w_in, w_out = I["w_in"][0], I["w_out"][0]
        expert_w = [I[n] for n in ("w_gate", "w_up", "w_down")]

        def expert_piece(e, p):
            w = expert_w[p // 4]
            r = (p % 4) * 2 * P
            return w[0, bass.ds(e, 1), r:r + 2 * P, :].rearrange("o (k p) n -> p (o k) n", p=P)

        tok = [(0, P), (P, P), (2 * P, NB)]

        @block.sync
        def _(sp):
            xp, xs, mt = I["x_prompt"][0], I["x_sample"], I["meta_tokens"]
            sp.dma_start(x_tok[:, 0, :], xp[0:P]).then_inc(ev["x_loaded"], 16)
            sp.dma_start(x_tok[:, 1, :], xp[P:2 * P]).then_inc(ev["x_loaded"], 16)
            sp.wait_ge(ev["zeroed"], 1)
            sp.dma_start(x_tok[0:NB, 2, :], xs.rearrange("b o d -> (b o) d")).then_inc(ev["x_tail"], 16)
            sp.dma_start(x_tok[32:32 + META, 2, :], mt).then_inc(ev["x_tail"], 16)
            sp.dma_start(wdt, w_in[:, COL_DT:COL_DT + HEADS].rearrange("(k p) n -> p k n", p=P)).then_inc(ev["wdt_loaded"], 16)
            for c in range(NC_):
                if c >= 6:
                    sp.wait_ge(ev["win_used"], c - 5)
                sp.dma_start(win(c), w_in[:, CHUNKS[c][0]:CHUNKS[c][0] + 512].rearrange("(k p) n -> p k n", p=P)
                             ).then_inc(win_landed[c % 6], 16)

            def load_wout(p):
                sp.dma_start(wout(p), w_out[WO_K[p] * P:(WO_K[p] + 2) * P].rearrange("(k p) n -> p k n", p=P)
                             ).then_inc(wo_landed[p % 4], 16)

            sp.wait_ge(ev["win_used"], 6)
            for p in range(4):
                load_wout(p)
            sp.wait_ge(ev["win_used"], NC_)
            for b in range(2):
                sp.dma_start(state_in[:, b], I["state_ssm"][0, b].rearrange("h p n -> (h p) n").rearrange(
                    "(m q) n -> q m n", q=P)).then_inc((ev["st_in0"], ev["st_in1"])[b], 16)
            for p in range(8):
                sp.dma_start(piece(p), expert_piece(0, p)).then_inc(landed[p], 16)
            sp.wait_ge(ev["hT_st"], 1)
            sp.dma_start(O["ssm_p"][0, 0].rearrange("h p n -> (h p) n").rearrange("(m q) n -> q m n", q=P),
                         view(ring, s0 + 3136, KT, P)).then_inc(ev["hT_out"], 16)
            for b in range(NB):
                sp.wait_ge(ev["sh_new"], b + 1)
                sp.dma_start(O["ssm_s"][0, b].rearrange("h p n -> (h p) n").rearrange("(m q) n -> q m n", q=P),
                             state_in[:, b % 2]).then_inc((ev["sh_out0"], ev["sh_out1"])[b % 2], 16)
                if b + 2 < NB:
                    sp.wait_ge((ev["sh_out0"], ev["sh_out1"])[b % 2], 16 * (b // 2 + 1))
                    sp.wait_ge(ev["sh_prod"], b + 1)
                    sp.dma_start(state_in[:, b % 2], I["state_ssm"][0, b + 2].rearrange("h p n -> (h p) n").rearrange(
                        "(m q) n -> q m n", q=P)).then_inc((ev["st_in0"], ev["st_in1"])[b % 2], 16)
            sp.wait_ge(ev["sh_out0"], 16 * (NB // 2))
            sp.wait_ge(ev["sh_out1"], 16 * (NB // 2))
            sp.wait_ge(ev["sy_ready"], 1)
            sp.wait_ge(ev["hT_out"], 16)
            sp.dma_start(bdn[0:NE, :], I["b_down"][0]).then_inc(ev["late_loaded"], 16)
            sp.wait_ge(ev["yvar_mm"], 1)
            for p in range(8, NP):
                sp.dma_start(piece(p), expert_piece(0, p)).then_inc(landed[p], 16)
            for p in range(4, 8):
                sp.wait_ge(ev["wo_used"], p - 3)
                load_wout(p)
            sp.wait_ge(ev["wo_used"], 8)
            sp.dma_start(gfin, I["g_final"].partition_broadcast(P)).then_inc(ev["late_loaded"], 16)

            with sp.Fori(0, NE - 1) as i:
                for p in range(NP):
                    sp.wait_ge(ev["piece_used"], i * NP + p + 1)
                    sp.dma_start(piece(p), expert_piece(i + 1, p)).then_inc(landed[p], 16)
            sp.wait_ge(ev["o_tab"], 1)
            n_over = sp.value_load(otab[0:1, OVER:OVER + 1], min_val=0, max_val=OVER)
            with sp.Fori(0, OVER) as j:
                with sp.If(j < n_over):
                    e = sp.value_load(otab[0:1, bass.ds(j, 1)], min_val=0, max_val=NE - 1)
                    sp.wait_ge(ev["piece_used"], j * NP + NE * NP)
                    for p in range(NP):
                        sp.dma_start(piece(p), expert_piece(e, p)).then_inc(landed[p], 16)
            sp.wait_ge(ev["f_ready"], 3)
            sp.dma_start(O["y_p"][0, 0:P], hout[:, 0, :]).then_inc(ev["f_out"], 16)
            sp.dma_start(O["y_p"][0, P:2 * P], hout[:, 1, :]).then_inc(ev["f_out"], 16)
            sp.dma_start(O["y_s"].rearrange("b o d -> (b o) d"), hout[0:NB, 2, :]).then_inc(ev["f_out"], 16)
            sp.wait_ge(ev["f_out"], 48)
            sp.wait_ge(ev["hT_out"], 16)
            sp.wait_ge(ev["kept_out"], 64)
            sp.wait_ge(ev["xst_out"], 32)

        @block.gpsimd
        def _(g):
            nc.gpsimd.memset(x_tok[0:48, 2, :], 0.0)
            nc.gpsimd.memset(stat, 1.0).then_inc(ev["zeroed"], 1)
            for t, base, op in ((ident, 0, ALU.not_equal), (tri, 0, ALU.is_gt), (tri_s, 0, ALU.is_ge)):
                nc.gpsimd.memset(t, 0.0)
            nc.gpsimd.memset(ones, 1.0)
            g.drain()
            for t, op in ((ident, ALU.not_equal), (tri, ALU.is_gt), (tri_s, ALU.is_ge)):
                nc.gpsimd.affine_select(out=t, in_=t, compare_op=op, fill=1.0, base=0, pattern=[[-1, P]],
                                        channel_multiplier=1)
            g.drain()
            nc.gpsimd.memset(cbuf[:, :, 0:30], 0.0)
            nc.gpsimd.memset(xraw[:, :, 0:3], 0.0).then_inc(ev["consts"], 1)
            n = 0
            for c, (_, kind, m0_) in enumerate(CHUNKS):
                if kind == "gate":
                    for m in range(4):
                        g.wait_ge(ev["evac_done"], 4 * c + m + 1)
                        v = cbuf[:, m0_ + m, 30:30 + T]
                        nc.gpsimd.tensor_tensor(v, v, sgt[:, n % 2, :], ALU.mult).then_inc(ev["glu_done"], 1)
                        n += 1
            g.drain()
            nc.gpsimd.tensor_copy(csmp[:, :, :, 30], cbuf[:, :, 30 + TP:30 + T]).then_inc(ev["pad_ready"], 1)
            g.wait_ge(ev["evac_done"], 28)
            nc.gpsimd.tensor_copy(xsmp[:, :, :, 3], xraw[:, :, 3 + TP:3 + T]).then_inc(ev["pad_ready"], 1)
            for u in range(4):
                c, gr = u // 2, u % 2
                g.wait_ge(ev["cb_raw"], u + 1)
                nc.gpsimd.affine_select(out=cbm, in_=cbm, compare_op=ALU.is_ge, fill=0.0, base=0,
                                        pattern=[[1, P]], channel_multiplier=-1)
                g.drain()
                g.wait_ge(ev["xdec_ready"], u + 1)
                nc.gpsimd.tensor_tensor(Mh, Mh, bc(cbm, 1, HPG), ALU.mult)
                nc.gpsimd.tensor_tensor(Ce, Ce, bc(xa[:, 10 + gr, 16 + c * P:16 + (c + 1) * P], 1, HPG),
                                        ALU.mult)
                g.drain()
                nc.gpsimd.tensor_copy(dec[:, 8:16], dec[:, 0:8]).then_inc(ev["m_ready"], 1)
            for b in range(NB):
                g.wait_ge(ev["sh_dec"], b + 1)
                g.wait_ge(ev["sh_bx"], b + 1)
                nc.gpsimd.tensor_tensor(state_in[:, b % 2], state_in[:, b % 2], sprod, ALU.add).then_inc(ev["sh_new"], 1)
            g.wait_ge(ev["late_loaded"], 16)
            nc.gpsimd.iota(iota_f, [[1, P]], base=0, channel_multiplier=0,
                           allow_small_or_imprecise_dtypes=True).then_inc(ev["iota_ready"], 1)

        @block.scalar
        def _(a):
            act = nc.scalar.activation
            rows = lambda name, n: I[name][0].rearrange("(k c) -> k c", c=P)[0:n]
            for r0, ap, n in ((0, rows("g_mix", 8), 8), (8, rows("conv_ssd_b", 12), 12), (20, rows("g_ssd_norm", 8), 8),
                              (28, rows("conv_conf_b", 8), 8), (36, rows("ln_conf_g", 8), 8),
                              (44, rows("ln_conf_b", 8), 8), (52, rows("g_ffn", 8), 8),
                              (60, I["conv_ssd_w"][0].rearrange("k (m c) -> (k m) c", c=P), 48)):
                a.dma_start(vrow[r0:r0 + n, :], ap).then_inc(ev["vec_loaded"], 16)
            cw = I["conv_conf_w"][0].rearrange("k (m c) -> (k m) c", c=P)
            for j in range(2):
                a.dma_start(cwrow[0:124, j, :], cw[124 * j:124 * (j + 1)]).then_inc(ev["bias_loaded"], 16)
                a.dma_start(bgrow[:, j, :], I["b_gate"][0].rearrange("e (m c) -> (e m) c", c=P)[P * j:P * (j + 1)]
                            ).then_inc(ev["bias_loaded"], 16)
                a.dma_start(burow[:, j, :], I["b_up"][0].rearrange("e (m c) -> (e m) c", c=P)[P * j:P * (j + 1)]
                            ).then_inc(ev["bias_loaded"], 16)
            a.dma_start(dtb, I["dt_bias"][0].partition_broadcast(P)).then_inc(ev["misc_loaded"], 16)
            a.dma_start(aneg, I["a_log"][0].partition_broadcast(P)).then_inc(ev["misc_loaded"], 16)
            a.dma_start(brt, I["b_router"][0].partition_broadcast(P)).then_inc(ev["misc_loaded"], 16)
            a.dma_start(wr, I["w_router"][0].rearrange("(k p) n -> p k n", p=P)).then_inc(ev["misc_loaded"], 16)
            dsv = I["d_skip"][0].rearrange("(m j) -> j m", j=2)
            for j in range(2):
                with nc.allow_non_contiguous_dma("sixteen scalars"):
                    a.dma_start(dsk[64 * j:64 * j + 64, :], dsv[j].partition_broadcast(64)).then_inc(ev["misc_loaded"], 16)

            a.wait_ge(ev["x_loaded"], 32)
            a.wait_ge(ev["zeroed"], 1)
            a.wait_ge(ev["x_tail"], 32)
            act(xs_tok[:, 0, :], x_tok[:, 0, :], ACT.Square, accum_out=stat[:, 0, 0:1])
            act(xs_tok[:, 1, :], x_tok[:, 1, :], ACT.Square, accum_out=stat[:, 0, 1:2])
            act(xs_tok[0:48, 2, :], x_tok[0:48, 2, :], ACT.Square, accum_out=stat[0:48, 0, 2:3])
            a.drain()
            act(stat[:, 3, 0:3], stat[:, 0, 0:3], ACT.Copy).then_inc(ev["ssq_ready"], 1)
            a.wait_ge(ev["rms_ready"], 1)
            act(stat[:, 2, 0:3], stat[:, 1, 0:3], ACT.Sqrt).then_inc(ev["std_ready"], 1)
            a.wait_ge(ev["rms_ready"], 2)
            act(xs_tok[:, 0, :], x_tok[:, 0, :], ACT.Copy, scale=stat[:, 1, 0:1]).then_inc(ev["xs_ready"], 1)
            act(xs_tok[:, 1, :], x_tok[:, 1, :], ACT.Copy, scale=stat[:, 1, 1:2]).then_inc(ev["xs_ready"], 1)
            act(xs_tok[0:48, 2, :], x_tok[0:48, 2, :], ACT.Copy, scale=stat[0:48, 1, 2:3]).then_inc(ev["xs_ready"], 1)
            hc = I["state_conf_conv"][0].rearrange("b k d -> (b k) d")
            for j in range(2):
                a.dma_start(hist_c[0:120, j, :], hc[120 * j:120 * (j + 1)]).then_inc(ev["hist_loaded"], 16)
            a.dma_start(hist_x[0:24, :], I["state_ssd_conv"][0].rearrange("b k d -> (b k) d")).then_inc(ev["hist_loaded"], 16)
            a.dma_start(O["conf_s"][0, :, 0:CW - 2, :], I["state_conf_conv"][0, :, 1:CW - 1, :]).then_inc(ev["kept_out"], 16)
            a.dma_start(O["ssd_s"][0, :, 0:SW - 2, :], I["state_ssd_conv"][0, :, 1:SW - 1, :]).then_inc(ev["kept_out"], 16)
            a.wait_ge(ev["dt_v"], 1)
            act(dte, dta, ACT.Exp, scale=-1.0).then_inc(ev["dt_exp"], 1)
            a.wait_ge(ev["dt_v"], 2)
            act(dta, dtw, ACT.Ln).then_inc(ev["dt_exp"], 1)
            a.wait_ge(ev["misc_loaded"], 96)
            act(aneg, aneg, ACT.Exp).then_inc(ev["dt_exp"], 1)

            n = 0
            for c, (_, kind, m0_) in enumerate(CHUNKS):
                for m in range(4):
                    j = 4 * c + m
                    if kind == "z" and m0_ + m == 0:
                        a.wait_ge(ev["hist_ready"], 5)
                    a.wait_ge(ev["win_done"], j + 1)
                    src = ps[:, j % 4, 0:T]
                    mm = m0_ + m
                    if kind == "val":
                        act(cbuf[:, mm, 30:30 + T], src, ACT.Copy).then_inc(ev["evac_done"], 1)
                    elif kind == "gate":
                        if n >= 2:
                            a.wait_ge(ev["glu_done"], n - 1)
                        act(sgt[:, n % 2, :], src, ACT.Sigmoid).then_inc(ev["evac_done"], 1)
                        n += 1
                    elif kind == "xbc":
                        act(xraw[:, mm, 3:3 + T], src, ACT.Copy).then_inc(ev["evac_done"], 1)
                    else:
                        act(zT[:, mm, :], ps[:, j % 4, 0:TN], ACT.Copy).then_inc(ev["evac_done"], 1)
            a.wait_ge(ev["cst_ready"], 1)
            a.dma_start(O["conf_p"][0, 0], cstage[0:CW - 1, :]).then_inc(ev["kept_out"], 16)
            a.dma_start(O["conf_s"][0, :, CW - 2, :], cstage[CW - 1:CW - 1 + NB, :]).then_inc(ev["kept_out"], 16)
            a.wait_ge(ev["xst_ready"], 1)
            a.dma_start(O["ssd_p"][0, 0], xstage[0:SW - 1, :]).then_inc(ev["xst_out"], 16)
            a.dma_start(O["ssd_s"][0, :, SW - 2, :], xstage[SW - 1:SW - 1 + NB, :]).then_inc(ev["xst_out"], 16)

            for h in range(2):
                a.wait_ge(ev["xpre_ready"], 1)
                if h:
                    a.wait_ge(ev["xa_ready"], 1)
                else:
                    a.wait_ge(ev["xst_out"], 32)
                act(flat(xsig), flat(xa[:, 6 * h:6 * h + 6, :]), ACT.Sigmoid).then_inc(ev["xsig_ready"], 1)
            a.wait_ge(ev["mean_mm"], 1)
            act(mu, ps[:, 4, 0:TN], ACT.Copy, scale=1.0 / D).then_inc(ev["mu_ready"], 1)
            a.wait_ge(ev["cent_ready"], 1)
            act(flat(csq), flat(conv), ACT.Square).then_inc(ev["csq_ready"], 1)
            a.wait_ge(ev["var_ready"], 1)
            act(rstd2, rstd, ACT.Sqrt).then_inc(ev["std_ready"], 1)
            a.wait_ge(ev["norm_ready"], 1)
            a.wait_ge(ev["var_mm"], 1)
            for m in range(KT):
                act(csq[:, m, :], conv[:, m, :], ACT.Sigmoid, scale=glg[:, m:m + 1], bias=glb[:, m:m + 1]
                    ).then_inc(ev["csig_ready"], 1)

            a.wait_ge(ev["meta_v"], 1)
            act(dec[0:META, :], dec[0:META, :], ACT.Exp).then_inc(ev["meta_exp"], 1)
            for u in range(4):
                a.wait_ge(ev["d_ready"], u + 1)
                act(flat(Mh), flat(Mh), ACT.Exp).then_inc(ev["e_ready"], 1)
                if u:
                    a.wait_ge(ev["y_mm"], u)
                act(flat(Ce), ps[:, 4:6, :].rearrange("p a b -> p (a b)"), ACT.Exp).then_inc(ev["ce_ready"], 1)
            a.wait_ge(ev["sexp_mm"], 1)
            act(flat(sdec), ps[:, 2, 0:64], ACT.Exp).then_inc(ev["sdec_ready"], 1)
            for b in range(NB):
                a.wait_ge((ev["st_in0"], ev["st_in1"])[b % 2], 16 * (b // 2 + 1))
                if b == 0:
                    a.wait_ge(ev["sdec_ready"], 1)
                for m in range(KT):
                    h = act(state_in[:, b % 2, m, :], state_in[:, b % 2, m, :], ACT.Copy, scale=sdec[:, m, b:b + 1])
                h.then_inc(ev["sh_dec"], 1)
            a.wait_ge(ev["y_mm"], 4)
            a.wait_ge(ev["m_ready"], 4)
            act(flat(zsig), flat(zT), ACT.Sigmoid).then_inc(ev["z_sig"], 1)
            a.wait_ge(ev["yg_ready"], 1)
            act(flat(ysq), flat(yT), ACT.Square).then_inc(ev["ysq_ready"], 1)
            a.wait_ge(ev["yvar_ready"], 1)
            act(rstd, rstd, ACT.Sqrt)
            act(rstd2, rstd2, ACT.Sqrt)
            a.drain()
            act(mu[:, 0:1], mu[:, 0:1], ACT.Copy).then_inc(ev["ystd_ready"], 1)

            for j, (c, r) in enumerate(tok):
                a.wait_ge(ev["h_tr"], j + 1)
                act(hsq[0:r, :], ps[0:r, 2 * j:2 * j + 2, :].rearrange("p a b -> p (a b)"), ACT.Square,
                    accum_out=stat[0:r, 0, j:j + 1])
                a.drain()
            act(stat[:, 3, 0:3], stat[:, 0, 0:3], ACT.Copy).then_inc(ev["hsq_ready"], 1)
            a.wait_ge(ev["hr_v"], 1)
            act(stat[:, 2, 0:3], stat[:, 1, 0:3], ACT.Sqrt).then_inc(ev["hstd_ready"], 1)
            a.wait_ge(ev["hr_v"], 2)
            for j, (c, r) in enumerate(tok):
                act(xn[0:r, j, :], ps[0:r, 2 * j:2 * j + 2, :].rearrange("p a b -> p (a b)"), ACT.Copy,
                    scale=stat[0:r, 1, j:j + 1]).then_inc(ev["xn_ready"], 1)
            a.wait_ge(ev["nm_ready"], 1)
            for j, (c, r) in enumerate(tok):
                act(topw[0:r, j, :], top8[0:r, j, 0:TOPK], ACT.Exp, bias=nmax[0:r, j:j + 1],
                    accum_out=rsum[0:r, j:j + 1])
                a.drain()
            act(stat[:, 3, 0:3], stat[:, 0, 0:3], ACT.Copy).then_inc(ev["topexp"], 1)

            def back(dst, bank):
                return act(flat(dst) if len(dst.shape) == 3 else dst,
                           ps[:, bank:bank + 2, :].rearrange("p a b -> p (a b)"), ACT.Copy)

            def y_rows(i):
                a.wait_ge(ev["ytr_done"], i + 1)
                a.wait_ge(ev["sc_done"], i * 8 + 8)
                back(ys, 6).then_inc(ev["y_back"], 1)

            def scatter_rows(i):
                a.wait_ge(ev["pt_done"], i + 2)
                act(Pm, ps[:, 6, 0:TN], ACT.Copy).then_inc(ev["p_ready"], 1)

            with a.Fori(0, NE) as i:
                a.wait_ge(ev["g_ready"], i + 1)
                act(flat(sig), flat(ge), ACT.Sigmoid, scale=ALPHA).then_inc(ev["sig_ready"], 1)
                y_rows(i)
                scatter_rows(i)
                a.wait_ge(ev["piece_used"], i * NP + NP)
                back(yTs, 4).then_inc(ev["yt_ready"], 1)
            y_rows(NE)
            scatter_rows(NE)

            a.wait_ge(ev["o_tab"], 1)
            n_over = a.value_load(otab[0:1, OVER:OVER + 1], min_val=0, max_val=OVER)
            with a.Fori(0, OVER) as j:
                with a.If(j < n_over):
                    a.wait_ge(ev["g_ready"], j + NE + 1)
                    act(flat(sig), flat(ge), ACT.Sigmoid, scale=ALPHA).then_inc(ev["sig_ready"], 1)
                    a.wait_ge(ev["piece_used"], j * NP + (NE + 1) * NP)
                    back(yTs, 4).then_inc(ev["yt_ready"], 1)
                    a.wait_ge(ev["ytr_done"], j + NE + 2)
                    back(ys, 6).then_inc(ev["y_back"], 1)
                    a.wait_ge(ev["pt_done"], j + NE + 3)
                    act(Pm, ps[:, 6, 0:TN], ACT.Copy).then_inc(ev["p_ready"], 1)

            for j, (c, r) in enumerate(tok):
                a.wait_ge(ev["h_tr"], j + 4)
                act(hsq[0:r, :], ps[0:r, 2 * j:2 * j + 2, :].rearrange("p a b -> p (a b)"), ACT.Square,
                    accum_out=stat[0:r, 0, j:j + 1])
                a.drain()
            act(stat[:, 3, 0:3], stat[:, 0, 0:3], ACT.Copy).then_inc(ev["hsq_ready"], 1)
            a.wait_ge(ev["hr_v"], 3)
            act(stat[:, 2, 0:3], stat[:, 1, 0:3], ACT.Sqrt).then_inc(ev["hstd_ready"], 1)

        @block.vector
        def _(v):
            V = nc.vector
            TT, TS, STT = V.tensor_tensor, V.tensor_scalar, V.scalar_tensor_tensor

            V.memset(dtt, 0.0)
            for k, (dst, src) in enumerate(((vcol, ps[:, 4, 0:108]), (flat(cwcol), ps[:, 5, 0:248]),
                                            (flat(bgT), ps[:, 6, 0:256]), (flat(buT), ps[:, 7, 0:256]))):
                v.wait_ge(ev["vt_done"], k + 1)
                V.tensor_copy(dst, src).then_inc(ev["vcol_ready"], 1)
            v.wait_ge(ev["ssq_ready"], 1)
            TS(stat[:, 1, 0:3], stat[:, 0, 0:3], 1.0 / D, EPS, ALU.mult, ALU.add).then_inc(ev["rms_ready"], 1)
            v.wait_ge(ev["std_ready"], 1)
            V.reciprocal(stat[:, 1, 0:3], stat[:, 2, 0:3]).then_inc(ev["rms_ready"], 1)
            for k in range(4):
                j, h = k // 2, k % 2
                v.wait_ge(ev["xtr_done"], k + 1)
                TT(uT[:, 4 * h:4 * h + 4, META + P * j:META + P * (j + 1)], ps[:, 4 + k, :].rearrange("p (m t) -> p m t", m=4),
                   bc(gmx[:, 4 * h:4 * h + 4], 2, P), ALU.mult).then_inc(ev["uT_ready"], 1)
            v.wait_ge(ev["xtr_done"], 5)
            tail = ps[:, 4, 0:384].rearrange("p (m t) -> p m t", m=8)
            TT(uT[:, :, TP:T], tail[:, :, 0:NB], bc(gmx, 2, NB), ALU.mult).then_inc(ev["uT_ready"], 1)
            TT(uT[:, :, 0:META], tail[:, :, 32:48], bc(gmx, 2, META), ALU.mult).then_inc(ev["uT_ready"], 1)

            v.wait_ge(ev["dt_mm"], 1)
            v.drain()
            dp = ps[:, 5, 0:64].rearrange("p (g h) -> p g h", g=4)
            for g_, r in ((0, P), (1, P), (2, NB), (3, META)):
                V.tensor_copy(dtt[0:r, g_, :], dp[0:r, g_, :])
            v.wait_ge(ev["misc_loaded"], 96)
            v.drain()
            TT(dtt, dtt, bc(dtb, 1, 4), ALU.add)
            v.drain()
            TS(dtd, dtt, -1.0, None, ALU.mult)
            v.drain()
            TT(dta, dtt, dtd, ALU.max)
            v.drain()
            TS(dtd, dtt, 0.0, None, ALU.max).then_inc(ev["dt_v"], 1)
            v.wait_ge(ev["dt_exp"], 1)
            TS(dtw, dte, 1.0, None, ALU.add).then_inc(ev["dt_v"], 1)
            v.wait_ge(ev["dt_exp"], 2)
            v.drain()
            TS(dtw, dtw, -1.0, None, ALU.add)
            v.drain()
            TS(dtt, dtw, 0.0, None, ALU.is_equal)
            v.drain()
            TT(dtw, dtw, dtt, ALU.add)
            TT(dtt, dtt, dte, ALU.mult)
            v.drain()
            V.reciprocal(dtw, dtw)
            TT(dta, dta, dte, ALU.mult)
            TT(dtt, dtt, dtd, ALU.add)
            v.drain()
            TT(dta, dta, dtw, ALU.mult)
            v.drain()
            TT(dtt, dtt, dta, ALU.add)
            v.wait_ge(ev["dt_exp"], 3)
            v.drain()
            STT(dta, dtt, -1.0, bc(aneg, 1, 4), ALU.mult, ALU.mult)
            v.drain()
            TT(wr, wr, bc(gff, 2, NE), ALU.mult).then_inc(ev["dt_ready"], 1)

            v.wait_ge(ev["consts"], 1)
            for h in range(2):
                v.wait_ge(ev["glu_done"], 4 * h + 4)
                for k in range(CW):
                    for m in range(4 * h, 4 * h + 4):
                        src = cbuf[:, m, META + k:META + k + SEQ]
                        w = cwcol[:, k, m:m + 1]
                        if k == 0:
                            TS(conv[:, m, 0:SEQ], src, w, gcb[:, m:m + 1], ALU.mult, ALU.add)
                        else:
                            STT(conv[:, m, 0:SEQ], src, w, conv[:, m, 0:SEQ], ALU.mult, ALU.add)
                    v.drain()
            for k in range(4):
                j, h = k // 2, k % 2
                v.wait_ge(ev["htr_done"], k + 1)
                V.tensor_copy(csmp[:, 4 * h:4 * h + 4, 4 * j:4 * j + 4, 0:30],
                              ps[:, 4 + k, 0:480].rearrange("p (m b k) -> p m b k", m=4, b=4)).then_inc(ev["hist_ready"], 1)
            v.wait_ge(ev["htr_done"], 5)
            V.tensor_copy(xsmp[:, :, :, 0:3], ps[:, 4, 0:288].rearrange("p (m b k) -> p m b k", m=12, b=8)
                          ).then_inc(ev["hist_ready"], 1)
            v.wait_ge(ev["cst_tr"], 1)
            V.tensor_copy(cstage[0:38, :], ps[0:38, 5:7, :].rearrange("p a b -> p (a b)")).then_inc(ev["cst_ready"], 1)
            v.wait_ge(ev["xst_tr"], 1)
            V.tensor_copy(xstage[0:11, :], ps[0:11, 5:8, :].rearrange("p a b -> p (a b)")).then_inc(ev["xst_ready"], 1)
            v.wait_ge(ev["pad_ready"], 1)
            v.drain()
            for m in range(KT):
                TT(csmp[:, m], csmp[:, m], bc(cwcol[:, :, m], 1, NB), ALU.mult)
            v.drain()
            V.tensor_reduce(conv[:, :, SEQ:TN], csmp, AX, ALU.add)
            v.drain()
            TT(conv[:, :, SEQ:TN], conv[:, :, SEQ:TN], bc(gcb, 2, NB), ALU.add).then_inc(ev["conv_done"], 1)

            xw = gxw.rearrange("p (k m) -> p k m", k=SW)
            for m3 in range(0, XT_, 4):
                v.wait_ge(ev["evac_done"], 16 + m3 + 4)
                for k in range(SW):
                    for m in range(m3, m3 + 4):
                        src = xraw[:, m, k:k + TP]
                        if k == 0:
                            TS(xa[:, m, 0:TP], src, xw[:, k, m:m + 1], gxb[:, m:m + 1], ALU.mult, ALU.add)
                        else:
                            STT(xa[:, m, 0:TP], src, xw[:, k, m:m + 1], xa[:, m, 0:TP], ALU.mult, ALU.add)
                    v.drain()
            v.wait_ge(ev["pad_ready"], 2)
            TT(xsmp, xsmp, bc(xw.rearrange("p k m -> p m k"), 2, NB), ALU.mult)
            v.drain()
            V.tensor_reduce(xa[:, :, TP:T], xsmp, AX, ALU.add)
            v.drain()
            TT(xa[:, :, TP:T], xa[:, :, TP:T], bc(gxb, 2, NB), ALU.add).then_inc(ev["xpre_ready"], 1)
            for h in range(2):
                v.wait_ge(ev["xsig_ready"], h + 1)
                TT(flat(xa[:, 6 * h:6 * h + 6, :]), flat(xa[:, 6 * h:6 * h + 6, :]), flat(xsig), ALU.mult
                   ).then_inc(ev["xa_ready"], 1)

            v.wait_ge(ev["mu_ready"], 1)
            TT(conv, conv, bc(mu, 1, KT), ALU.subtract).then_inc(ev["cent_ready"], 1)
            v.wait_ge(ev["var_mm"], 1)
            TS(rstd, ps[:, 5, 0:TN], 1.0 / D, EPS, ALU.mult, ALU.add).then_inc(ev["var_ready"], 1)
            v.wait_ge(ev["std_ready"], 2)
            V.reciprocal(rstd, rstd2)
            v.drain()
            TT(conv, conv, bc(rstd, 1, KT), ALU.mult).then_inc(ev["norm_ready"], 1)
            for m in range(KT):
                v.wait_ge(ev["csig_ready"], m + 1)
                TS(conv[:, m, :], conv[:, m, :], glg[:, m:m + 1], glb[:, m:m + 1], ALU.mult, ALU.add)
            v.drain()
            TT(flat(conv), flat(conv), flat(csq), ALU.mult).then_inc(ev["conf_ready"], 1)

            v.wait_ge(ev["acum_mm"], 1)
            am = ps[:, 6, 0:64].rearrange("p (g h) -> p g h", g=4)
            V.tensor_copy(acum, am[:, 0:2, :])
            V.tensor_copy(dec[0:META, :], am[0:META, 2, :])
            v.drain()
            TT(dec[0:META, :], am[0:META, 3, :], dec[0:META, :], ALU.subtract).then_inc(ev["meta_v"], 1)

            def rows_of_chunk(n, r, g_):
                v.wait_ge(ev["xtok_mm"], n + 1)
                for h in range(2):
                    TT(xdt[0:r, 8 * h:8 * h + 8, :], ps[0:r, h, :].rearrange("p (h d) -> p h d", h=HPG),
                       bc(dtt[0:r, g_, 8 * h:8 * h + 8], 2, HD), ALU.mult)
                V.tensor_copy(flat(btok[0:r]), ps[0:r, 2, 0:256]).then_inc(ev["xdt_ready"], 1)

            v.wait_ge(ev["xst_out"], 32)
            rows_of_chunk(0, META, 3)
            v.wait_ge(ev["meta_exp"], 1)
            v.drain()
            TT(xdec[0:META], xdt[0:META], bc(dec[0:META, :], 2, HD), ALU.mult).then_inc(ev["hT_ready"], 1)
            for g_ in range(GROUPS):
                v.wait_ge(ev["st_mm"], g_ + 1)
                V.tensor_copy(hT[:, 8 * g_:8 * g_ + 8, :], ps[:, 7, :].rearrange("p (h d) -> p h d", h=HPG)
                              ).then_inc(ev["hT_ready"], 1)
            for c in range(2):
                if c:
                    v.wait_ge(ev["st_mm"], 6 - 2)
                rows_of_chunk(1 + c, P, c)
                for g_ in range(GROUPS):
                    u = 2 * c + g_
                    v.wait_ge(ev["cb_mm"], u + 1)
                    if u:
                        v.wait_ge(ev["m_ready"], u)
                    V.tensor_copy(cbm, ps[:, 3, 0:P]).then_inc(ev["cb_raw"], 1)
                    v.wait_ge(ev["acb_mm"], u + 1)
                    if u:
                        v.wait_ge(ev["y_mm"], u)
                    for h in range(2):
                        TT(Mh[:, 4 * h:4 * h + 4, :], ps[:, 4 + h, :].rearrange("p (h d) -> p h d", h=4),
                           bc(acum[:, c, 8 * g_ + 4 * h:8 * g_ + 4 * h + 4], 2, P), ALU.subtract)
                    v.drain()
                    TS(flat(Mh), flat(Mh), 0.0, None, ALU.min).then_inc(ev["d_ready"], 1)
                    v.wait_ge(ev["e_ready"], u + 1)
                    V.tensor_copy(dec[:, 0:8], Mh[:, :, P - 1])
                    v.wait_ge(ev["ce_ready"], u + 1)
                    V.tensor_copy(cdec[:, 0:8], Ce[:, :, P - 1])
                    v.drain()
                    TT(xdec[:, 8 * g_:8 * g_ + 8, :], xdt[:, 8 * g_:8 * g_ + 8, :], bc(dec[:, 0:8], 2, HD), ALU.mult
                       ).then_inc(ev["xdec_ready"], 1)
                    v.wait_ge(ev["y_mm"], u + 1)
                    for k in range(4):
                        m = 4 * g_ + k
                        h = STT(yT[:, m, c * P:(c + 1) * P], xa[:, m, META + c * P:META + (c + 1) * P], dsk[:, m:m + 1],
                                ps[:, 6, k * P:(k + 1) * P], ALU.mult, ALU.add)
                    h.then_inc(ev["y_ready"], 1)
                    TT(hT[:, 8 * g_:8 * g_ + 8, :], hT[:, 8 * g_:8 * g_ + 8, :], bc(cdec[:, 0:8], 2, HD), ALU.mult)
                    v.drain()
                    v.wait_ge(ev["st_mm"], 3 + u)
                    TT(hT[:, 8 * g_:8 * g_ + 8, :], hT[:, 8 * g_:8 * g_ + 8, :],
                       ps[:, 7, :].rearrange("p (h d) -> p h d", h=HPG), ALU.add).then_inc(ev["hT_ready"], 1)
            v.wait_ge(ev["hT_tr"], 1)
            V.tensor_copy(view(ring, s0 + 3136, D), ps[:, 0:2, :].rearrange("p a b -> p (a b)")).then_inc(ev["hT_st"], 1)

            v.wait_ge(ev["sexp_mm"], 1)
            V.tensor_copy(flat(sdt), ps[:, 3, 0:64])
            v.drain()
            TT(sdt, sdt, xa[:, 0:KT, TP:T], ALU.mult)
            v.drain()
            for b in range(NB):
                v.wait_ge(ev["sbc_mm"], b + 1)
                sbc = ps[:, 4 + b % 2, :].rearrange("p (j n) -> p j n", j=4)
                if b:
                    v.drain()
                for g_ in range(GROUPS):
                    h = TT(sprod[:, 4 * g_:4 * g_ + 4, :], bc(sbc[:, g_, :], 1, 4), bc(sdt[:, 4 * g_:4 * g_ + 4, b], 2, P),
                           ALU.mult)
                h.then_inc(ev["sh_bx"], 1)
                v.wait_ge(ev["sh_new"], b + 1)
                for g_ in range(GROUPS):
                    h = TT(sprod[:, 4 * g_:4 * g_ + 4, :], bc(sbc[:, 2 + g_, :], 1, 4),
                           state_in[:, b % 2, 4 * g_:4 * g_ + 4, :], ALU.mult)
                h.then_inc(ev["sh_prod"], 1)
                v.drain()
                V.tensor_reduce(yT[:, :, SEQ + b], sprod, AX, ALU.add)
            v.drain()
            TT(sdt, xa[:, 0:KT, TP:T], bc(dsk, 2, NB), ALU.mult)
            v.drain()
            TT(yT[:, :, SEQ:TN], yT[:, :, SEQ:TN], sdt, ALU.add).then_inc(ev["sy_ready"], 1)
            v.wait_ge(ev["z_sig"], 1)
            TT(flat(zT), flat(zT), flat(zsig), ALU.mult)
            v.drain()
            TT(flat(yT), flat(yT), flat(zT), ALU.mult).then_inc(ev["yg_ready"], 1)
            v.wait_ge(ev["yvar_mm"], 1)
            TS(rstd, ps[:, 4, 0:TN], 2.0 / D, EPS, ALU.mult, ALU.add)
            TS(rstd2, ps[:, 5, 0:TN], 2.0 / D, EPS, ALU.mult, ALU.add).then_inc(ev["yvar_ready"], 1)
            v.wait_ge(ev["ystd_ready"], 1)
            V.reciprocal(rstd, rstd)
            V.reciprocal(rstd2, rstd2)
            v.drain()
            for m in range(KT):
                h = STT(yT[:, m, :], yT[:, m, :], gsn[:, m:m + 1], rstd if m < 4 else rstd2, ALU.mult, ALU.mult)
            h.then_inc(ev["yn_ready"], 1)

            v.wait_ge(ev["wo_mm"], 1)
            v.drain()
            for m in range(KT):
                V.tensor_copy(accT[:, m, :], ps[:, m, 0:TN]).then_inc(ev["acc_ready"], 1)
            V.memset(slotp, -FAR)
            V.memset(gates, 0.0)
            V.memset(flat(yTs), 0.0).then_inc(ev["yt_ready"], 1)
            V.memset(zero32, 0.0).then_inc(ev["g_read"], 1)
            V.memset(nbo, 0.0).then_inc(ev["u_read"], 1)
            v.wait_ge(ev["hsq_ready"], 1)
            TS(stat[:, 1, 0:3], stat[:, 0, 0:3], 1.0 / D, EPS, ALU.mult, ALU.add).then_inc(ev["hr_v"], 1)
            v.wait_ge(ev["hstd_ready"], 1)
            V.reciprocal(stat[:, 1, 0:3], stat[:, 2, 0:3]).then_inc(ev["hr_v"], 1)
            v.drain()
            v.wait_ge(ev["lg_mm"], 1)
            lg = ps[:, 6, 0:96].rearrange("p (j e) -> p j e", j=3)
            for j, (c, r) in enumerate(tok):
                STT(logit[0:r, j, :], lg[0:r, j, :], stat[0:r, 1, j:j + 1], brt[0:r, :], ALU.mult, ALU.add)
            v.drain()
            for j, (c, r) in enumerate(tok):
                V.max(top8[0:r, j, :], logit[0:r, j, :])
            v.drain()
            for j, (c, r) in enumerate(tok):
                V.max_index(topi[0:r, j, :], top8[0:r, j, :], logit[0:r, j, :])
                h = TS(nmax[0:r, j:j + 1], top8[0:r, j, 0:1], -1.0, None, ALU.mult)
            h.then_inc(ev["nm_ready"], 1)
            v.drain()
            for j, (c, r) in enumerate(tok):
                V.tensor_copy(topf[0:r, j, :], topi[0:r, j, 0:TOPK])
            v.wait_ge(ev["iota_ready"], 1)
            v.drain()
            for j, (c, r) in enumerate(tok):
                TT(eq[0:r], bc(iota_f[0:r, 0:NE], 1, TOPK), bc(topf[0:r, j, :], 2, NE), ALU.is_equal)
                v.drain()
                V.tensor_reduce(mask[0:r, j, :], eq[0:r].rearrange("p k e -> p e k"), AX, ALU.add)
                if j == 0:
                    v.wait_ge(ev["topexp"], 1)
                    V.reciprocal(rsum[:, 0:2], rsum[:, 0:2])
                    V.reciprocal(rsum[0:NB, 2:3], rsum[0:NB, 2:3])
                    v.drain()
                TS(topw[0:r, j, :], topw[0:r, j, :], rsum[0:r, j:j + 1], None, ALU.mult)
                v.drain()
                TT(eq[0:r], eq[0:r], bc(topw[0:r, j, :], 2, NE), ALU.mult)
                v.drain()
                h = V.tensor_reduce(gates[0:r, j, 1:NE + 1], eq[0:r].rearrange("p k e -> p e k"), AX, ALU.add)
                h.then_inc(ev["gates_ready"], 1)
                TS(tmp96[0:r, j, :], mask[0:r, j, :], FAR, -FAR, ALU.mult, ALU.add)
                v.drain()
            v.wait_ge(ev["pos_mm"], 1)
            pm = ps[:, 7, 0:128].rearrange("p (j e) -> p j e", j=4)
            for j, (c, r) in enumerate(tok):
                TT(slotp[0:r, j, 1:NE + 1], pm[0:r, j, :], tmp96[0:r, j, :], ALU.add)
            V.tensor_copy(cntf, pm[:, 3, :])
            V.memset(cnti[0:1, NE:NE + 1], 0)
            V.tensor_copy(cnti[0:1, 0:NE], pm[0:1, 3, :])
            v.drain()
            V.memset(nbo, 0.0).then_inc(ev["cnt_ready"], 1)
            v.drain()

            def choose(dst, col, scale=None):
                for j, (c, r) in enumerate(tok):
                    sl = slotp[0:r, j, bass.ds(col, 1)]
                    if scale is None:
                        h = TS(dst[0:r, j, :], iota_f[0:r, :], sl, None, ALU.is_equal)
                    else:
                        h = TS(dst[0:r, j, :], iota_f[0:r, :], sl, gates[0:r, j, bass.ds(col, 1)], ALU.is_equal, ALU.mult)
                return h

            choose(S, 1).then_inc(ev["s_ready"], 1)
            TS(nbo, cntf, float(CAP), None, ALU.is_gt)
            TS(cum, cntf, float(2 * CAP), None, ALU.is_gt)
            V.memset(zero32, 0.0)
            v.drain()
            TT(nbo, nbo, cum, ALU.add)
            v.drain()
            V.tensor_tensor_scan(cum, nbo, zero32, 0.0, ALU.add, ALU.add)
            v.drain()
            for k in range(OVER):
                TS(ole[:, k, :], cum, float(k), None, ALU.is_le)
            v.drain()
            V.tensor_reduce(oe[:, 0:OVER], ole, AX, ALU.add)
            V.tensor_copy(oe[:, OVER:OVER + 1], cum[:, NE - 1:NE])
            v.drain()
            TT(ole, ole, bc(nbo, 1, OVER), ALU.mult)
            v.drain()
            V.tensor_reduce(ob, ole, AX, ALU.add)
            TS(oe[:, 0:OVER], oe[:, 0:OVER], float(NE - 1), None, ALU.min)
            v.drain()
            V.tensor_copy(otab, oe).then_inc(ev["o_tab"], 1)
            TS(ob, ob, -float(CAP), None, ALU.mult)
            for k in range(OVER):
                v.drain()
                TS(ob[:, k:k + 1], ob[:, k:k + 1], float(CAP * (k + 1)), None, ALU.add)
            v.wait_ge(ev["pt_done"], 1)
            V.tensor_copy(gT[0:NE, :], ps[0:NE, 6, 0:TN]).then_inc(ev["gt_ready"], 1)

            def take_inputs():
                return TT(xg, ps[:, 4:6, :].rearrange("p a (m s) -> p (a m) s", s=CAP), bc(gff, 2, CAP), ALU.mult)

            def add_back(n):
                for m in range(KT):
                    v.wait_ge(ev["sc_done"], n + m + 1)
                    TT(accT[:, m, :], ps[:, 7 - m % 2, 0:TN], accT[:, m, :], ALU.add).then_inc(ev["acc_done"], 1)

            v.wait_ge(ev["xg_done"], 1)
            take_inputs().then_inc(ev["xg_ready"], 1)
            add_back(0)

            def swiglu(e, n):
                v.wait_ge(ev["piece_used"], n * NP + 4 - NP)
                TT(ge, ps[:, 0:2, :].rearrange("p a (m s) -> p (a m) s", s=CAP),
                   bc(bgT[:, bass.ds(e, 1), :].rearrange("p o m -> p (o m)"), 2, CAP), ALU.add).then_inc(ev["g_read"], 1)
                v.drain()
                TS(flat(ge), flat(ge), LIMIT, None, ALU.min).then_inc(ev["g_ready"], 1)
                v.wait_ge(ev["piece_used"], n * NP + 8 - NP)
                TT(ue, ps[:, 2:4, :].rearrange("p a (m s) -> p (a m) s", s=CAP),
                   bc(buT[:, bass.ds(e, 1), :].rearrange("p o m -> p (o m)"), 2, CAP), ALU.add).then_inc(ev["u_read"], 1)
                v.drain()
                TS(flat(ue), flat(ue), LIMIT, -LIMIT, ALU.min, ALU.max)
                v.drain()
                STT(flat(ue), flat(ue), 1.0, flat(ge), ALU.add, ALU.mult)
                v.drain()
                v.wait_ge(ev["sig_ready"], n)
                TT(flat(hdn), flat(ue), flat(sig), ALU.mult).then_inc(ev["hdn_ready"], 1)

            with v.Fori(0, NE) as i:
                v.wait_ge(ev["pt_done"], i + 1)
                choose(Sg, i, scale=True).then_inc(ev["sg_ready"], 1)
                v.wait_ge(ev["xg_done"], i + 1)
                choose(S, i + 2).then_inc(ev["s_ready"], 1)
                swiglu(i, i + 1)
                v.wait_ge(ev["xg_done"], i + 2)
                take_inputs().then_inc(ev["xg_ready"], 1)
                add_back(i * 8 + 8)
            v.wait_ge(ev["pt_done"], NE + 1)
            choose(Sg, NE, scale=True).then_inc(ev["sg_ready"], 1)
            add_back(NE * 8 + 8)

            n_over = v.value_load(otab[0:1, OVER:OVER + 1], min_val=0, max_val=OVER)
            with v.Fori(0, OVER) as j:
                with v.If(j < n_over):
                    e = v.value_load(otab[0:1, bass.ds(j, 1)], min_val=0, max_val=NE - 1)
                    v.drain()
                    TS(oslot, slotp[:, :, bass.ds(e + 1, 1)].rearrange("p j o -> p (j o)"), ob[:, bass.ds(j, 1)], None,
                       ALU.subtract)
                    v.drain()
                    for t, (c, r) in enumerate(tok):
                        TS(S[0:r, t, :], iota_f[0:r, :], oslot[0:r, t:t + 1], None, ALU.is_equal)
                        TS(Sg[0:r, t, :], iota_f[0:r, :], oslot[0:r, t:t + 1], gates[0:r, t, bass.ds(e + 1, 1)],
                           ALU.is_equal, ALU.mult)
                    v.drain()
                    V.memset(zero32, 0.0).then_inc(ev["s_ready"], 1)
                    v.wait_ge(ev["xg_done"], j + NE + 2)
                    take_inputs().then_inc(ev["xg_ready"], 1)
                    swiglu(e, j + NE + 1)
                    add_back(j * 8 + 8 * (NE + 2))

            v.drain()
            V.memset(zero32, 0.0).then_inc(ev["f_rd"], 1)
            v.wait_ge(ev["hsq_ready"], 2)
            TS(stat[:, 1, 0:3], stat[:, 0, 0:3], 1.0 / D, EPS, ALU.mult, ALU.add).then_inc(ev["hr_v"], 1)
            v.wait_ge(ev["hstd_ready"], 2)
            V.reciprocal(stat[:, 1, 0:3], stat[:, 2, 0:3])
            v.wait_ge(ev["late_loaded"], 32)
            v.drain()
            for j, (c, r) in enumerate(tok):
                STT(hout[0:r, j, :], ps[0:r, 2 * j:2 * j + 2, :].rearrange("p a b -> p (a b)"), stat[0:r, 1, j:j + 1],
                    gfin[0:r, :], ALU.mult, ALU.mult).then_inc(ev["f_ready"], 1)

        @block.tensor
        def _(pe):
            MM = nc.tensor.matmul

            def TR(out, in_):
                r = in_.shape[0]
                return nc.tensor.transpose(out, in_, ident[0:r, 0:r])

            def ident_at(r0, n):
                return ident[r0:r0 + n, r0:r0 + n]

            pe.wait_ge(ev["consts"], 1)
            pe.wait_ge(ev["vec_loaded"], 16 * 8)
            TR(ps[:, 4, 0:108], vrow[0:108, :]).then_inc(ev["vt_done"], 1)
            pe.wait_ge(ev["bias_loaded"], 16 * 6)
            for j in range(2):
                h = TR(ps[:, 5, 124 * j:124 * (j + 1)], cwrow[0:124, j, :])
            h.then_inc(ev["vt_done"], 1)
            for j in range(2):
                h = TR(ps[:, 6, P * j:P * (j + 1)], bgrow[:, j, :])
            h.then_inc(ev["vt_done"], 1)
            for j in range(2):
                h = TR(ps[:, 7, P * j:P * (j + 1)], burow[:, j, :])
            h.then_inc(ev["vt_done"], 1)
            for k in range(4):
                j, h_ = k // 2, k % 2
                pe.wait_ge(ev["xs_ready"], j + 1)
                pe.wait_ge(ev["vcol_ready"], k + 1)
                for m in range(4):
                    h = TR(ps[:, 4 + k, P * m:P * (m + 1)], xs_tok[:, j, P * (4 * h_ + m):P * (4 * h_ + m + 1)])
                h.then_inc(ev["xtr_done"], 1)
            pe.wait_ge(ev["xs_ready"], 3)
            pe.wait_ge(ev["uT_ready"], 1)
            for m in range(KT):
                h = TR(ps[:, 4, 48 * m:48 * (m + 1)], xs_tok[0:48, 2, P * m:P * (m + 1)])
            h.then_inc(ev["xtr_done"], 1)
            pe.wait_ge(ev["uT_ready"], 6)
            pe.wait_ge(ev["wdt_loaded"], 16)
            for g_, (c, r) in enumerate(((META, P), (META + P, P), (TP, NB), (0, META))):
                for k in range(KT):
                    h = MM(ps[0:r, 5, HEADS * g_:HEADS * (g_ + 1)], uT[:, k, c:c + r], wdt[:, k, :],
                           start=(k == 0), stop=(k == KT - 1))
            h.then_inc(ev["dt_mm"], 1)

            def w_in_chunk(c):
                pe.wait_ge(win_landed[c % 6], 16 * (c // 6 + 1))
                kind = CHUNKS[c][1]
                w = win(c)
                for m in range(4):
                    j = 4 * c + m
                    if j >= 4:
                        pe.wait_ge(ev["evac_done"], j - 3)
                    lo = META if kind == "z" else 0
                    for k in range(KT):
                        h = MM(ps[:, j % 4, 0:T - lo], w[:, k, P * m:P * (m + 1)], uT[:, k, lo:T],
                               start=(k == 0), stop=(k == KT - 1))
                    h.then_inc(ev["win_done"], 1)
                nop_used(ev["win_used"])

            def nop_used(s_):
                pe.drain().then_inc(s_, 1)

            for c in range(4):
                w_in_chunk(c)
            pe.wait_ge(ev["hist_loaded"], 48)
            pe.wait_ge(ev["dt_v"], 1)
            for k in range(4):
                j, h_ = k // 2, k % 2
                for m in range(4):
                    h = TR(ps[:, 4 + k, 120 * m:120 * (m + 1)], hist_c[0:120, j, P * (4 * h_ + m):P * (4 * h_ + m + 1)])
                h.then_inc(ev["htr_done"], 1)
            w_in_chunk(4)
            w_in_chunk(5)
            pe.wait_ge(ev["hist_ready"], 1)
            for m in range(XT_):
                h = TR(ps[:, 4, 24 * m:24 * (m + 1)], hist_x[0:24, P * m:P * (m + 1)])
            h.then_inc(ev["htr_done"], 1)
            pe.wait_ge(ev["hist_ready"], 3)
            pe.wait_ge(ev["glu_done"], 8)
            for m in range(KT):
                h = TR(ps[0:38, 5 + m // 4, P * (m % 4):P * (m % 4 + 1)], cbuf[:, m, 30 + T - 38:30 + T])
            h.then_inc(ev["cst_tr"], 1)
            w_in_chunk(6)
            pe.wait_ge(ev["hist_ready"], 4)
            pe.wait_ge(ev["cst_ready"], 1)
            pe.wait_ge(ev["evac_done"], 28)
            for m in range(XT_):
                h = TR(ps[0:11, 5 + m // 4, P * (m % 4):P * (m % 4 + 1)], xraw[:, m, 3 + T - 11:3 + T])
            h.then_inc(ev["xst_tr"], 1)
            w_in_chunk(7)
            w_in_chunk(8)

            pe.wait_ge(ev["conv_done"], 1)
            for m in range(KT):
                h = MM(ps[:, 4, 0:TN], ones, conv[:, m, :], start=(m == 0), stop=(m == KT - 1))
            h.then_inc(ev["mean_mm"], 1)
            pe.wait_ge(ev["csq_ready"], 1)
            pe.wait_ge(ev["xst_ready"], 1)
            for m in range(KT):
                h = MM(ps[:, 5, 0:TN], ones, csq[:, m, :], start=(m == 0), stop=(m == KT - 1))
            h.then_inc(ev["var_mm"], 1)

            pe.wait_ge(ev["dt_ready"], 1)
            for c in range(2):
                MM(ps[:, 6, HEADS * c:HEADS * (c + 1)], tri, dta[:, c, :], start=True, stop=True)
            MM(ps[0:META, 6, 32:48], tri[0:META, 0:META], dta[0:META, 3, :], start=True, stop=True)
            MM(ps[0:META, 6, 48:64], ones[0:META, 0:META], dta[0:META, 3, :], start=True, stop=True
               ).then_inc(ev["acum_mm"], 1)

            def chunk_rows(n, c, r):
                pe.wait_ge(ev["xa_ready"], 2)
                if n:
                    pe.wait_ge(ev["xdt_ready"], n)
                for m in range(KT):
                    TR(ps[0:r, m // 4, P * (m % 4):P * (m % 4 + 1)], xa[:, m, c:c + r])
                for g_ in range(GROUPS):
                    h = TR(ps[0:r, 2, P * g_:P * (g_ + 1)], xa[:, KT + g_, c:c + r])
                h.then_inc(ev["xtok_mm"], 1)

            pe.wait_ge(ev["evac_done"], 36)
            chunk_rows(0, 0, META)
            pe.wait_ge(ev["xdt_ready"], 1)
            for g_ in range(GROUPS):
                pe.wait_ge(ev["hT_ready"], 1 + g_)
                MM(ps[:, 7, :], btok[0:META, g_, :], xdec[0:META, 8 * g_:8 * g_ + 8, :].rearrange("p h d -> p (h d)"),
                   start=True, stop=True).then_inc(ev["st_mm"], 1)
            for c in range(2):
                cs = META + c * P
                chunk_rows(1 + c, cs, P)
                for g_ in range(GROUPS):
                    u = 2 * c + g_
                    if u:
                        pe.wait_ge(ev["cb_raw"], u)
                    MM(ps[:, 3, 0:P], xa[:, KT + g_, cs:cs + P], xa[:, KT + 2 + g_, cs:cs + P], start=True, stop=True
                       ).then_inc(ev["cb_mm"], 1)
                    pe.wait_ge(ev["mu_ready"], 1)
                    pe.wait_ge(ev["var_ready"], 1)
                    if u:
                        pe.wait_ge(ev["ce_ready"], u)
                    for k in range(HPG):
                        h = MM(ps[:, 4 + k // 4, P * (k % 4):P * (k % 4 + 1)],
                               dta[:, c, 8 * g_ + k:8 * g_ + k + 1].to_broadcast([P, P]), tri, start=True, stop=True)
                    h.then_inc(ev["acb_mm"], 1)
                    pe.wait_ge(ev["xdt_ready"], 2 + c)
                    pe.wait_ge(ev["m_ready"], u + 1)
                    pe.wait_ge(ev["hT_ready"], 3 + u)
                    pe.wait_ge(ev["meta_v"], 1)
                    if u:
                        pe.wait_ge(ev["y_ready"], u)
                    for k in range(HPG):
                        r0 = 64 * (k % 2)
                        dst = ps[r0:r0 + 64, 6, P * (k // 2):P * (k // 2 + 1)]
                        MM(dst, xdt[:, 8 * g_ + k, :], Mh[:, k, :], start=True, stop=False)
                        h = MM(dst, hT[:, 8 * g_ + k, :], Ce[:, k, :], start=False, stop=True)
                    h.then_inc(ev["y_mm"], 1)
                    pe.wait_ge(ev["xdec_ready"], u + 1)
                    MM(ps[:, 7, :], btok[:, g_, :], xdec[:, 8 * g_:8 * g_ + 8, :].rearrange("p h d -> p (h d)"),
                       start=True, stop=True).then_inc(ev["st_mm"], 1)
            pe.wait_ge(ev["hT_ready"], 7)
            for m in range(KT):
                h = TR(ps[:, m // 4, P * (m % 4):P * (m % 4 + 1)], hT[:, 2 * m:2 * m + 2, :].rearrange("p h d -> p (h d)"))
            h.then_inc(ev["hT_tr"], 1)

            for which, src in enumerate((dtt, dta)):
                for hd in range(HEADS):
                    r0, m = 64 * (hd % 2), hd // 2
                    h = MM(ps[r0:r0 + 64, 3 - which, NB * m:NB * (m + 1)],
                           src[0:NB, 2, hd:hd + 1].to_broadcast([NB, HD]), ident[0:NB, 0:NB], start=True, stop=True)
            h.then_inc(ev["sexp_mm"], 1)
            pe.wait_ge(ev["ce_ready"], 4)
            for b in range(NB):
                if b >= 2:
                    pe.wait_ge(ev["sh_prod"], b - 1)
                for j in range(4):
                    h = MM(ps[:, 4 + b % 2, P * j:P * (j + 1)], xa[:, KT + j, TP + b:TP + b + 1].to_broadcast([P, P]),
                           ident, start=True, stop=True)
                h.then_inc(ev["sbc_mm"], 1)
            pe.wait_ge(ev["ysq_ready"], 1)
            pe.wait_ge(ev["sh_prod"], NB)
            for g_ in range(GROUPS):
                for m in range(4):
                    h = MM(ps[:, 4 + g_, 0:TN], ones, ysq[:, 4 * g_ + m, :], start=(m == 0), stop=(m == 3))
            h.then_inc(ev["yvar_mm"], 1)

            pe.wait_ge(ev["conf_ready"], 1)
            pe.wait_ge(ev["hT_st"], 1)
            pe.wait_ge(ev["sdec_ready"], 1)
            pe.wait_ge(ev["yvar_ready"], 1)
            for p in range(8):
                pe.wait_ge(wo_landed[p % 4], 16 * (p // 4 + 1))
                if p == 4:
                    pe.wait_ge(ev["yn_ready"], 1)
                src = conv if p < 4 else yT
                for k in range(2):
                    kk = WO_K[p] % KT + k
                    for m in range(KT):
                        MM(ps[:, m, 0:TN], wout(p)[:, k, P * m:P * (m + 1)], src[:, kk, :],
                           start=(p == 0 and k == 0), stop=False, skip_group_check=True)
                nop_used(ev["wo_used"])
            for m in range(KT):
                for j, (c, r) in enumerate(tok):
                    h = MM(ps[:, m, c:c + r], x_tok[0:r, j, P * m:P * (m + 1)], ident[0:r, 0:r],
                           start=False, stop=(j == 2), skip_group_check=True)
            h.then_inc(ev["wo_mm"], 1)

            pe.wait_ge(ev["acc_ready"], 8)
            for j, (c, r) in enumerate(tok):
                for k in range(KT):
                    h = MM(ps[0:r, 6, NE * j:NE * (j + 1)], accT[:, k, c:c + r], wr[:, k, :],
                           start=(k == 0), stop=(k == KT - 1))
            h.then_inc(ev["lg_mm"], 1)
            for j, (c, r) in enumerate(tok):
                for m in range(KT):
                    h = TR(ps[0:r, 2 * j + m // 4, P * (m % 4):P * (m % 4 + 1)], accT[:, m, c:c + r])
                h.then_inc(ev["h_tr"], 1)
            pe.wait_ge(ev["gates_ready"], 3)
            for j, (c, r) in enumerate(tok):
                for i_ in range(j):
                    MM(ps[0:r, 7, NE * j:NE * (j + 1)], ones[:, 0:r], mask[:, i_, :], start=(i_ == 0), stop=False)
                MM(ps[0:r, 7, NE * j:NE * (j + 1)], tri_s[0:r, 0:r], mask[0:r, j, :], start=(j == 0), stop=True)
            for j, (c, r) in enumerate(tok):
                h = MM(ps[:, 7, 96:128], ones[0:r, :], mask[0:r, j, :], start=(j == 0), stop=(j == 2))
            h.then_inc(ev["pos_mm"], 1)
            for j, (c, r) in enumerate(tok):
                h = TR(ps[0:NE, 6, c:c + r], gates[0:r, j, 1:NE + 1])
            h.then_inc(ev["pt_done"], 1)

            def gather(n=CAP):
                for k in range(KT):
                    for j, (c, r) in enumerate(tok):
                        h = MM(ps[:, 4 + k // 4, CAP * (k % 4):CAP * (k % 4) + n], xn[0:r, j, P * k:P * (k + 1)], S[0:r, j, 0:n],
                               start=(j == 0), stop=(j == 2))
                h.then_inc(ev["xg_done"], 1)

            def scatter(lhs, rhs, n):
                for m in range(KT):
                    if m >= 2:
                        pe.wait_ge(ev["acc_done"], n + m - 1)
                    MM(ps[:, 7 - m % 2, 0:TN], lhs(m), rhs, start=True, stop=True).then_inc(ev["sc_done"], 1)

            def products(first, src, bank, i16, n=CAP):
                for p in range(first, first + 4):
                    pe.wait_ge(landed[p], i16)
                    for k in range(2):
                        kk = 2 * (p - first) + k
                        for m in range(KT):
                            h = MM(ps[:, bank + m // 4, CAP * (m % 4):CAP * (m % 4) + n], piece(p)[:, k, P * m:P * (m + 1)],
                                   src[:, kk, 0:n], start=(kk == 0 and m % 4 == 0), stop=(kk == KT - 1),
                                   skip_group_check=True)
                    h.then_inc(ev["piece_used"], 1)

            pe.wait_ge(ev["s_ready"], 1)
            pe.wait_ge(ev["xn_ready"], 3)
            gather()
            pe.wait_ge(ev["gt_ready"], 1)
            pe.wait_ge(ev["late_loaded"], 16)
            scatter(lambda m: bdn[0:NE, P * m:P * (m + 1)], gT[0:NE, :], 0)

            def turn_back():
                for m in range(KT):
                    h = TR(ps[:, 6 + m // 4, P * (m % 4):P * (m % 4 + 1)], yTs[:, m, :])
                h.then_inc(ev["ytr_done"], 1)

            def turn_slots():
                for j, (c, r) in enumerate(tok):
                    h = TR(ps[:, 6, c:c + r], Sg[0:r, j, :])
                h.then_inc(ev["pt_done"], 1)

            def finish_former(i):
                pe.wait_ge(ev["y_back"], i + 1)
                pe.wait_ge(ev["sg_ready"], i + 1)
                turn_slots()
                pe.wait_ge(ev["p_ready"], i + 1)
                scatter(lambda m: ys[:, P * m:P * (m + 1)], Pm, i * 8 + 8)

            def by_width(count, what):
                with pe.If(count < HALF + 1):
                    what(HALF)
                with pe.Else():
                    what(CAP)

            pe.wait_ge(ev["cnt_ready"], 1)
            with pe.Fori(0, NE) as i:
                count = pe.value_load(cnti[0:1, bass.ds(i, 1)], min_val=0, max_val=TN)
                following = pe.value_load(cnti[0:1, bass.ds(i + 1, 1)], min_val=0, max_val=TN)
                pe.wait_ge(ev["xg_ready"], i + 1)
                pe.wait_ge(ev["g_read"], i + 1)
                by_width(count, lambda n: products(0, xg, 0, i * 16 + 16, n))
                pe.wait_ge(ev["yt_ready"], i + 1)
                pe.wait_ge(ev["acc_done"], i * 8 + 8)
                turn_back()
                pe.wait_ge(ev["u_read"], i + 1)
                by_width(count, lambda n: products(4, xg, 2, i * 16 + 16, n))
                pe.wait_ge(ev["s_ready"], i + 2)
                by_width(following, gather)
                finish_former(i)
                pe.wait_ge(ev["hdn_ready"], i + 1)
                pe.wait_ge(ev["xg_ready"], i + 2)
                by_width(count, lambda n: products(8, hdn, 4, i * 16 + 16, n))
            pe.wait_ge(ev["yt_ready"], NE + 1)
            pe.wait_ge(ev["acc_done"], NE * 8 + 8)
            turn_back()
            finish_former(NE)

            pe.wait_ge(ev["o_tab"], 1)
            pe.wait_ge(ev["acc_done"], NE * 8 + 16)
            n_over = pe.value_load(otab[0:1, OVER:OVER + 1], min_val=0, max_val=OVER)
            with pe.Fori(0, OVER) as j:
                with pe.If(j < n_over):
                    pe.wait_ge(ev["s_ready"], j + NE + 2)
                    gather()
                    pe.wait_ge(ev["xg_ready"], j + NE + 2)
                    products(0, xg, 0, j * 16 + 16 * (NE + 1))
                    products(4, xg, 2, j * 16 + 16 * (NE + 1))
                    pe.wait_ge(ev["hdn_ready"], j + NE + 1)
                    products(8, hdn, 4, j * 16 + 16 * (NE + 1))
                    pe.wait_ge(ev["yt_ready"], j + NE + 2)
                    turn_back()
                    pe.wait_ge(ev["y_back"], j + NE + 2)
                    turn_slots()
                    pe.wait_ge(ev["p_ready"], j + NE + 2)
                    scatter(lambda m: ys[:, P * m:P * (m + 1)], Pm, j * 8 + 8 * (NE + 2))
                    pe.wait_ge(ev["acc_done"], j * 8 + 8 * (NE + 3))

            pe.wait_ge(ev["f_rd"], 1)
            for j, (c, r) in enumerate(tok):
                for m in range(KT):
                    h = TR(ps[0:r, 2 * j + m // 4, P * (m % 4):P * (m % 4 + 1)], accT[:, m, c:c + r])
                h.then_inc(ev["h_tr"], 1)


_INS = ["x_prompt", "x_sample", "state_ssm", "state_ssd_conv", "state_conf_conv", "meta_tokens", "g_mix", "w_in",
        "conv_ssd_w", "conv_ssd_b", "dt_bias", "a_log", "d_skip", "g_ssd_norm", "conv_conf_w", "conv_conf_b",
        "ln_conf_g", "ln_conf_b", "w_out", "g_ffn", "w_router", "b_router", "w_gate", "b_gate", "w_up", "b_up",
        "w_down", "b_down", "g_final"]
_OUTS = {"y_p": (1, SEQ, D), "y_s": (NB, 1, D), "ssm_p": (1, 1, HEADS, HD, NST), "ssd_p": (1, 1, SW - 1, XBC),
         "conf_p": (1, 1, CW - 1, D), "ssm_s": (1, NB, HEADS, HD, NST), "ssd_s": (1, NB, SW - 1, XBC),
         "conf_s": (1, NB, CW - 1, D)}


def kernel(**inputs):
    import numpy as _np
    import concourse.bacc as _bacc
    from concourse import mybir as _mybir
    from concourse.bass_utils import run_bass_kernel_spmd as _run

    nc = _bacc.Bacc("TRN2", target_bir_lowering=False, num_devices=1)
    arrays, ins, outs = {}, {}, {}
    for name in _INS:
        a = _np.ascontiguousarray(inputs[name])
        arrays[f"in_{name}"] = a
        ins[name] = nc.dram_tensor(f"in_{name}", a.shape, _mybir.dt.from_np(a.dtype), kind="ExternalInput").ap()
    for name, shape in _OUTS.items():
        outs[name] = nc.dram_tensor(f"out_{name}", shape, F32, kind="ExternalOutput").ap()
    build(nc, ins, outs)
    r = _run(nc, [arrays], core_ids=[0])
    return tuple(r.results[0][f"out_{name}"] for name in _OUTS)
```

```python
from contextlib import ExitStack

import concourse.bass as bass
from concourse import mybir
from concourse.alu_op_type import AluOpType as ALU

F32 = mybir.dt.float32
I32 = mybir.dt.int32
U32 = mybir.dt.uint32
ACT = mybir.ActivationFunctionType
AX = mybir.AxisListType.X

P = 128
D = 1024
KT = D // P
META, SEQ, NB = 16, 256, 8
TP = META + SEQ
T = TP + NB
TN = SEQ + NB
HEADS, HD, NST, GROUPS = 16, 64, 128, 2
HPG = HEADS // GROUPS
XBC = D + 2 * GROUPS * NST
XT_ = XBC // P
CW, SW = 31, 4
NE, TOPK = 32, 4
CAP = 128
HALF = 64
OVER = (TN * TOPK) // (CAP + 1)
EPS = 1e-5
LIMIT, ALPHA = 7.0, 1.702
FAR = 4096.0

COL_Z, COL_X, COL_DT, COL_VAL, COL_GATE = 0, D, D + XBC, D + XBC + HEADS, 2 * D + XBC + HEADS


def build(nc, I, O):
    ctx = ExitStack()
    with ctx:
        def sb(name, n, dt=F32):
            return ctx.enter_context(nc.sbuf_tensor(name, [P, n], dt))

        def sem(name):
            return ctx.enter_context(nc.semaphore(name))

        def view(t, off, *dims):
            n = 1
            for d in dims:
                n *= d
            a = t[:, off:off + n]
            if len(dims) == 1:
                return a
            names = "abc"[:len(dims)]
            return a.rearrange("p (" + " ".join(names) + ") -> p " + " ".join(names),
                               **dict(zip(names, dims)))

        def flat(ap):
            names = " ".join("abcd"[:len(ap.shape) - 1])
            return ap.rearrange(f"p {names} -> p ({names})")

        def bc(ap, axis, n):
            a = ap.unsqueeze(axis)
            s = list(a.shape)
            s[axis] = n
            return a.to_broadcast(s)

        PIECE = 2 * D
        NP = 12
        ring = sb("ring", NP * PIECE)
        extra = sb("extra", 4 * PIECE)
        acts = sb("acts", 3072 + 2240 + 2480 + 3136 + 3360 + 2112)
        small = sb("small", 3480)
        ps = ctx.enter_context(nc.psum_tensor("ps", [P, 8, 512], F32))

        o = 0
        x_tok = view(acts, o, 3, D); o += 3072
        uT = view(acts, o, KT, T); st_off = o; o += 2240
        cbuf = view(acts, o, KT, 30 + T); yT = view(acts, o, KT, TN); o += 2480
        xs_tok = view(acts, o, 3, D); conv = view(acts, o, KT, TN); cstage = view(acts, o + 2112, D); o += 3136
        xa = view(acts, o, XT_, T); hist_x = view(acts, o, XBC); xn = view(acts, o, 3, D); o += 3360
        zT = view(acts, o, KT, TN); hist_c = view(acts, o, 2, D); accT = zT; o += 2112
        csq = view(acts, 3072 + 2240, KT, TN)
        state_in = view(acts, st_off, 2, KT, P)
        t0 = 8 * PIECE
        csmp = view(ring, t0, KT, NB, CW)
        sprod = view(ring, t0, KT, P)
        xsmp = view(ring, t0 + 1984, XT_, NB, SW)
        xraw = view(ring, t0 + 2368, XT_, 3 + T)
        xstage = view(ring, t0 + 5764, XBC)
        xsig = view(ring, t0 + 5764, 6, T)
        s0 = t0 + 2368
        Mh = view(ring, s0, HPG, P)
        Ce = view(ring, s0 + 1024, HPG, P)
        ysq = view(ring, s0, KT, TN)
        zsig = view(ring, s0, KT, TN)
        xdt = view(ring, s0 + 2112, HEADS, HD)
        xdec = view(ring, s0 + 3136, HEADS, HD)
        hT = view(ring, s0 + 4160, HEADS, HD)
        btok = view(ring, s0 + 5184, GROUPS, NST)
        cbm = view(ring, s0 + 5440, P)

        so = [0]

        def sm(*dims):
            n = 1
            for d in dims:
                n *= d
            v = view(small, so[0], *dims)
            so[0] += n
            return v

        ident, tri, tri_s, ones = sm(P), sm(P), sm(P), sm(P)
        r_ = t0 + 5764
        vrow = view(ring, r_, P)
        vcol = sm(108)
        cwrow, cwcol = view(ring, r_ + 128, 2, P), sm(CW, KT)
        
        
        wdt, wr = sm(KT, HEADS), sm(KT, NE)
        brt, dtb, aneg, dsk = sm(NE), sm(HEADS), sm(HEADS), sm(KT)
        dtt, dta, dtw, dte, dtd = sm(4, HEADS), sm(4, HEADS), sm(4, HEADS), sm(4, HEADS), sm(4, HEADS)
        acum = sm(2, HEADS)
        dec, cdec = sm(HEADS), sm(HEADS)
        sgt = sm(2, T)
        stat = sm(4, 4)
        sdt, sdec = sm(KT, NB), sm(KT, NB)
        ysum = sm(KT)
        mu = sm(TN)
        assert so[0] <= 3480, so[0]
        gmx, gxb, gsn, gcb = vcol[:, 0:8], vcol[:, 8:20], vcol[:, 20:28], vcol[:, 28:36]
        glg, glb, gff, gxw = vcol[:, 36:44], vcol[:, 44:52], vcol[:, 52:60], vcol[:, 60:108]
        rstd = sgt[:, 0, :][:, 0:TN]
        rstd2 = sgt[:, 1, :][:, 0:TN]

        ge, sig = view(extra, 0, D), view(extra, 1024, D)
        ue, hdn = view(extra, 2048, D), view(extra, 3072, D)
        xg, ys = view(extra, 4096, D), view(extra, 5120, D)
        xT, hT_e = view(extra, 6144, KT, CAP), view(extra, 7168, KT, CAP)
        bg_rows, bu_rows = view(acts, 0, D), view(acts, D, D)
        Sg = view(acts, 2 * D, 6, CAP)
        oh = view(acts, 2 * D + 768, P)
        S = view(acts, 9840, 3, CAP)
        m0 = 3072
        Pm = view(acts, m0, 2, TN)
        bdn = view(acts, m0 + 528, D)
        gT = view(acts, m0 + 1552, TN)
        iota_f, iota_h = view(acts, m0 + 1816, P), view(acts, m0 + 1944, P)
        c0 = 5312
        slotp, gates = view(acts, c0, 3, NE + 2), view(acts, c0 + 102, 3, NE + 2)
        logit, top8 = view(acts, c0 + 204, 3, NE), view(acts, c0 + 300, 3, 8)
        topf, topw = view(acts, c0 + 324, 3, TOPK), view(acts, c0 + 336, 3, TOPK)
        eq, mask = view(acts, c0 + 348, TOPK, NE), view(acts, c0 + 476, 3, NE)
        tmp96 = view(acts, c0 + 572, 3, NE)
        cntf, nbo, cum = view(acts, c0 + 668, NE), view(acts, c0 + 700, NE), view(acts, c0 + 732, NE)
        ole, oe, ob = view(acts, c0 + 764, OVER, NE), view(acts, c0 + 1020, OVER + 1), view(acts, c0 + 1029, OVER)
        oslot = view(acts, c0 + 1037, 3)
        topi = view(acts, c0 + 1040, 3, 8).bitcast(U32)
        otab = view(acts, c0 + 1064, OVER + 1).bitcast(I32)
        zero32 = view(acts, c0 + 1073, NE)
        cnti = view(acts, c0 + 1111, NE + 2).bitcast(I32)
        rsum, nmax = view(acts, c0 + 1105, 3), view(acts, c0 + 1108, 3)
        hout = view(acts, 0, 3, D)
        gfin = view(acts, 7792, D)
        hsq = view(acts, 7792 + 1024, D)

        names = ("zeroed consts x_loaded x_tail vec_loaded bias_loaded hist_loaded misc_loaded wdt_loaded "
                 "ssq_ready rms_ready xs_ready vt_done vcol_ready xtr_done uT_ready htr_done hist_ready win_done "
                 "evac_done glu_done pad_ready dt_mm dt_ready dt_exp dt_v xst_tr xst_ready xst_out cst_tr "
                 "cst_ready kept_out conv_done mean_mm mu_ready cent_ready csq_ready var_mm var_ready std_ready "
                 "norm_ready csig_ready conf_ready xpre_ready xsig_ready xa_ready win_used z_sig acum_mm meta_exp "
                 "meta_v xtok_mm xdt_ready cb_mm cb_raw acb_mm d_ready e_ready ce_ready m_ready xdec_ready y_mm "
                 "st_mm y_ready hT_ready hT_tr hT_st hT_out sexp_mm sdec_ready st_in0 st_in1 sbc_mm sh_dec sh_bx "
                 "sh_new sh_prod sy_ready sh_out0 sh_out1 yg_ready ysq_ready yvar_mm yvar_ready ystd_ready "
                 "yn_ready wo_used wo_mm acc_ready h_tr hsq_ready hr_v hstd_ready xn_ready lg_mm nm_ready topexp "
                 "gates_ready pos_mm cnt_ready gt_ready ht_done ht_ready xt_done xt_ready xg_out oh_ready "
                 "rows_zeroed rows_loaded late_loaded xg_done pt_done sc_done g_ready u_read hdn_ready y_back "
                 "p_ready acc_done s_ready sg_ready sig_ready piece_used o_tab f_ready f_out f_rd iota_ready").split()
        ev = {n: sem(n) for n in names}
        landed = [sem(f"piece_landed{i}") for i in range(NP)]
        win_landed = [sem(f"win_landed{i}") for i in range(6)]
        wo_landed = [sem(f"wo_landed{i}") for i in range(4)]
        block = ctx.enter_context(nc.Block())

        CHUNKS = [(COL_VAL, "val", 0), (COL_GATE, "gate", 0), (COL_VAL + 512, "val", 4), (COL_GATE + 512, "gate", 4),
                  (COL_X, "xbc", 0), (COL_X + 512, "xbc", 4), (COL_X + 1024, "xbc", 8), (COL_Z, "z", 0), (COL_Z + 512, "z", 4)]
        PLACE = [(ring, 0), (ring, 4096), (ring, 8192), (ring, 12288), (extra, 0), (extra, 4096),
                 (ring, 0), (ring, 4096), (ring, 8192)]
        NC_ = len(CHUNKS)

        def win(c):
            return view(PLACE[c][0], PLACE[c][1], KT, 512)

        def wout(p):
            return view(extra, (p % 4) * PIECE, 2, D)

        def piece(p):
            return view(ring, p * PIECE, 2, D)

        WO_K = [8, 10, 12, 14, 0, 2, 4, 6]
        w_in, w_out = I["w_in"][0], I["w_out"][0]
        expert_w = [I[n] for n in ("w_gate", "w_up", "w_down")]

        def expert_piece(e, p):
            w = expert_w[p // 4]
            r = (p % 4) * 2 * P
            return w[0, bass.ds(e, 1), r:r + 2 * P, :].rearrange("o (k p) n -> p (o k) n", p=P)

        tok = [(0, P), (P, P), (2 * P, NB)]

        @block.sync
        def _(sp):
            xp, xs, mt = I["x_prompt"][0], I["x_sample"], I["meta_tokens"]
            sp.dma_start(x_tok[:, 0, :], xp[0:P]).then_inc(ev["x_loaded"], 16)
            sp.dma_start(x_tok[:, 1, :], xp[P:2 * P]).then_inc(ev["x_loaded"], 16)
            sp.wait_ge(ev["zeroed"], 1)
            sp.dma_start(x_tok[0:NB, 2, :], xs.rearrange("b o d -> (b o) d")).then_inc(ev["x_tail"], 16)
            sp.dma_start(x_tok[32:32 + META, 2, :], mt).then_inc(ev["x_tail"], 16)
            sp.dma_start(wdt, w_in[:, COL_DT:COL_DT + HEADS].rearrange("(k p) n -> p k n", p=P)).then_inc(ev["wdt_loaded"], 16)
            for c in range(NC_):
                if c >= 6:
                    sp.wait_ge(ev["win_used"], c - 5)
                sp.dma_start(win(c), w_in[:, CHUNKS[c][0]:CHUNKS[c][0] + 512].rearrange("(k p) n -> p k n", p=P)
                             ).then_inc(win_landed[c % 6], 16)

            def load_wout(p):
                sp.dma_start(wout(p), w_out[WO_K[p] * P:(WO_K[p] + 2) * P].rearrange("(k p) n -> p k n", p=P)
                             ).then_inc(wo_landed[p % 4], 16)

            sp.wait_ge(ev["win_used"], 6)
            for p in range(4):
                load_wout(p)
            sp.wait_ge(ev["win_used"], NC_)
            for b in range(2):
                sp.dma_start(state_in[:, b], I["state_ssm"][0, b].rearrange("h p n -> (h p) n").rearrange(
                    "(m q) n -> q m n", q=P)).then_inc((ev["st_in0"], ev["st_in1"])[b], 16)
            for p in range(8):
                sp.dma_start(piece(p), expert_piece(0, p)).then_inc(landed[p], 16)
            sp.wait_ge(ev["hT_st"], 1)
            sp.dma_start(O["ssm_p"][0, 0].rearrange("h p n -> (h p) n").rearrange("(m q) n -> q m n", q=P),
                         view(ring, s0 + 3136, KT, P)).then_inc(ev["hT_out"], 16)
            for b in range(NB):
                sp.wait_ge(ev["sh_new"], b + 1)
                sp.dma_start(O["ssm_s"][0, b].rearrange("h p n -> (h p) n").rearrange("(m q) n -> q m n", q=P),
                             state_in[:, b % 2]).then_inc((ev["sh_out0"], ev["sh_out1"])[b % 2], 16)
                if b + 2 < NB:
                    sp.wait_ge((ev["sh_out0"], ev["sh_out1"])[b % 2], 16 * (b // 2 + 1))
                    sp.wait_ge(ev["sh_prod"], b + 1)
                    sp.dma_start(state_in[:, b % 2], I["state_ssm"][0, b + 2].rearrange("h p n -> (h p) n").rearrange(
                        "(m q) n -> q m n", q=P)).then_inc((ev["st_in0"], ev["st_in1"])[b % 2], 16)
            sp.wait_ge(ev["sh_out0"], 16 * (NB // 2))
            sp.wait_ge(ev["sh_out1"], 16 * (NB // 2))
            sp.wait_ge(ev["sy_ready"], 1)
            sp.wait_ge(ev["hT_out"], 16)
            sp.dma_start(bdn[0:NE, :], I["b_down"][0]).then_inc(ev["late_loaded"], 16)
            sp.wait_ge(ev["yvar_mm"], 1)
            for p in range(8, NP):
                sp.dma_start(piece(p), expert_piece(0, p)).then_inc(landed[p], 16)
            for p in range(4, 8):
                sp.wait_ge(ev["wo_used"], p - 3)
                load_wout(p)
            sp.wait_ge(ev["wo_used"], 8)
            sp.dma_start(gfin, I["g_final"].partition_broadcast(P)).then_inc(ev["late_loaded"], 16)

            sp.wait_ge(ev["rows_zeroed"], 1)
            sp.dma_start(bg_rows[0:NE, :], I["b_gate"][0]).then_inc(ev["rows_loaded"], 16)
            sp.dma_start(bu_rows[0:NE, :], I["b_up"][0]).then_inc(ev["rows_loaded"], 16)

            with sp.Fori(0, NE - 1) as i:
                for p in range(NP):
                    sp.wait_ge(ev["piece_used"], i * NP + p + 1)
                    sp.dma_start(piece(p), expert_piece(i + 1, p)).then_inc(landed[p], 16)
            sp.wait_ge(ev["o_tab"], 1)
            n_over = sp.value_load(otab[0:1, OVER:OVER + 1], min_val=0, max_val=OVER)
            with sp.Fori(0, OVER) as j:
                with sp.If(j < n_over):
                    e = sp.value_load(otab[0:1, bass.ds(j, 1)], min_val=0, max_val=NE - 1)
                    sp.wait_ge(ev["piece_used"], j * NP + NE * NP)
                    for p in range(NP):
                        sp.dma_start(piece(p), expert_piece(e, p)).then_inc(landed[p], 16)
            sp.wait_ge(ev["f_ready"], 3)
            sp.dma_start(O["y_p"][0, 0:P], hout[:, 0, :]).then_inc(ev["f_out"], 16)
            sp.dma_start(O["y_p"][0, P:2 * P], hout[:, 1, :]).then_inc(ev["f_out"], 16)
            sp.dma_start(O["y_s"].rearrange("b o d -> (b o) d"), hout[0:NB, 2, :]).then_inc(ev["f_out"], 16)
            sp.wait_ge(ev["f_out"], 48)
            sp.wait_ge(ev["hT_out"], 16)
            sp.wait_ge(ev["kept_out"], 64)
            sp.wait_ge(ev["xst_out"], 32)

        @block.gpsimd
        def _(g):
            nc.gpsimd.memset(x_tok[0:48, 2, :], 0.0)
            nc.gpsimd.memset(stat, 1.0).then_inc(ev["zeroed"], 1)
            for t, base, op in ((ident, 0, ALU.not_equal), (tri, 0, ALU.is_gt), (tri_s, 0, ALU.is_ge)):
                nc.gpsimd.memset(t, 0.0)
            nc.gpsimd.memset(ones, 1.0)
            g.drain()
            for t, op in ((ident, ALU.not_equal), (tri, ALU.is_gt), (tri_s, ALU.is_ge)):
                nc.gpsimd.affine_select(out=t, in_=t, compare_op=op, fill=1.0, base=0, pattern=[[-1, P]],
                                        channel_multiplier=1)
            g.drain()
            nc.gpsimd.memset(cbuf[:, :, 0:30], 0.0)
            nc.gpsimd.memset(xraw[:, :, 0:3], 0.0).then_inc(ev["consts"], 1)
            n = 0
            for c, (_, kind, m0_) in enumerate(CHUNKS):
                if kind == "gate":
                    for m in range(4):
                        g.wait_ge(ev["evac_done"], 4 * c + m + 1)
                        v = cbuf[:, m0_ + m, 30:30 + T]
                        nc.gpsimd.tensor_tensor(v, v, sgt[:, n % 2, :], ALU.mult).then_inc(ev["glu_done"], 1)
                        n += 1
            g.drain()
            nc.gpsimd.tensor_copy(csmp[:, :, :, 30], cbuf[:, :, 30 + TP:30 + T]).then_inc(ev["pad_ready"], 1)
            g.wait_ge(ev["evac_done"], 28)
            nc.gpsimd.tensor_copy(xsmp[:, :, :, 3], xraw[:, :, 3 + TP:3 + T]).then_inc(ev["pad_ready"], 1)
            for u in range(4):
                c, gr = u // 2, u % 2
                g.wait_ge(ev["cb_raw"], u + 1)
                nc.gpsimd.affine_select(out=cbm, in_=cbm, compare_op=ALU.is_ge, fill=0.0, base=0,
                                        pattern=[[1, P]], channel_multiplier=-1)
                g.drain()
                g.wait_ge(ev["xdec_ready"], u + 1)
                nc.gpsimd.tensor_tensor(Mh, Mh, bc(cbm, 1, HPG), ALU.mult)
                nc.gpsimd.tensor_tensor(Ce, Ce, bc(xa[:, 10 + gr, 16 + c * P:16 + (c + 1) * P], 1, HPG),
                                        ALU.mult)
                g.drain()
                nc.gpsimd.tensor_copy(dec[:, 8:16], dec[:, 0:8]).then_inc(ev["m_ready"], 1)
            for b in range(NB):
                g.wait_ge(ev["sh_dec"], b + 1)
                g.wait_ge(ev["sh_bx"], b + 1)
                nc.gpsimd.tensor_tensor(state_in[:, b % 2], state_in[:, b % 2], sprod, ALU.add).then_inc(ev["sh_new"], 1)
            g.wait_ge(ev["late_loaded"], 16)
            nc.gpsimd.iota(iota_f, [[1, P]], base=0, channel_multiplier=0,
                           allow_small_or_imprecise_dtypes=True)
            nc.gpsimd.iota(iota_h, [[1, P]], base=-HALF, channel_multiplier=0,
                           allow_small_or_imprecise_dtypes=True).then_inc(ev["iota_ready"], 1)
            g.wait_ge(ev["wo_mm"], 1)
            nc.gpsimd.memset(view(acts, 0, 2 * D), 0.0)
            nc.gpsimd.memset(oh, 0.0).then_inc(ev["rows_zeroed"], 1)

        @block.scalar
        def _(a):
            act = nc.scalar.activation
            rows = lambda name, n: I[name][0].rearrange("(k c) -> k c", c=P)[0:n]
            for r0, ap, n in ((0, rows("g_mix", 8), 8), (8, rows("conv_ssd_b", 12), 12), (20, rows("g_ssd_norm", 8), 8),
                              (28, rows("conv_conf_b", 8), 8), (36, rows("ln_conf_g", 8), 8),
                              (44, rows("ln_conf_b", 8), 8), (52, rows("g_ffn", 8), 8),
                              (60, I["conv_ssd_w"][0].rearrange("k (m c) -> (k m) c", c=P), 48)):
                a.dma_start(vrow[r0:r0 + n, :], ap).then_inc(ev["vec_loaded"], 16)
            cw = I["conv_conf_w"][0].rearrange("k (m c) -> (k m) c", c=P)
            for j in range(2):
                a.dma_start(cwrow[0:124, j, :], cw[124 * j:124 * (j + 1)]).then_inc(ev["bias_loaded"], 16)
            a.dma_start(dtb, I["dt_bias"][0].partition_broadcast(P)).then_inc(ev["misc_loaded"], 16)
            a.dma_start(aneg, I["a_log"][0].partition_broadcast(P)).then_inc(ev["misc_loaded"], 16)
            a.dma_start(brt, I["b_router"][0].partition_broadcast(P)).then_inc(ev["misc_loaded"], 16)
            a.dma_start(wr, I["w_router"][0].rearrange("(k p) n -> p k n", p=P)).then_inc(ev["misc_loaded"], 16)
            dsv = I["d_skip"][0].rearrange("(m j) -> j m", j=2)
            for j in range(2):
                with nc.allow_non_contiguous_dma("sixteen scalars"):
                    a.dma_start(dsk[64 * j:64 * j + 64, :], dsv[j].partition_broadcast(64)).then_inc(ev["misc_loaded"], 16)

            a.wait_ge(ev["x_loaded"], 32)
            a.wait_ge(ev["zeroed"], 1)
            a.wait_ge(ev["x_tail"], 32)
            act(xs_tok[:, 0, :], x_tok[:, 0, :], ACT.Square, accum_out=stat[:, 0, 0:1])
            act(xs_tok[:, 1, :], x_tok[:, 1, :], ACT.Square, accum_out=stat[:, 0, 1:2])
            act(xs_tok[0:48, 2, :], x_tok[0:48, 2, :], ACT.Square, accum_out=stat[0:48, 0, 2:3])
            a.drain()
            act(stat[:, 3, 0:3], stat[:, 0, 0:3], ACT.Copy).then_inc(ev["ssq_ready"], 1)
            a.wait_ge(ev["rms_ready"], 1)
            act(stat[:, 2, 0:3], stat[:, 1, 0:3], ACT.Sqrt).then_inc(ev["std_ready"], 1)
            a.wait_ge(ev["rms_ready"], 2)
            act(xs_tok[:, 0, :], x_tok[:, 0, :], ACT.Copy, scale=stat[:, 1, 0:1]).then_inc(ev["xs_ready"], 1)
            act(xs_tok[:, 1, :], x_tok[:, 1, :], ACT.Copy, scale=stat[:, 1, 1:2]).then_inc(ev["xs_ready"], 1)
            act(xs_tok[0:48, 2, :], x_tok[0:48, 2, :], ACT.Copy, scale=stat[0:48, 1, 2:3]).then_inc(ev["xs_ready"], 1)
            hc = I["state_conf_conv"][0].rearrange("b k d -> (b k) d")
            for j in range(2):
                a.dma_start(hist_c[0:120, j, :], hc[120 * j:120 * (j + 1)]).then_inc(ev["hist_loaded"], 16)
            a.dma_start(hist_x[0:24, :], I["state_ssd_conv"][0].rearrange("b k d -> (b k) d")).then_inc(ev["hist_loaded"], 16)
            a.dma_start(O["conf_s"][0, :, 0:CW - 2, :], I["state_conf_conv"][0, :, 1:CW - 1, :]).then_inc(ev["kept_out"], 16)
            a.dma_start(O["ssd_s"][0, :, 0:SW - 2, :], I["state_ssd_conv"][0, :, 1:SW - 1, :]).then_inc(ev["kept_out"], 16)
            a.wait_ge(ev["dt_v"], 1)
            act(dte, dta, ACT.Exp, scale=-1.0).then_inc(ev["dt_exp"], 1)
            a.wait_ge(ev["dt_v"], 2)
            act(dta, dtw, ACT.Ln).then_inc(ev["dt_exp"], 1)
            a.wait_ge(ev["misc_loaded"], 96)
            act(aneg, aneg, ACT.Exp).then_inc(ev["dt_exp"], 1)

            n = 0
            for c, (_, kind, m0_) in enumerate(CHUNKS):
                for m in range(4):
                    j = 4 * c + m
                    if kind == "z" and m0_ + m == 0:
                        a.wait_ge(ev["hist_ready"], 5)
                    a.wait_ge(ev["win_done"], j + 1)
                    src = ps[:, j % 4, 0:T]
                    mm = m0_ + m
                    if kind == "val":
                        act(cbuf[:, mm, 30:30 + T], src, ACT.Copy).then_inc(ev["evac_done"], 1)
                    elif kind == "gate":
                        if n >= 2:
                            a.wait_ge(ev["glu_done"], n - 1)
                        act(sgt[:, n % 2, :], src, ACT.Sigmoid).then_inc(ev["evac_done"], 1)
                        n += 1
                    elif kind == "xbc":
                        act(xraw[:, mm, 3:3 + T], src, ACT.Copy).then_inc(ev["evac_done"], 1)
                    else:
                        act(zT[:, mm, :], ps[:, j % 4, 0:TN], ACT.Copy).then_inc(ev["evac_done"], 1)
            a.wait_ge(ev["cst_ready"], 1)
            a.dma_start(O["conf_p"][0, 0], cstage[0:CW - 1, :]).then_inc(ev["kept_out"], 16)
            a.dma_start(O["conf_s"][0, :, CW - 2, :], cstage[CW - 1:CW - 1 + NB, :]).then_inc(ev["kept_out"], 16)
            a.wait_ge(ev["xst_ready"], 1)
            a.dma_start(O["ssd_p"][0, 0], xstage[0:SW - 1, :]).then_inc(ev["xst_out"], 16)
            a.dma_start(O["ssd_s"][0, :, SW - 2, :], xstage[SW - 1:SW - 1 + NB, :]).then_inc(ev["xst_out"], 16)

            for h in range(2):
                a.wait_ge(ev["xpre_ready"], 1)
                if h:
                    a.wait_ge(ev["xa_ready"], 1)
                else:
                    a.wait_ge(ev["xst_out"], 32)
                act(flat(xsig), flat(xa[:, 6 * h:6 * h + 6, :]), ACT.Sigmoid).then_inc(ev["xsig_ready"], 1)
            a.wait_ge(ev["mean_mm"], 1)
            act(mu, ps[:, 4, 0:TN], ACT.Copy, scale=1.0 / D).then_inc(ev["mu_ready"], 1)
            a.wait_ge(ev["cent_ready"], 1)
            act(flat(csq), flat(conv), ACT.Square).then_inc(ev["csq_ready"], 1)
            a.wait_ge(ev["var_ready"], 1)
            act(rstd2, rstd, ACT.Sqrt).then_inc(ev["std_ready"], 1)
            a.wait_ge(ev["norm_ready"], 1)
            a.wait_ge(ev["var_mm"], 1)
            for m in range(KT):
                act(csq[:, m, :], conv[:, m, :], ACT.Sigmoid, scale=glg[:, m:m + 1], bias=glb[:, m:m + 1]
                    ).then_inc(ev["csig_ready"], 1)

            a.wait_ge(ev["meta_v"], 1)
            act(dec[0:META, :], dec[0:META, :], ACT.Exp).then_inc(ev["meta_exp"], 1)
            for u in range(4):
                a.wait_ge(ev["d_ready"], u + 1)
                act(flat(Mh), flat(Mh), ACT.Exp).then_inc(ev["e_ready"], 1)
                if u:
                    a.wait_ge(ev["y_mm"], u)
                act(flat(Ce), ps[:, 4:6, :].rearrange("p a b -> p (a b)"), ACT.Exp).then_inc(ev["ce_ready"], 1)
            a.wait_ge(ev["sexp_mm"], 1)
            act(flat(sdec), ps[:, 2, 0:64], ACT.Exp).then_inc(ev["sdec_ready"], 1)
            for b in range(NB):
                a.wait_ge((ev["st_in0"], ev["st_in1"])[b % 2], 16 * (b // 2 + 1))
                if b == 0:
                    a.wait_ge(ev["sdec_ready"], 1)
                for m in range(KT):
                    h = act(state_in[:, b % 2, m, :], state_in[:, b % 2, m, :], ACT.Copy, scale=sdec[:, m, b:b + 1])
                h.then_inc(ev["sh_dec"], 1)
            a.wait_ge(ev["y_mm"], 4)
            a.wait_ge(ev["m_ready"], 4)
            act(flat(zsig), flat(zT), ACT.Sigmoid).then_inc(ev["z_sig"], 1)
            a.wait_ge(ev["yg_ready"], 1)
            act(flat(ysq), flat(yT), ACT.Square).then_inc(ev["ysq_ready"], 1)
            a.wait_ge(ev["yvar_ready"], 1)
            act(rstd, rstd, ACT.Sqrt)
            act(rstd2, rstd2, ACT.Sqrt)
            a.drain()
            act(mu[:, 0:1], mu[:, 0:1], ACT.Copy).then_inc(ev["ystd_ready"], 1)

            for j, (c, r) in enumerate(tok):
                a.wait_ge(ev["h_tr"], j + 1)
                act(hsq[0:r, :], ps[0:r, 2 * j:2 * j + 2, :].rearrange("p a b -> p (a b)"), ACT.Square,
                    accum_out=stat[0:r, 0, j:j + 1])
                a.drain()
            act(stat[:, 3, 0:3], stat[:, 0, 0:3], ACT.Copy).then_inc(ev["hsq_ready"], 1)
            a.wait_ge(ev["hr_v"], 1)
            act(stat[:, 2, 0:3], stat[:, 1, 0:3], ACT.Sqrt).then_inc(ev["hstd_ready"], 1)
            a.wait_ge(ev["hr_v"], 2)
            for j, (c, r) in enumerate(tok):
                act(xn[0:r, j, :], ps[0:r, 2 * j:2 * j + 2, :].rearrange("p a b -> p (a b)"), ACT.Copy,
                    scale=stat[0:r, 1, j:j + 1]).then_inc(ev["xn_ready"], 1)
            a.wait_ge(ev["nm_ready"], 1)
            for j, (c, r) in enumerate(tok):
                act(topw[0:r, j, :], top8[0:r, j, 0:TOPK], ACT.Exp, bias=nmax[0:r, j:j + 1],
                    accum_out=rsum[0:r, j:j + 1])
                a.drain()
            act(stat[:, 3, 0:3], stat[:, 0, 0:3], ACT.Copy).then_inc(ev["topexp"], 1)

            def back(dst, bank):
                return act(dst, ps[:, bank:bank + 2, :].rearrange("p a b -> p (a b)"), ACT.Copy)

            def inputs_out(i):
                a.wait_ge(ev["xg_done"], i + 2)
                back(xg, 4).then_inc(ev["xg_out"], 1)

            def places_out(i):
                a.wait_ge(ev["pt_done"], i + 2)
                act(Pm, ps[:, 6:8, 0:TN], ACT.Copy).then_inc(ev["p_ready"], 1)

            def sigmoid(i):
                a.wait_ge(ev["g_ready"], i + 1)
                act(sig, ge, ACT.Sigmoid, scale=ALPHA).then_inc(ev["sig_ready"], 1)

            def hidden_out(i):
                a.wait_ge(ev["ht_done"], i + 1)
                back(flat(hT_e), 0).then_inc(ev["ht_ready"], 1)

            def output_out(i):
                a.wait_ge(ev["piece_used"], i * NP + NP)
                back(ys, 4).then_inc(ev["y_back"], 1)

            inputs_out(-1)
            with a.Fori(0, NE) as i:
                sigmoid(i)
                inputs_out(i)
                places_out(i)
                hidden_out(i)
                output_out(i)
            places_out(NE)

            a.wait_ge(ev["o_tab"], 1)
            n_over = a.value_load(otab[0:1, OVER:OVER + 1], min_val=0, max_val=OVER)
            with a.Fori(0, OVER) as j:
                with a.If(j < n_over):
                    inputs_out(j + NE)
                    sigmoid(j + NE)
                    hidden_out(j + NE)
                    output_out(j + NE)
                    places_out(j + NE + 1)

            for j, (c, r) in enumerate(tok):
                a.wait_ge(ev["h_tr"], j + 4)
                act(hsq[0:r, :], ps[0:r, 2 * j:2 * j + 2, :].rearrange("p a b -> p (a b)"), ACT.Square,
                    accum_out=stat[0:r, 0, j:j + 1])
                a.drain()
            act(stat[:, 3, 0:3], stat[:, 0, 0:3], ACT.Copy).then_inc(ev["hsq_ready"], 1)
            a.wait_ge(ev["hr_v"], 3)
            act(stat[:, 2, 0:3], stat[:, 1, 0:3], ACT.Sqrt).then_inc(ev["hstd_ready"], 1)

        @block.vector
        def _(v):
            V = nc.vector
            TT, TS, STT = V.tensor_tensor, V.tensor_scalar, V.scalar_tensor_tensor

            V.memset(dtt, 0.0)
            for k, (dst, src) in enumerate(((vcol, ps[:, 4, 0:108]), (flat(cwcol), ps[:, 5, 0:248]))):
                v.wait_ge(ev["vt_done"], k + 1)
                V.tensor_copy(dst, src).then_inc(ev["vcol_ready"], 1)
            v.wait_ge(ev["ssq_ready"], 1)
            TS(stat[:, 1, 0:3], stat[:, 0, 0:3], 1.0 / D, EPS, ALU.mult, ALU.add).then_inc(ev["rms_ready"], 1)
            v.wait_ge(ev["std_ready"], 1)
            V.reciprocal(stat[:, 1, 0:3], stat[:, 2, 0:3]).then_inc(ev["rms_ready"], 1)
            for k in range(4):
                j, h = k // 2, k % 2
                v.wait_ge(ev["xtr_done"], k + 1)
                TT(uT[:, 4 * h:4 * h + 4, META + P * j:META + P * (j + 1)], ps[:, 4 + k, :].rearrange("p (m t) -> p m t", m=4),
                   bc(gmx[:, 4 * h:4 * h + 4], 2, P), ALU.mult).then_inc(ev["uT_ready"], 1)
            v.wait_ge(ev["xtr_done"], 5)
            tail = ps[:, 4, 0:384].rearrange("p (m t) -> p m t", m=8)
            TT(uT[:, :, TP:T], tail[:, :, 0:NB], bc(gmx, 2, NB), ALU.mult).then_inc(ev["uT_ready"], 1)
            TT(uT[:, :, 0:META], tail[:, :, 32:48], bc(gmx, 2, META), ALU.mult).then_inc(ev["uT_ready"], 1)

            v.wait_ge(ev["dt_mm"], 1)
            v.drain()
            dp = ps[:, 5, 0:64].rearrange("p (g h) -> p g h", g=4)
            for g_, r in ((0, P), (1, P), (2, NB), (3, META)):
                V.tensor_copy(dtt[0:r, g_, :], dp[0:r, g_, :])
            v.wait_ge(ev["misc_loaded"], 96)
            v.drain()
            TT(dtt, dtt, bc(dtb, 1, 4), ALU.add)
            v.drain()
            TS(dtd, dtt, -1.0, None, ALU.mult)
            v.drain()
            TT(dta, dtt, dtd, ALU.max)
            v.drain()
            TS(dtd, dtt, 0.0, None, ALU.max).then_inc(ev["dt_v"], 1)
            v.wait_ge(ev["dt_exp"], 1)
            TS(dtw, dte, 1.0, None, ALU.add).then_inc(ev["dt_v"], 1)
            v.wait_ge(ev["dt_exp"], 2)
            v.drain()
            TS(dtw, dtw, -1.0, None, ALU.add)
            v.drain()
            TS(dtt, dtw, 0.0, None, ALU.is_equal)
            v.drain()
            TT(dtw, dtw, dtt, ALU.add)
            TT(dtt, dtt, dte, ALU.mult)
            v.drain()
            V.reciprocal(dtw, dtw)
            TT(dta, dta, dte, ALU.mult)
            TT(dtt, dtt, dtd, ALU.add)
            v.drain()
            TT(dta, dta, dtw, ALU.mult)
            v.drain()
            TT(dtt, dtt, dta, ALU.add)
            v.wait_ge(ev["dt_exp"], 3)
            v.drain()
            STT(dta, dtt, -1.0, bc(aneg, 1, 4), ALU.mult, ALU.mult)
            v.drain()
            TT(wr, wr, bc(gff, 2, NE), ALU.mult).then_inc(ev["dt_ready"], 1)

            v.wait_ge(ev["consts"], 1)
            for h in range(2):
                v.wait_ge(ev["glu_done"], 4 * h + 4)
                for k in range(CW):
                    for m in range(4 * h, 4 * h + 4):
                        src = cbuf[:, m, META + k:META + k + SEQ]
                        w = cwcol[:, k, m:m + 1]
                        if k == 0:
                            TS(conv[:, m, 0:SEQ], src, w, gcb[:, m:m + 1], ALU.mult, ALU.add)
                        else:
                            STT(conv[:, m, 0:SEQ], src, w, conv[:, m, 0:SEQ], ALU.mult, ALU.add)
                    v.drain()
            for k in range(4):
                j, h = k // 2, k % 2
                v.wait_ge(ev["htr_done"], k + 1)
                V.tensor_copy(csmp[:, 4 * h:4 * h + 4, 4 * j:4 * j + 4, 0:30],
                              ps[:, 4 + k, 0:480].rearrange("p (m b k) -> p m b k", m=4, b=4)).then_inc(ev["hist_ready"], 1)
            v.wait_ge(ev["htr_done"], 5)
            V.tensor_copy(xsmp[:, :, :, 0:3], ps[:, 4, 0:288].rearrange("p (m b k) -> p m b k", m=12, b=8)
                          ).then_inc(ev["hist_ready"], 1)
            v.wait_ge(ev["cst_tr"], 1)
            V.tensor_copy(cstage[0:38, :], ps[0:38, 5:7, :].rearrange("p a b -> p (a b)")).then_inc(ev["cst_ready"], 1)
            v.wait_ge(ev["xst_tr"], 1)
            V.tensor_copy(xstage[0:11, :], ps[0:11, 5:8, :].rearrange("p a b -> p (a b)")).then_inc(ev["xst_ready"], 1)
            v.wait_ge(ev["pad_ready"], 1)
            v.drain()
            for m in range(KT):
                TT(csmp[:, m], csmp[:, m], bc(cwcol[:, :, m], 1, NB), ALU.mult)
            v.drain()
            V.tensor_reduce(conv[:, :, SEQ:TN], csmp, AX, ALU.add)
            v.drain()
            TT(conv[:, :, SEQ:TN], conv[:, :, SEQ:TN], bc(gcb, 2, NB), ALU.add).then_inc(ev["conv_done"], 1)

            xw = gxw.rearrange("p (k m) -> p k m", k=SW)
            for m3 in range(0, XT_, 4):
                v.wait_ge(ev["evac_done"], 16 + m3 + 4)
                for k in range(SW):
                    for m in range(m3, m3 + 4):
                        src = xraw[:, m, k:k + TP]
                        if k == 0:
                            TS(xa[:, m, 0:TP], src, xw[:, k, m:m + 1], gxb[:, m:m + 1], ALU.mult, ALU.add)
                        else:
                            STT(xa[:, m, 0:TP], src, xw[:, k, m:m + 1], xa[:, m, 0:TP], ALU.mult, ALU.add)
                    v.drain()
            v.wait_ge(ev["pad_ready"], 2)
            TT(xsmp, xsmp, bc(xw.rearrange("p k m -> p m k"), 2, NB), ALU.mult)
            v.drain()
            V.tensor_reduce(xa[:, :, TP:T], xsmp, AX, ALU.add)
            v.drain()
            TT(xa[:, :, TP:T], xa[:, :, TP:T], bc(gxb, 2, NB), ALU.add).then_inc(ev["xpre_ready"], 1)
            for h in range(2):
                v.wait_ge(ev["xsig_ready"], h + 1)
                TT(flat(xa[:, 6 * h:6 * h + 6, :]), flat(xa[:, 6 * h:6 * h + 6, :]), flat(xsig), ALU.mult
                   ).then_inc(ev["xa_ready"], 1)

            v.wait_ge(ev["mu_ready"], 1)
            TT(conv, conv, bc(mu, 1, KT), ALU.subtract).then_inc(ev["cent_ready"], 1)
            v.wait_ge(ev["var_mm"], 1)
            TS(rstd, ps[:, 5, 0:TN], 1.0 / D, EPS, ALU.mult, ALU.add).then_inc(ev["var_ready"], 1)
            v.wait_ge(ev["std_ready"], 2)
            V.reciprocal(rstd, rstd2)
            v.drain()
            TT(conv, conv, bc(rstd, 1, KT), ALU.mult).then_inc(ev["norm_ready"], 1)
            for m in range(KT):
                v.wait_ge(ev["csig_ready"], m + 1)
                TS(conv[:, m, :], conv[:, m, :], glg[:, m:m + 1], glb[:, m:m + 1], ALU.mult, ALU.add)
            v.drain()
            TT(flat(conv), flat(conv), flat(csq), ALU.mult).then_inc(ev["conf_ready"], 1)

            v.wait_ge(ev["acum_mm"], 1)
            am = ps[:, 6, 0:64].rearrange("p (g h) -> p g h", g=4)
            V.tensor_copy(acum, am[:, 0:2, :])
            V.tensor_copy(dec[0:META, :], am[0:META, 2, :])
            v.drain()
            TT(dec[0:META, :], am[0:META, 3, :], dec[0:META, :], ALU.subtract).then_inc(ev["meta_v"], 1)

            def rows_of_chunk(n, r, g_):
                v.wait_ge(ev["xtok_mm"], n + 1)
                for h in range(2):
                    TT(xdt[0:r, 8 * h:8 * h + 8, :], ps[0:r, h, :].rearrange("p (h d) -> p h d", h=HPG),
                       bc(dtt[0:r, g_, 8 * h:8 * h + 8], 2, HD), ALU.mult)
                V.tensor_copy(flat(btok[0:r]), ps[0:r, 2, 0:256]).then_inc(ev["xdt_ready"], 1)

            v.wait_ge(ev["xst_out"], 32)
            rows_of_chunk(0, META, 3)
            v.wait_ge(ev["meta_exp"], 1)
            v.drain()
            TT(xdec[0:META], xdt[0:META], bc(dec[0:META, :], 2, HD), ALU.mult).then_inc(ev["hT_ready"], 1)
            for g_ in range(GROUPS):
                v.wait_ge(ev["st_mm"], g_ + 1)
                V.tensor_copy(hT[:, 8 * g_:8 * g_ + 8, :], ps[:, 7, :].rearrange("p (h d) -> p h d", h=HPG)
                              ).then_inc(ev["hT_ready"], 1)
            for c in range(2):
                if c:
                    v.wait_ge(ev["st_mm"], 6 - 2)
                rows_of_chunk(1 + c, P, c)
                for g_ in range(GROUPS):
                    u = 2 * c + g_
                    v.wait_ge(ev["cb_mm"], u + 1)
                    if u:
                        v.wait_ge(ev["m_ready"], u)
                    V.tensor_copy(cbm, ps[:, 3, 0:P]).then_inc(ev["cb_raw"], 1)
                    v.wait_ge(ev["acb_mm"], u + 1)
                    if u:
                        v.wait_ge(ev["y_mm"], u)
                    for h in range(2):
                        TT(Mh[:, 4 * h:4 * h + 4, :], ps[:, 4 + h, :].rearrange("p (h d) -> p h d", h=4),
                           bc(acum[:, c, 8 * g_ + 4 * h:8 * g_ + 4 * h + 4], 2, P), ALU.subtract)
                    v.drain()
                    TS(flat(Mh), flat(Mh), 0.0, None, ALU.min).then_inc(ev["d_ready"], 1)
                    v.wait_ge(ev["e_ready"], u + 1)
                    V.tensor_copy(dec[:, 0:8], Mh[:, :, P - 1])
                    v.wait_ge(ev["ce_ready"], u + 1)
                    V.tensor_copy(cdec[:, 0:8], Ce[:, :, P - 1])
                    v.drain()
                    TT(xdec[:, 8 * g_:8 * g_ + 8, :], xdt[:, 8 * g_:8 * g_ + 8, :], bc(dec[:, 0:8], 2, HD), ALU.mult
                       ).then_inc(ev["xdec_ready"], 1)
                    v.wait_ge(ev["y_mm"], u + 1)
                    for k in range(4):
                        m = 4 * g_ + k
                        h = STT(yT[:, m, c * P:(c + 1) * P], xa[:, m, META + c * P:META + (c + 1) * P], dsk[:, m:m + 1],
                                ps[:, 6, k * P:(k + 1) * P], ALU.mult, ALU.add)
                    h.then_inc(ev["y_ready"], 1)
                    TT(hT[:, 8 * g_:8 * g_ + 8, :], hT[:, 8 * g_:8 * g_ + 8, :], bc(cdec[:, 0:8], 2, HD), ALU.mult)
                    v.drain()
                    v.wait_ge(ev["st_mm"], 3 + u)
                    TT(hT[:, 8 * g_:8 * g_ + 8, :], hT[:, 8 * g_:8 * g_ + 8, :],
                       ps[:, 7, :].rearrange("p (h d) -> p h d", h=HPG), ALU.add).then_inc(ev["hT_ready"], 1)
            v.wait_ge(ev["hT_tr"], 1)
            V.tensor_copy(view(ring, s0 + 3136, D), ps[:, 0:2, :].rearrange("p a b -> p (a b)")).then_inc(ev["hT_st"], 1)

            v.wait_ge(ev["sexp_mm"], 1)
            V.tensor_copy(flat(sdt), ps[:, 3, 0:64])
            v.drain()
            TT(sdt, sdt, xa[:, 0:KT, TP:T], ALU.mult)
            v.drain()
            for b in range(NB):
                v.wait_ge(ev["sbc_mm"], b + 1)
                sbc = ps[:, 4 + b % 2, :].rearrange("p (j n) -> p j n", j=4)
                if b:
                    v.drain()
                for g_ in range(GROUPS):
                    h = TT(sprod[:, 4 * g_:4 * g_ + 4, :], bc(sbc[:, g_, :], 1, 4), bc(sdt[:, 4 * g_:4 * g_ + 4, b], 2, P),
                           ALU.mult)
                h.then_inc(ev["sh_bx"], 1)
                v.wait_ge(ev["sh_new"], b + 1)
                for g_ in range(GROUPS):
                    h = TT(sprod[:, 4 * g_:4 * g_ + 4, :], bc(sbc[:, 2 + g_, :], 1, 4),
                           state_in[:, b % 2, 4 * g_:4 * g_ + 4, :], ALU.mult)
                h.then_inc(ev["sh_prod"], 1)
                v.drain()
                V.tensor_reduce(yT[:, :, SEQ + b], sprod, AX, ALU.add)
            v.drain()
            TT(sdt, xa[:, 0:KT, TP:T], bc(dsk, 2, NB), ALU.mult)
            v.drain()
            TT(yT[:, :, SEQ:TN], yT[:, :, SEQ:TN], sdt, ALU.add).then_inc(ev["sy_ready"], 1)
            v.wait_ge(ev["z_sig"], 1)
            TT(flat(zT), flat(zT), flat(zsig), ALU.mult)
            v.drain()
            TT(flat(yT), flat(yT), flat(zT), ALU.mult).then_inc(ev["yg_ready"], 1)
            v.wait_ge(ev["yvar_mm"], 1)
            TS(rstd, ps[:, 4, 0:TN], 2.0 / D, EPS, ALU.mult, ALU.add)
            TS(rstd2, ps[:, 5, 0:TN], 2.0 / D, EPS, ALU.mult, ALU.add).then_inc(ev["yvar_ready"], 1)
            v.wait_ge(ev["ystd_ready"], 1)
            V.reciprocal(rstd, rstd)
            V.reciprocal(rstd2, rstd2)
            v.drain()
            for m in range(KT):
                h = STT(yT[:, m, :], yT[:, m, :], gsn[:, m:m + 1], rstd if m < 4 else rstd2, ALU.mult, ALU.mult)
            h.then_inc(ev["yn_ready"], 1)

            v.wait_ge(ev["wo_mm"], 1)
            v.drain()
            for m in range(KT):
                V.tensor_copy(accT[:, m, :], ps[:, m, 0:TN]).then_inc(ev["acc_ready"], 1)
            V.memset(slotp, -FAR)
            V.memset(gates, 0.0)
            V.memset(ys, 0.0).then_inc(ev["y_back"], 1)
            V.memset(zero32, 0.0).then_inc(ev["ht_ready"], 1)
            V.memset(nbo, 0.0).then_inc(ev["u_read"], 1)
            v.wait_ge(ev["hsq_ready"], 1)
            TS(stat[:, 1, 0:3], stat[:, 0, 0:3], 1.0 / D, EPS, ALU.mult, ALU.add).then_inc(ev["hr_v"], 1)
            v.wait_ge(ev["hstd_ready"], 1)
            V.reciprocal(stat[:, 1, 0:3], stat[:, 2, 0:3]).then_inc(ev["hr_v"], 1)
            v.drain()
            v.wait_ge(ev["lg_mm"], 1)
            lg = ps[:, 6, 0:96].rearrange("p (j e) -> p j e", j=3)
            for j, (c, r) in enumerate(tok):
                STT(logit[0:r, j, :], lg[0:r, j, :], stat[0:r, 1, j:j + 1], brt[0:r, :], ALU.mult, ALU.add)
            v.drain()
            for j, (c, r) in enumerate(tok):
                V.max(top8[0:r, j, :], logit[0:r, j, :])
            v.drain()
            for j, (c, r) in enumerate(tok):
                V.max_index(topi[0:r, j, :], top8[0:r, j, :], logit[0:r, j, :])
                h = TS(nmax[0:r, j:j + 1], top8[0:r, j, 0:1], -1.0, None, ALU.mult)
            h.then_inc(ev["nm_ready"], 1)
            v.drain()
            for j, (c, r) in enumerate(tok):
                V.tensor_copy(topf[0:r, j, :], topi[0:r, j, 0:TOPK])
            v.wait_ge(ev["iota_ready"], 1)
            v.drain()
            for j, (c, r) in enumerate(tok):
                TT(eq[0:r], bc(iota_f[0:r, 0:NE], 1, TOPK), bc(topf[0:r, j, :], 2, NE), ALU.is_equal)
                v.drain()
                V.tensor_reduce(mask[0:r, j, :], eq[0:r].rearrange("p k e -> p e k"), AX, ALU.add)
                if j == 0:
                    v.wait_ge(ev["topexp"], 1)
                    V.reciprocal(rsum[:, 0:2], rsum[:, 0:2])
                    V.reciprocal(rsum[0:NB, 2:3], rsum[0:NB, 2:3])
                    v.drain()
                TS(topw[0:r, j, :], topw[0:r, j, :], rsum[0:r, j:j + 1], None, ALU.mult)
                v.drain()
                TT(eq[0:r], eq[0:r], bc(topw[0:r, j, :], 2, NE), ALU.mult)
                v.drain()
                h = V.tensor_reduce(gates[0:r, j, 1:NE + 1], eq[0:r].rearrange("p k e -> p e k"), AX, ALU.add)
                h.then_inc(ev["gates_ready"], 1)
                TS(tmp96[0:r, j, :], mask[0:r, j, :], FAR, -FAR, ALU.mult, ALU.add)
                v.drain()
            v.wait_ge(ev["pos_mm"], 1)
            pm = ps[:, 7, 0:128].rearrange("p (j e) -> p j e", j=4)
            for j, (c, r) in enumerate(tok):
                TT(slotp[0:r, j, 1:NE + 1], pm[0:r, j, :], tmp96[0:r, j, :], ALU.add)
            V.tensor_copy(cntf, pm[:, 3, :])
            V.memset(cnti[0:1, :], 0)
            v.drain()
            V.tensor_copy(cnti[0:1, 1:NE + 1], pm[0:1, 3, :])
            v.drain()
            V.memset(nbo, 0.0).then_inc(ev["cnt_ready"], 1)
            v.drain()

            def choose_slots(col):
                for j, (c, r) in enumerate(tok):
                    h = TS(S[0:r, j, :], iota_f[0:r, :], slotp[0:r, j, bass.ds(col, 1)], None, ALU.is_equal)
                return h

            def choose_gates(col):
                for k, io in enumerate((iota_f, iota_h)):
                    for j, (c, r) in enumerate(tok):
                        h = TS(Sg[0:r, 3 * k + j, :], io[0:r, :], slotp[0:r, j, bass.ds(col, 1)],
                               gates[0:r, j, bass.ds(col, 1)], ALU.is_equal, ALU.mult)
                return h

            def choose_bias(e):
                return V.tensor_copy(oh[0:NE, :], ident[0:NE, bass.ds(e, 1)].to_broadcast([NE, P]))

            v.wait_ge(ev["kept_out"], 64)
            choose_slots(1).then_inc(ev["s_ready"], 1)
            v.wait_ge(ev["rows_zeroed"], 1)
            choose_bias(0).then_inc(ev["oh_ready"], 1)
            TS(nbo, cntf, float(CAP), None, ALU.is_gt)
            TS(cum, cntf, float(2 * CAP), None, ALU.is_gt)
            V.memset(zero32, 0.0)
            v.drain()
            TT(nbo, nbo, cum, ALU.add)
            v.drain()
            V.tensor_tensor_scan(cum, nbo, zero32, 0.0, ALU.add, ALU.add)
            v.drain()
            for k in range(OVER):
                TS(ole[:, k, :], cum, float(k), None, ALU.is_le)
            v.drain()
            V.tensor_reduce(oe[:, 0:OVER], ole, AX, ALU.add)
            V.tensor_copy(oe[:, OVER:OVER + 1], cum[:, NE - 1:NE])
            v.drain()
            TT(ole, ole, bc(nbo, 1, OVER), ALU.mult)
            v.drain()
            V.tensor_reduce(ob, ole, AX, ALU.add)
            TS(oe[:, 0:OVER], oe[:, 0:OVER], float(NE - 1), None, ALU.min)
            v.drain()
            V.tensor_copy(otab, oe).then_inc(ev["o_tab"], 1)
            TS(ob, ob, -float(CAP), None, ALU.mult)
            for k in range(OVER):
                v.drain()
                TS(ob[:, k:k + 1], ob[:, k:k + 1], float(CAP * (k + 1)), None, ALU.add)
            v.wait_ge(ev["pt_done"], 1)
            V.tensor_copy(gT[0:NE, :], ps[0:NE, 6, 0:TN]).then_inc(ev["gt_ready"], 1)

            def take_inputs(n):
                src = ps[:, 6:8, :].rearrange("p a b -> p (a b)")
                if n == HALF:
                    return TT(xT[:, 0:4, :].rearrange("p c (h s) -> p c h s", h=2),
                              src[:, 0:512].rearrange("p (c h s) -> p c h s", c=4, h=2),
                              bc(gff.rearrange("p (h c) -> p c h", h=2), 3, HALF), ALU.mult)
                return TT(xT, src.rearrange("p (k s) -> p k s", k=KT), bc(gff, 2, CAP), ALU.mult)

            def by_width(count, what):
                with v.If(count < HALF + 1):
                    what(HALF)
                with v.Else():
                    what(CAP)

            def add_back(n):
                for m in range(KT):
                    v.wait_ge(ev["sc_done"], n + m + 1)
                    TT(accT[:, m, :], ps[:, 7 - m % 2, 0:TN], accT[:, m, :], ALU.add).then_inc(ev["acc_done"], 1)

            def swiglu(n):
                gate, up = (ps[:, b:b + 2, :].rearrange("p a b -> p (a b)") for b in (0, 2))
                v.wait_ge(ev["piece_used"], n * NP + 4)
                TS(ge, gate, LIMIT, None, ALU.min).then_inc(ev["g_ready"], 1)
                v.wait_ge(ev["piece_used"], n * NP + 8)
                TS(ue, up, LIMIT, -LIMIT, ALU.min, ALU.max).then_inc(ev["u_read"], 1)
                v.drain()
                STT(ue, ue, 1.0, ge, ALU.add, ALU.mult)
                v.drain()
                v.wait_ge(ev["sig_ready"], n + 1)
                TT(hdn, ue, sig, ALU.mult).then_inc(ev["hdn_ready"], 1)

            add_back(0)
            v.wait_ge(ev["xt_done"], 1)
            by_width(v.value_load(cnti[0:1, 1:2], min_val=0, max_val=TN),
                     lambda n: take_inputs(n).then_inc(ev["xt_ready"], 1))
            with v.Fori(0, NE) as i:
                following = v.value_load(cnti[0:1, bass.ds(i + 2, 1)], min_val=0, max_val=TN)
                v.wait_ge(ev["pt_done"], i + 1)
                choose_gates(i).then_inc(ev["sg_ready"], 1)
                v.wait_ge(ev["xg_done"], i + 1)
                choose_slots(i + 2).then_inc(ev["s_ready"], 1)
                swiglu(i)
                choose_bias(i + 1).then_inc(ev["oh_ready"], 1)
                add_back(i * 8 + 8)

                def following_inputs(n):
                    v.wait_ge(ev["xt_done"], i + 2)
                    take_inputs(n).then_inc(ev["xt_ready"], 1)

                by_width(following, following_inputs)
            v.wait_ge(ev["pt_done"], NE + 1)
            choose_gates(NE).then_inc(ev["sg_ready"], 1)
            add_back(NE * 8 + 8)

            n_over = v.value_load(otab[0:1, OVER:OVER + 1], min_val=0, max_val=OVER)
            with v.Fori(0, OVER) as j:
                with v.If(j < n_over):
                    e = v.value_load(otab[0:1, bass.ds(j, 1)], min_val=0, max_val=NE - 1)
                    v.drain()
                    TS(oslot, slotp[:, :, bass.ds(e + 1, 1)].rearrange("p j o -> p (j o)"), ob[:, bass.ds(j, 1)], None,
                       ALU.subtract)
                    v.drain()
                    for t, (c, r) in enumerate(tok):
                        TS(S[0:r, t, :], iota_f[0:r, :], oslot[0:r, t:t + 1], None, ALU.is_equal)
                        TS(Sg[0:r, t, :], iota_f[0:r, :], oslot[0:r, t:t + 1], gates[0:r, t, bass.ds(e + 1, 1)],
                           ALU.is_equal, ALU.mult)
                    choose_bias(e)
                    v.drain()
                    V.memset(zero32, 0.0).then_inc(ev["s_ready"], 1)
                    v.wait_ge(ev["xt_done"], j + NE + 2)
                    take_inputs(CAP).then_inc(ev["xt_ready"], 1)
                    swiglu(j + NE)
                    add_back(j * 8 + 8 * (NE + 2))

            v.drain()
            V.memset(zero32, 0.0).then_inc(ev["f_rd"], 1)
            v.wait_ge(ev["hsq_ready"], 2)
            TS(stat[:, 1, 0:3], stat[:, 0, 0:3], 1.0 / D, EPS, ALU.mult, ALU.add).then_inc(ev["hr_v"], 1)
            v.wait_ge(ev["hstd_ready"], 2)
            V.reciprocal(stat[:, 1, 0:3], stat[:, 2, 0:3])
            v.wait_ge(ev["late_loaded"], 32)
            v.drain()
            for j, (c, r) in enumerate(tok):
                STT(hout[0:r, j, :], ps[0:r, 2 * j:2 * j + 2, :].rearrange("p a b -> p (a b)"), stat[0:r, 1, j:j + 1],
                    gfin[0:r, :], ALU.mult, ALU.mult).then_inc(ev["f_ready"], 1)

        @block.tensor
        def _(pe):
            MM = nc.tensor.matmul

            def TR(out, in_):
                r = in_.shape[0]
                return nc.tensor.transpose(out, in_, ident[0:r, 0:r])

            def ident_at(r0, n):
                return ident[r0:r0 + n, r0:r0 + n]

            pe.wait_ge(ev["consts"], 1)
            pe.wait_ge(ev["vec_loaded"], 16 * 8)
            TR(ps[:, 4, 0:108], vrow[0:108, :]).then_inc(ev["vt_done"], 1)
            pe.wait_ge(ev["bias_loaded"], 32)
            for j in range(2):
                h = TR(ps[:, 5, 124 * j:124 * (j + 1)], cwrow[0:124, j, :])
            h.then_inc(ev["vt_done"], 1)
            for k in range(4):
                j, h_ = k // 2, k % 2
                pe.wait_ge(ev["xs_ready"], j + 1)
                pe.wait_ge(ev["vcol_ready"], min(k + 1, 2))
                for m in range(4):
                    h = TR(ps[:, 4 + k, P * m:P * (m + 1)], xs_tok[:, j, P * (4 * h_ + m):P * (4 * h_ + m + 1)])
                h.then_inc(ev["xtr_done"], 1)
            pe.wait_ge(ev["xs_ready"], 3)
            pe.wait_ge(ev["uT_ready"], 1)
            for m in range(KT):
                h = TR(ps[:, 4, 48 * m:48 * (m + 1)], xs_tok[0:48, 2, P * m:P * (m + 1)])
            h.then_inc(ev["xtr_done"], 1)
            pe.wait_ge(ev["uT_ready"], 6)
            pe.wait_ge(ev["wdt_loaded"], 16)
            for g_, (c, r) in enumerate(((META, P), (META + P, P), (TP, NB), (0, META))):
                for k in range(KT):
                    h = MM(ps[0:r, 5, HEADS * g_:HEADS * (g_ + 1)], uT[:, k, c:c + r], wdt[:, k, :],
                           start=(k == 0), stop=(k == KT - 1))
            h.then_inc(ev["dt_mm"], 1)

            def w_in_chunk(c):
                pe.wait_ge(win_landed[c % 6], 16 * (c // 6 + 1))
                kind = CHUNKS[c][1]
                w = win(c)
                for m in range(4):
                    j = 4 * c + m
                    if j >= 4:
                        pe.wait_ge(ev["evac_done"], j - 3)
                    lo = META if kind == "z" else 0
                    for k in range(KT):
                        h = MM(ps[:, j % 4, 0:T - lo], w[:, k, P * m:P * (m + 1)], uT[:, k, lo:T],
                               start=(k == 0), stop=(k == KT - 1))
                    h.then_inc(ev["win_done"], 1)
                nop_used(ev["win_used"])

            def nop_used(s_):
                pe.drain().then_inc(s_, 1)

            for c in range(4):
                w_in_chunk(c)
            pe.wait_ge(ev["hist_loaded"], 48)
            pe.wait_ge(ev["dt_v"], 1)
            for k in range(4):
                j, h_ = k // 2, k % 2
                for m in range(4):
                    h = TR(ps[:, 4 + k, 120 * m:120 * (m + 1)], hist_c[0:120, j, P * (4 * h_ + m):P * (4 * h_ + m + 1)])
                h.then_inc(ev["htr_done"], 1)
            w_in_chunk(4)
            w_in_chunk(5)
            pe.wait_ge(ev["hist_ready"], 1)
            for m in range(XT_):
                h = TR(ps[:, 4, 24 * m:24 * (m + 1)], hist_x[0:24, P * m:P * (m + 1)])
            h.then_inc(ev["htr_done"], 1)
            pe.wait_ge(ev["hist_ready"], 3)
            pe.wait_ge(ev["glu_done"], 8)
            for m in range(KT):
                h = TR(ps[0:38, 5 + m // 4, P * (m % 4):P * (m % 4 + 1)], cbuf[:, m, 30 + T - 38:30 + T])
            h.then_inc(ev["cst_tr"], 1)
            w_in_chunk(6)
            pe.wait_ge(ev["hist_ready"], 4)
            pe.wait_ge(ev["cst_ready"], 1)
            pe.wait_ge(ev["evac_done"], 28)
            for m in range(XT_):
                h = TR(ps[0:11, 5 + m // 4, P * (m % 4):P * (m % 4 + 1)], xraw[:, m, 3 + T - 11:3 + T])
            h.then_inc(ev["xst_tr"], 1)
            w_in_chunk(7)
            w_in_chunk(8)

            pe.wait_ge(ev["conv_done"], 1)
            for m in range(KT):
                h = MM(ps[:, 4, 0:TN], ones, conv[:, m, :], start=(m == 0), stop=(m == KT - 1))
            h.then_inc(ev["mean_mm"], 1)
            pe.wait_ge(ev["csq_ready"], 1)
            pe.wait_ge(ev["xst_ready"], 1)
            for m in range(KT):
                h = MM(ps[:, 5, 0:TN], ones, csq[:, m, :], start=(m == 0), stop=(m == KT - 1))
            h.then_inc(ev["var_mm"], 1)

            pe.wait_ge(ev["dt_ready"], 1)
            for c in range(2):
                MM(ps[:, 6, HEADS * c:HEADS * (c + 1)], tri, dta[:, c, :], start=True, stop=True)
            MM(ps[0:META, 6, 32:48], tri[0:META, 0:META], dta[0:META, 3, :], start=True, stop=True)
            MM(ps[0:META, 6, 48:64], ones[0:META, 0:META], dta[0:META, 3, :], start=True, stop=True
               ).then_inc(ev["acum_mm"], 1)

            def chunk_rows(n, c, r):
                pe.wait_ge(ev["xa_ready"], 2)
                if n:
                    pe.wait_ge(ev["xdt_ready"], n)
                for m in range(KT):
                    TR(ps[0:r, m // 4, P * (m % 4):P * (m % 4 + 1)], xa[:, m, c:c + r])
                for g_ in range(GROUPS):
                    h = TR(ps[0:r, 2, P * g_:P * (g_ + 1)], xa[:, KT + g_, c:c + r])
                h.then_inc(ev["xtok_mm"], 1)

            pe.wait_ge(ev["evac_done"], 36)
            chunk_rows(0, 0, META)
            pe.wait_ge(ev["xdt_ready"], 1)
            for g_ in range(GROUPS):
                pe.wait_ge(ev["hT_ready"], 1 + g_)
                MM(ps[:, 7, :], btok[0:META, g_, :], xdec[0:META, 8 * g_:8 * g_ + 8, :].rearrange("p h d -> p (h d)"),
                   start=True, stop=True).then_inc(ev["st_mm"], 1)
            for c in range(2):
                cs = META + c * P
                chunk_rows(1 + c, cs, P)
                for g_ in range(GROUPS):
                    u = 2 * c + g_
                    if u:
                        pe.wait_ge(ev["cb_raw"], u)
                    MM(ps[:, 3, 0:P], xa[:, KT + g_, cs:cs + P], xa[:, KT + 2 + g_, cs:cs + P], start=True, stop=True
                       ).then_inc(ev["cb_mm"], 1)
                    pe.wait_ge(ev["mu_ready"], 1)
                    pe.wait_ge(ev["var_ready"], 1)
                    if u:
                        pe.wait_ge(ev["ce_ready"], u)
                    for k in range(HPG):
                        h = MM(ps[:, 4 + k // 4, P * (k % 4):P * (k % 4 + 1)],
                               dta[:, c, 8 * g_ + k:8 * g_ + k + 1].to_broadcast([P, P]), tri, start=True, stop=True)
                    h.then_inc(ev["acb_mm"], 1)
                    pe.wait_ge(ev["xdt_ready"], 2 + c)
                    pe.wait_ge(ev["m_ready"], u + 1)
                    pe.wait_ge(ev["hT_ready"], 3 + u)
                    pe.wait_ge(ev["meta_v"], 1)
                    if u:
                        pe.wait_ge(ev["y_ready"], u)
                    for k in range(HPG):
                        r0 = 64 * (k % 2)
                        dst = ps[r0:r0 + 64, 6, P * (k // 2):P * (k // 2 + 1)]
                        MM(dst, xdt[:, 8 * g_ + k, :], Mh[:, k, :], start=True, stop=False)
                        h = MM(dst, hT[:, 8 * g_ + k, :], Ce[:, k, :], start=False, stop=True)
                    h.then_inc(ev["y_mm"], 1)
                    pe.wait_ge(ev["xdec_ready"], u + 1)
                    MM(ps[:, 7, :], btok[:, g_, :], xdec[:, 8 * g_:8 * g_ + 8, :].rearrange("p h d -> p (h d)"),
                       start=True, stop=True).then_inc(ev["st_mm"], 1)
            pe.wait_ge(ev["hT_ready"], 7)
            for m in range(KT):
                h = TR(ps[:, m // 4, P * (m % 4):P * (m % 4 + 1)], hT[:, 2 * m:2 * m + 2, :].rearrange("p h d -> p (h d)"))
            h.then_inc(ev["hT_tr"], 1)

            for which, src in enumerate((dtt, dta)):
                for hd in range(HEADS):
                    r0, m = 64 * (hd % 2), hd // 2
                    h = MM(ps[r0:r0 + 64, 3 - which, NB * m:NB * (m + 1)],
                           src[0:NB, 2, hd:hd + 1].to_broadcast([NB, HD]), ident[0:NB, 0:NB], start=True, stop=True)
            h.then_inc(ev["sexp_mm"], 1)
            pe.wait_ge(ev["ce_ready"], 4)
            for b in range(NB):
                if b >= 2:
                    pe.wait_ge(ev["sh_prod"], b - 1)
                for j in range(4):
                    h = MM(ps[:, 4 + b % 2, P * j:P * (j + 1)], xa[:, KT + j, TP + b:TP + b + 1].to_broadcast([P, P]),
                           ident, start=True, stop=True)
                h.then_inc(ev["sbc_mm"], 1)
            pe.wait_ge(ev["ysq_ready"], 1)
            pe.wait_ge(ev["sh_prod"], NB)
            for g_ in range(GROUPS):
                for m in range(4):
                    h = MM(ps[:, 4 + g_, 0:TN], ones, ysq[:, 4 * g_ + m, :], start=(m == 0), stop=(m == 3))
            h.then_inc(ev["yvar_mm"], 1)

            pe.wait_ge(ev["conf_ready"], 1)
            pe.wait_ge(ev["hT_st"], 1)
            pe.wait_ge(ev["sdec_ready"], 1)
            pe.wait_ge(ev["yvar_ready"], 1)
            for p in range(8):
                pe.wait_ge(wo_landed[p % 4], 16 * (p // 4 + 1))
                if p == 4:
                    pe.wait_ge(ev["yn_ready"], 1)
                src = conv if p < 4 else yT
                for k in range(2):
                    kk = WO_K[p] % KT + k
                    for m in range(KT):
                        MM(ps[:, m, 0:TN], wout(p)[:, k, P * m:P * (m + 1)], src[:, kk, :],
                           start=(p == 0 and k == 0), stop=False, skip_group_check=True)
                nop_used(ev["wo_used"])
            for m in range(KT):
                for j, (c, r) in enumerate(tok):
                    h = MM(ps[:, m, c:c + r], x_tok[0:r, j, P * m:P * (m + 1)], ident[0:r, 0:r],
                           start=False, stop=(j == 2), skip_group_check=True)
            h.then_inc(ev["wo_mm"], 1)

            pe.wait_ge(ev["acc_ready"], 8)
            for j, (c, r) in enumerate(tok):
                for k in range(KT):
                    h = MM(ps[0:r, 6, NE * j:NE * (j + 1)], accT[:, k, c:c + r], wr[:, k, :],
                           start=(k == 0), stop=(k == KT - 1))
            h.then_inc(ev["lg_mm"], 1)
            for j, (c, r) in enumerate(tok):
                for m in range(KT):
                    h = TR(ps[0:r, 2 * j + m // 4, P * (m % 4):P * (m % 4 + 1)], accT[:, m, c:c + r])
                h.then_inc(ev["h_tr"], 1)
            pe.wait_ge(ev["gates_ready"], 3)
            for j, (c, r) in enumerate(tok):
                for i_ in range(j):
                    MM(ps[0:r, 7, NE * j:NE * (j + 1)], ones[:, 0:r], mask[:, i_, :], start=(i_ == 0), stop=False)
                MM(ps[0:r, 7, NE * j:NE * (j + 1)], tri_s[0:r, 0:r], mask[0:r, j, :], start=(j == 0), stop=True)
            for j, (c, r) in enumerate(tok):
                h = MM(ps[:, 7, 96:128], ones[0:r, :], mask[0:r, j, :], start=(j == 0), stop=(j == 2))
            h.then_inc(ev["pos_mm"], 1)
            for j, (c, r) in enumerate(tok):
                h = TR(ps[0:NE, 6, c:c + r], gates[0:r, j, 1:NE + 1])
            h.then_inc(ev["pt_done"], 1)

            def halves(n, bank):
                if n == HALF:
                    return [ps[HALF * h:HALF * (h + 1), bank, :] for h in range(2)]
                return [ps[:, bank + h, :] for h in range(2)]

            def gather(n):
                for j, (c, r) in enumerate(tok):
                    for h_, dst in enumerate(halves(n, 4)):
                        h = MM(dst, S[0:r, j, 0:n], xn[0:r, j, 512 * h_:512 * (h_ + 1)], start=(j == 0), stop=(j == 2))
                h.then_inc(ev["xg_done"], 1)

            def turn(src, n, bank, done):
                for c in range(4 if n == HALF else 8):
                    h = TR(ps[:, bank + c // 4, P * (c % 4):P * (c % 4 + 1)], src[:, P * c:P * (c + 1)])
                h.then_inc(done, 1)

            def bias(n, rows, bank):
                for h_, dst in enumerate(halves(n, bank)):
                    MM(dst, oh[:, 0:n], rows[:, 512 * h_:512 * (h_ + 1)], start=True, stop=False, skip_group_check=True)

            def products(n, first, src, bank, i16, fresh=False):
                for p in range(first, first + 4):
                    pe.wait_ge(landed[p], i16)
                    for k in range(2):
                        kk = 2 * (p - first) + k
                        x = src[:, kk % 4, HALF * (kk // 4):HALF * (kk // 4 + 1)] if n == HALF else src[:, kk, :]
                        for h_, dst in enumerate(halves(n, bank)):
                            h = MM(dst, x, piece(p)[:, k, 512 * h_:512 * (h_ + 1)], start=(fresh and kk == 0),
                                   stop=(kk == KT - 1), skip_group_check=True)
                    h.then_inc(ev["piece_used"], 1)

            def scatter(lhs, rhs, n):
                for m in range(KT):
                    if m >= 2:
                        pe.wait_ge(ev["acc_done"], n + m - 1)
                    MM(ps[:, 7 - m % 2, 0:TN], lhs(m), rhs(m), start=True, stop=True).then_inc(ev["sc_done"], 1)

            def turn_slots():
                for k in range(2):
                    for j, (c, r) in enumerate(tok):
                        h = TR(ps[:, 6 + k, c:c + r], Sg[0:r, 3 * k + j, :])
                h.then_inc(ev["pt_done"], 1)

            def scatter_rows(n, i8):
                if n == HALF:
                    scatter(lambda m: ys[:, P * (m % 4):P * (m % 4 + 1)], lambda m: Pm[:, m // 4, :], i8)
                else:
                    scatter(lambda m: ys[:, P * m:P * (m + 1)], lambda m: Pm[:, 0, :], i8)

            def by_width(count, what):
                with pe.If(count < HALF + 1):
                    what(HALF)
                with pe.Else():
                    what(CAP)

            def count_of(i):
                return pe.value_load(cnti[0:1, bass.ds(i, 1)], min_val=0, max_val=TN)

            pe.wait_ge(ev["cnt_ready"], 1)
            pe.wait_ge(ev["s_ready"], 1)
            pe.wait_ge(ev["xn_ready"], 3)
            first = count_of(1)
            by_width(first, gather)
            pe.wait_ge(ev["gt_ready"], 1)
            pe.wait_ge(ev["late_loaded"], 16)
            scatter(lambda m: bdn[0:NE, P * m:P * (m + 1)], lambda m: gT[0:NE, :], 0)
            pe.wait_ge(ev["xg_out"], 1)
            pe.wait_ge(ev["acc_done"], 8)
            by_width(first, lambda n: turn(xg, n, 6, ev["xt_done"]))
            pe.wait_ge(ev["rows_loaded"], 32)
            with pe.Fori(0, NE) as i:
                former, count, following = count_of(i), count_of(i + 1), count_of(i + 2)
                pe.wait_ge(ev["xt_ready"], i + 1)
                pe.wait_ge(ev["oh_ready"], i + 1)
                pe.wait_ge(ev["ht_ready"], i + 1)
                pe.wait_ge(ev["u_read"], i + 1)

                def gate_up(n):
                    bias(n, bg_rows, 0)
                    products(n, 0, xT, 0, i * 16 + 16)
                    bias(n, bu_rows, 2)
                    products(n, 4, xT, 2, i * 16 + 16)

                by_width(count, gate_up)
                pe.wait_ge(ev["s_ready"], i + 2)
                pe.wait_ge(ev["y_back"], i + 1)
                by_width(following, gather)
                pe.wait_ge(ev["sg_ready"], i + 1)
                pe.wait_ge(ev["acc_done"], i * 8 + 8)
                turn_slots()
                pe.wait_ge(ev["p_ready"], i + 1)
                by_width(former, lambda n: scatter_rows(n, i * 8 + 8))
                pe.wait_ge(ev["hdn_ready"], i + 1)
                by_width(count, lambda n: turn(hdn, n, 0, ev["ht_done"]))
                pe.wait_ge(ev["xg_out"], i + 2)
                pe.wait_ge(ev["acc_done"], i * 8 + 16)
                by_width(following, lambda n: turn(xg, n, 6, ev["xt_done"]))
                pe.wait_ge(ev["ht_ready"], i + 2)
                by_width(count, lambda n: products(n, 8, hT_e, 4, i * 16 + 16, fresh=True))
            pe.wait_ge(ev["y_back"], NE + 1)
            pe.wait_ge(ev["sg_ready"], NE + 1)
            pe.wait_ge(ev["xt_ready"], NE + 1)
            turn_slots()
            pe.wait_ge(ev["p_ready"], NE + 1)
            by_width(count_of(NE), lambda n: scatter_rows(n, NE * 8 + 8))

            pe.wait_ge(ev["o_tab"], 1)
            pe.wait_ge(ev["acc_done"], NE * 8 + 16)
            n_over = pe.value_load(otab[0:1, OVER:OVER + 1], min_val=0, max_val=OVER)
            with pe.Fori(0, OVER) as j:
                with pe.If(j < n_over):
                    pe.wait_ge(ev["s_ready"], j + NE + 2)
                    gather(CAP)
                    pe.wait_ge(ev["xg_out"], j + NE + 2)
                    turn(xg, CAP, 6, ev["xt_done"])
                    pe.wait_ge(ev["xt_ready"], j + NE + 2)
                    bias(CAP, bg_rows, 0)
                    products(CAP, 0, xT, 0, j * 16 + 16 * (NE + 1))
                    pe.wait_ge(ev["u_read"], j + NE + 1)
                    bias(CAP, bu_rows, 2)
                    products(CAP, 4, xT, 2, j * 16 + 16 * (NE + 1))
                    pe.wait_ge(ev["hdn_ready"], j + NE + 1)
                    turn(hdn, CAP, 0, ev["ht_done"])
                    pe.wait_ge(ev["ht_ready"], j + NE + 2)
                    products(CAP, 8, hT_e, 4, j * 16 + 16 * (NE + 1), fresh=True)
                    turn_slots()
                    pe.wait_ge(ev["y_back"], j + NE + 2)
                    pe.wait_ge(ev["p_ready"], j + NE + 2)
                    scatter_rows(CAP, j * 8 + 8 * (NE + 2))
                    pe.wait_ge(ev["acc_done"], j * 8 + 8 * (NE + 3))

            pe.wait_ge(ev["f_rd"], 1)
            for j, (c, r) in enumerate(tok):
                for m in range(KT):
                    h = TR(ps[0:r, 2 * j + m // 4, P * (m % 4):P * (m % 4 + 1)], accT[:, m, c:c + r])
                h.then_inc(ev["h_tr"], 1)


_INS = ["x_prompt", "x_sample", "state_ssm", "state_ssd_conv", "state_conf_conv", "meta_tokens", "g_mix", "w_in",
        "conv_ssd_w", "conv_ssd_b", "dt_bias", "a_log", "d_skip", "g_ssd_norm", "conv_conf_w", "conv_conf_b",
        "ln_conf_g", "ln_conf_b", "w_out", "g_ffn", "w_router", "b_router", "w_gate", "b_gate", "w_up", "b_up",
        "w_down", "b_down", "g_final"]
_OUTS = {"y_p": (1, SEQ, D), "y_s": (NB, 1, D), "ssm_p": (1, 1, HEADS, HD, NST), "ssd_p": (1, 1, SW - 1, XBC),
         "conf_p": (1, 1, CW - 1, D), "ssm_s": (1, NB, HEADS, HD, NST), "ssd_s": (1, NB, SW - 1, XBC),
         "conf_s": (1, NB, CW - 1, D)}


def kernel(**inputs):
    import numpy as _np
    import concourse.bacc as _bacc
    from concourse import mybir as _mybir
    from concourse.bass_utils import run_bass_kernel_spmd as _run

    nc = _bacc.Bacc("TRN2", target_bir_lowering=False, num_devices=1)
    arrays, ins, outs = {}, {}, {}
    for name in _INS:
        a = _np.ascontiguousarray(inputs[name])
        arrays[f"in_{name}"] = a
        ins[name] = nc.dram_tensor(f"in_{name}", a.shape, _mybir.dt.from_np(a.dtype), kind="ExternalInput").ap()
    for name, shape in _OUTS.items():
        outs[name] = nc.dram_tensor(f"out_{name}", shape, F32, kind="ExternalOutput").ap()
    build(nc, ins, outs)
    r = _run(nc, [arrays], core_ids=[0])
    return tuple(r.results[0][f"out_{name}"] for name in _OUTS)
```

```python
from contextlib import ExitStack

import concourse.bass as bass
from concourse import mybir
from concourse.alu_op_type import AluOpType as ALU

F32 = mybir.dt.float32
I32 = mybir.dt.int32
U32 = mybir.dt.uint32
ACT = mybir.ActivationFunctionType
AX = mybir.AxisListType.X

P = 128
D = 1024
KT = D // P
META, SEQ, NB = 16, 256, 8
TP = META + SEQ
T = TP + NB
TN = SEQ + NB
HEADS, HD, NST, GROUPS = 16, 64, 128, 2
HPG = HEADS // GROUPS
XBC = D + 2 * GROUPS * NST
XT_ = XBC // P
CW, SW = 31, 4
NE, TOPK = 32, 4
CAP = 128
HALF = 64
OVER = (TN * TOPK) // (CAP + 1)
EPS = 1e-5
LIMIT, ALPHA = 7.0, 1.702
FAR = 4096.0

COL_Z, COL_X, COL_DT, COL_VAL, COL_GATE = 0, D, D + XBC, D + XBC + HEADS, 2 * D + XBC + HEADS


def build(nc, I, O):
    ctx = ExitStack()
    with ctx:
        def sb(name, n, dt=F32):
            return ctx.enter_context(nc.sbuf_tensor(name, [P, n], dt))

        def sem(name):
            return ctx.enter_context(nc.semaphore(name))

        def view(t, off, *dims):
            n = 1
            for d in dims:
                n *= d
            a = t[:, off:off + n]
            if len(dims) == 1:
                return a
            names = "abc"[:len(dims)]
            return a.rearrange("p (" + " ".join(names) + ") -> p " + " ".join(names),
                               **dict(zip(names, dims)))

        def flat(ap):
            names = " ".join("abcd"[:len(ap.shape) - 1])
            return ap.rearrange(f"p {names} -> p ({names})")

        def bc(ap, axis, n):
            a = ap.unsqueeze(axis)
            s = list(a.shape)
            s[axis] = n
            return a.to_broadcast(s)

        PIECE = 2 * D
        NP = 12
        ring = sb("ring", NP * PIECE)
        extra = sb("extra", 4 * PIECE)
        acts = sb("acts", 3072 + 2240 + 2480 + 3136 + 3360 + 2112)
        small = sb("small", 3480)
        ps = ctx.enter_context(nc.psum_tensor("ps", [P, 8, 512], F32))

        o = 0
        x_tok = view(acts, o, 3, D); o += 3072
        uT = view(acts, o, KT, T); st_off = o; o += 2240
        cbuf = view(acts, o, KT, 30 + T); o += 2480
        xs_tok = view(acts, o, 3, D); conv = view(acts, o, KT, TN); xsig = view(acts, o, 6, T); cstage = view(acts, o + 2112, D); o += 3136
        xa = view(acts, o, XT_, T); hist_x = view(acts, o, XBC); xn = view(acts, o, 3, D); o += 3360
        zT = view(acts, o, KT, TN); hist_c = view(acts, o, 2, D); accT = zT; o += 2112
        csq = view(acts, 3072 + 2240, KT, TN)
        state_in = view(acts, st_off, 2, KT, P)
        t0 = 8 * PIECE
        csmp = view(ring, t0, KT, NB, CW)
        yT = view(ring, 6 * PIECE, KT, TN)
        sprod = view(ring, 6 * PIECE + 2112, KT, P)
        xsmp = view(ring, t0 + 1984, XT_, NB, SW)
        xraw = view(ring, t0 + 2368, XT_, 3 + T)
        xstage = view(ring, t0 + 5764, XBC)
        s0 = t0 + 2368
        Mh = view(ring, s0, HPG, P)
        Ce = view(ring, s0 + 1024, HPG, P)
        ysq = view(ring, s0, KT, TN)
        zsig = view(ring, s0, KT, TN)
        xdt = view(ring, s0 + 2112, HEADS, HD)
        xdec = view(ring, s0 + 3136, HEADS, HD)
        hT = view(ring, s0 + 4160, HEADS, HD)
        btok = view(ring, s0 + 5184, GROUPS, NST)
        cbm = view(ring, s0 + 5440, P)

        so = [0]

        def sm(*dims):
            n = 1
            for d in dims:
                n *= d
            v = view(small, so[0], *dims)
            so[0] += n
            return v

        ident, tri, tri_s, ones = sm(P), sm(P), sm(P), sm(P)
        r_ = t0 + 5764
        vrow = view(ring, r_, P)
        vcol = sm(108)
        cwrow, cwcol = view(ring, r_ + 128, 2, P), sm(CW, KT)
        
        
        wdt, wr = sm(KT, HEADS), sm(KT, NE)
        brt, dtb, aneg, dsk = sm(NE), sm(HEADS), sm(HEADS), sm(KT)
        dtt, dta, dtw, dte, dtd = sm(4, HEADS), sm(4, HEADS), sm(4, HEADS), sm(4, HEADS), sm(4, HEADS)
        acum = sm(2, HEADS)
        dec, cdec = sm(HEADS), sm(HEADS)
        sgt = sm(2, T)
        stat = sm(4, 4)
        sdt, sdec = sm(KT, NB), sm(KT, NB)
        ysum = sm(KT)
        mu = sm(TN)
        assert so[0] <= 3480, so[0]
        gmx, gxb, gsn, gcb = vcol[:, 0:8], vcol[:, 8:20], vcol[:, 20:28], vcol[:, 28:36]
        glg, glb, gff, gxw = vcol[:, 36:44], vcol[:, 44:52], vcol[:, 52:60], vcol[:, 60:108]
        rstd = sgt[:, 0, :][:, 0:TN]
        rstd2 = sgt[:, 1, :][:, 0:TN]

        ge, sig = view(extra, 0, D), view(extra, 1024, D)
        ue, hdn = view(extra, 2048, D), view(extra, 3072, D)
        xg, ys = view(extra, 4096, D), view(extra, 5120, D)
        xT, hT_e = view(extra, 6144, KT, CAP), view(extra, 7168, KT, CAP)
        bg_rows, bu_rows = view(acts, 0, D), view(acts, D, D)
        Sg = view(acts, 2 * D, 6, CAP)
        oh = view(acts, 2 * D + 768, P)
        S = view(acts, 9840, 3, CAP)
        m0 = 3072
        Pm = view(acts, m0, 2, TN)
        bdn = view(acts, m0 + 528, D)
        gT = view(acts, m0 + 1552, TN)
        iota_f, iota_h = view(acts, m0 + 1816, P), view(acts, m0 + 1944, P)
        c0 = 5312
        slotp, gates = view(acts, c0, 3, NE + 2), view(acts, c0 + 102, 3, NE + 2)
        logit, top8 = view(acts, c0 + 204, 3, NE), view(acts, c0 + 300, 3, 8)
        topf, topw = view(acts, c0 + 324, 3, TOPK), view(acts, c0 + 336, 3, TOPK)
        eq, mask = view(acts, c0 + 348, TOPK, NE), view(acts, c0 + 476, 3, NE)
        tmp96 = view(acts, c0 + 572, 3, NE)
        cntf, nbo, cum = view(acts, c0 + 668, NE), view(acts, c0 + 700, NE), view(acts, c0 + 732, NE)
        ole, oe, ob = view(acts, c0 + 764, OVER, NE), view(acts, c0 + 1020, OVER + 1), view(acts, c0 + 1029, OVER)
        oslot = view(acts, c0 + 1037, 3)
        topi = view(acts, c0 + 1040, 3, 8).bitcast(U32)
        otab = view(acts, c0 + 1064, OVER + 1).bitcast(I32)
        zero32 = view(acts, c0 + 1073, NE)
        cnti = view(acts, c0 + 1111, NE + 2).bitcast(I32)
        rsum, nmax = view(acts, c0 + 1105, 3), view(acts, c0 + 1108, 3)
        hout = view(acts, 0, 3, D)
        gfin = view(acts, 7792, D)
        hsq = view(acts, 7792 + 1024, D)

        names = ("zeroed consts x_loaded x_tail vec_loaded bias_loaded hist_loaded misc_loaded wdt_loaded "
                 "ssq_ready rms_ready xs_ready vt_done vcol_ready xtr_done uT_ready histx_loaded cw_tr htr_done hist_ready win_done "
                 "evac_done glu_done xpad_ready pad_ready dt_mm dt_ready dt_exp dt_v xst_tr xst_ready xst_out cst_tr "
                 "cst_ready kept_out conv_done mean_mm mu_ready cent_ready csq_ready var_mm var_ready std_ready "
                 "norm_ready csig_ready conf_ready xpre_ready xsig_ready xa_ready win_used z_sig acum_mm meta_exp "
                 "meta_v xtok_mm xdt_ready cb_mm cb_raw acb_mm d_ready e_ready ce_ready m_ready xdec_ready y_mm "
                 "st_mm y_ready hT_ready hT_tr hT_st hT_out sexp_mm sdec_ready st_in0 st_in1 sbc_mm sh_dec sh_bx "
                 "sh_new sh_prod sy_ready sh_out0 sh_out1 yg_ready ysq_ready yvar_mm yvar_ready ystd_ready "
                 "yn_ready wo_y_landed wo_conf_landed wo_used wo_mm acc_ready h_tr hsq_ready hr_v hstd_ready xn_ready lg_mm nm_ready topexp "
                 "gates_ready pos_mm cnt_ready gt_ready ht_done ht_ready xt_done xt_ready xg_out oh_ready "
                 "rows_zeroed rows_loaded late_loaded xg_done pt_done sc_done g_ready u_read hdn_ready y_back "
                 "p_ready acc_done s_ready sg_ready sig_ready piece_used o_tab f_ready f_out f_rd iota_ready").split()
        ev = {n: sem(n) for n in names}
        landed = [sem(f"piece_landed{i}") for i in range(NP)]
        win_landed = [sem(f"win_landed{i}") for i in range(6)]
        block = ctx.enter_context(nc.Block())

        CHUNKS = [(COL_X, "xbc", 0), (COL_X + 512, "xbc", 4), (COL_X + 1024, "xbc", 8),
                  (COL_VAL, "val", 0), (COL_GATE, "gate", 0), (COL_VAL + 512, "val", 4), (COL_GATE + 512, "gate", 4),
                  (COL_Z, "z", 0), (COL_Z + 512, "z", 4)]
        PLACE = [(ring, 0), (ring, 4096), (ring, 8192), (ring, 12288), (extra, 0), (extra, 4096),
                 (ring, 0), (ring, 4096), (ring, 8192)]
        NC_ = len(CHUNKS)
        X_TILES, TILES = XT_, 4 * NC_
        UNIT_TILES, UNIT_END = (18, 22, 26, 30), (21, 25, 29, 33)
        TAPS = ((0, 0, 0, 4), (4, 5, 11, 15), (15, 16, 22, 27), (27, 28, 34, 38))
        DEC_TAPS = (38, 41, 44, 47, 50, 53, 56, 59, 2 * CW)
        GATE_TILES = {j: n for n, j in enumerate([j for j in range(TILES) if CHUNKS[j // 4][1] == "gate"])}

        def tile_bank(j):
            return j % 4 if j < X_TILES else 3 * (j % 2)

        def win(c):
            return view(PLACE[c][0], PLACE[c][1], KT, 512)

        def wout(p):
            return view(extra if p < 4 else ring, (p % 4) * PIECE, 2, D)

        def piece(p):
            return view(ring, p * PIECE, 2, D)

        w_in, w_out = I["w_in"][0], I["w_out"][0]
        expert_w = [I[n] for n in ("w_gate", "w_up", "w_down")]

        def expert_piece(e, p):
            w = expert_w[p // 4]
            r = (p % 4) * 2 * P
            return w[0, bass.ds(e, 1), r:r + 2 * P, :].rearrange("o (k p) n -> p (o k) n", p=P)

        tok = [(0, P), (P, P), (2 * P, NB)]

        @block.sync
        def _(sp):
            xp, xs, mt = I["x_prompt"][0], I["x_sample"], I["meta_tokens"]
            sp.dma_start(x_tok[:, 0, :], xp[0:P]).then_inc(ev["x_loaded"], 16)
            sp.wait_ge(ev["zeroed"], 1)
            sp.dma_start(x_tok[0:NB, 2, :], xs.rearrange("b o d -> (b o) d")).then_inc(ev["x_tail"], 16)
            sp.dma_start(x_tok[32:32 + META, 2, :], mt).then_inc(ev["x_tail"], 16)
            sp.dma_start(wdt, w_in[:, COL_DT:COL_DT + HEADS].rearrange("(k p) n -> p k n", p=P)).then_inc(ev["wdt_loaded"], 16)
            sp.wait_ge(ev["vec_loaded"], 16 * 8)
            for c in range(NC_):
                if c == 2:
                    hc = I["state_conf_conv"][0].rearrange("b k d -> (b k) d")
                    sp.dma_start(hist_x[0:24, :], I["state_ssd_conv"][0].rearrange("b k d -> (b k) d")
                                 ).then_inc(ev["histx_loaded"], 16)
                    for j in range(2):
                        sp.dma_start(hist_c[0:120, j, :], hc[120 * j:120 * (j + 1)]).then_inc(ev["hist_loaded"], 16)
                if c >= 6:
                    sp.wait_ge(ev["win_used"], c - 5)
                sp.dma_start(win(c), w_in[:, CHUNKS[c][0]:CHUNKS[c][0] + 512].rearrange("(k p) n -> p k n", p=P)
                             ).then_inc(win_landed[c % 6], 16)

            def load_wout(p, landed_):
                sp.dma_start(wout(p), w_out[2 * p * P:2 * (p + 1) * P].rearrange("(k p) n -> p k n", p=P)
                             ).then_inc(landed_, 16)

            def prefetch(p):
                sp.dma_start(piece(p), expert_piece(0, p)).then_inc(landed[p], 16)

            sp.wait_ge(ev["win_used"], 6)
            for p in range(4):
                load_wout(p, ev["wo_y_landed"])
            sp.wait_ge(ev["win_used"], NC_)
            for b in range(2):
                sp.dma_start(state_in[:, b], I["state_ssm"][0, b].rearrange("h p n -> (h p) n").rearrange(
                    "(m q) n -> q m n", q=P)).then_inc((ev["st_in0"], ev["st_in1"])[b], 16)
            for p in range(4, 8):
                load_wout(p, ev["wo_conf_landed"])
            for p in range(4, 6):
                prefetch(p)
            sp.wait_ge(ev["hT_st"], 1)
            sp.dma_start(O["ssm_p"][0, 0].rearrange("h p n -> (h p) n").rearrange("(m q) n -> q m n", q=P),
                         view(ring, s0 + 3136, KT, P)).then_inc(ev["hT_out"], 16)
            for b in range(NB):
                sp.wait_ge(ev["sh_new"], b + 1)
                sp.dma_start(O["ssm_s"][0, b].rearrange("h p n -> (h p) n").rearrange("(m q) n -> q m n", q=P),
                             state_in[:, b % 2]).then_inc((ev["sh_out0"], ev["sh_out1"])[b % 2], 16)
                if b + 2 < NB:
                    sp.wait_ge((ev["sh_out0"], ev["sh_out1"])[b % 2], 16 * (b // 2 + 1))
                    sp.wait_ge(ev["sh_prod"], b + 1)
                    sp.dma_start(state_in[:, b % 2], I["state_ssm"][0, b + 2].rearrange("h p n -> (h p) n").rearrange(
                        "(m q) n -> q m n", q=P)).then_inc((ev["st_in0"], ev["st_in1"])[b % 2], 16)
            sp.wait_ge(ev["sh_out0"], 16 * (NB // 2))
            sp.wait_ge(ev["sh_out1"], 16 * (NB // 2))
            sp.wait_ge(ev["sy_ready"], 1)
            sp.wait_ge(ev["hT_out"], 16)
            sp.dma_start(bdn[0:NE, :], I["b_down"][0]).then_inc(ev["late_loaded"], 16)
            sp.wait_ge(ev["yvar_mm"], 1)
            sp.wait_ge(ev["conv_done"], 1)
            for p in range(8, NP):
                prefetch(p)
            sp.wait_ge(ev["wo_used"], 1)
            prefetch(6)
            prefetch(7)
            sp.wait_ge(ev["wo_used"], 2)
            for p in range(4):
                prefetch(p)

            sp.wait_ge(ev["rows_zeroed"], 1)
            sp.dma_start(gfin, I["g_final"].partition_broadcast(P)).then_inc(ev["late_loaded"], 16)
            sp.dma_start(bg_rows[0:NE, :], I["b_gate"][0]).then_inc(ev["rows_loaded"], 16)
            sp.dma_start(bu_rows[0:NE, :], I["b_up"][0]).then_inc(ev["rows_loaded"], 16)

            with sp.Fori(0, NE - 1) as i:
                for p in range(NP):
                    sp.wait_ge(ev["piece_used"], i * NP + p + 1)
                    sp.dma_start(piece(p), expert_piece(i + 1, p)).then_inc(landed[p], 16)
            sp.wait_ge(ev["o_tab"], 1)
            n_over = sp.value_load(otab[0:1, OVER:OVER + 1], min_val=0, max_val=OVER)
            with sp.Fori(0, OVER) as j:
                with sp.If(j < n_over):
                    e = sp.value_load(otab[0:1, bass.ds(j, 1)], min_val=0, max_val=NE - 1)
                    sp.wait_ge(ev["piece_used"], j * NP + NE * NP)
                    for p in range(NP):
                        sp.dma_start(piece(p), expert_piece(e, p)).then_inc(landed[p], 16)
            sp.wait_ge(ev["f_ready"], 3)
            sp.dma_start(O["y_p"][0, 0:P], hout[:, 0, :]).then_inc(ev["f_out"], 16)
            sp.dma_start(O["y_p"][0, P:2 * P], hout[:, 1, :]).then_inc(ev["f_out"], 16)
            sp.dma_start(O["y_s"].rearrange("b o d -> (b o) d"), hout[0:NB, 2, :]).then_inc(ev["f_out"], 16)
            sp.wait_ge(ev["f_out"], 48)
            sp.wait_ge(ev["hT_out"], 16)
            sp.wait_ge(ev["kept_out"], 64)
            sp.wait_ge(ev["xst_out"], 32)

        @block.gpsimd
        def _(g):
            nc.gpsimd.memset(x_tok[0:48, 2, :], 0.0)
            nc.gpsimd.memset(stat, 1.0).then_inc(ev["zeroed"], 1)
            for t, base, op in ((ident, 0, ALU.not_equal), (tri, 0, ALU.is_gt), (tri_s, 0, ALU.is_ge)):
                nc.gpsimd.memset(t, 0.0)
            nc.gpsimd.memset(ones, 1.0)
            g.drain()
            for t, op in ((ident, ALU.not_equal), (tri, ALU.is_gt), (tri_s, ALU.is_ge)):
                nc.gpsimd.affine_select(out=t, in_=t, compare_op=op, fill=1.0, base=0, pattern=[[-1, P]],
                                        channel_multiplier=1)
            g.drain()
            nc.gpsimd.memset(cbuf[:, :, 0:30], 0.0)
            nc.gpsimd.memset(xraw[:, :, 0:3], 0.0).then_inc(ev["consts"], 1)
            g.wait_ge(ev["evac_done"], X_TILES)
            nc.gpsimd.tensor_copy(xsmp[:, :, :, 3], xraw[:, :, 3 + TP:3 + T]).then_inc(ev["xpad_ready"], 1)

            def glu(first, last):
                for j in range(first, last):
                    if j in GATE_TILES:
                        n = GATE_TILES[j]
                        g.wait_ge(ev["evac_done"], j + 1)
                        v = cbuf[:, n, 30:30 + T]
                        nc.gpsimd.tensor_tensor(v, v, sgt[:, n % 2, :], ALU.mult).then_inc(ev["glu_done"], 1)

            glu(0, UNIT_TILES[0])
            for u in range(4):
                c, gr = u // 2, u % 2
                g.wait_ge(ev["cb_raw"], u + 1)
                nc.gpsimd.affine_select(out=cbm, in_=cbm, compare_op=ALU.is_ge, fill=0.0, base=0,
                                        pattern=[[1, P]], channel_multiplier=-1)
                g.drain()
                g.wait_ge(ev["xdec_ready"], u + 1)
                nc.gpsimd.tensor_tensor(Mh, Mh, bc(cbm, 1, HPG), ALU.mult)
                nc.gpsimd.tensor_tensor(Ce, Ce, bc(xa[:, 10 + gr, 16 + c * P:16 + (c + 1) * P], 1, HPG),
                                        ALU.mult).then_inc(ev["m_ready"], 1)
                g.drain()
                glu(UNIT_TILES[u], UNIT_TILES[u + 1] if u < 3 else TILES)
            g.drain()
            nc.gpsimd.tensor_copy(csmp[:, :, :, 30], cbuf[:, :, 30 + TP:30 + T]).then_inc(ev["pad_ready"], 1)
            for b in range(NB):
                g.wait_ge(ev["sh_dec"], b + 1)
                g.wait_ge(ev["sh_bx"], b + 1)
                nc.gpsimd.tensor_tensor(state_in[:, b % 2], state_in[:, b % 2], sprod, ALU.add).then_inc(ev["sh_new"], 1)
            g.wait_ge(ev["late_loaded"], 16)
            nc.gpsimd.iota(iota_f, [[1, P]], base=0, channel_multiplier=0,
                           allow_small_or_imprecise_dtypes=True)
            nc.gpsimd.iota(iota_h, [[1, P]], base=-HALF, channel_multiplier=0,
                           allow_small_or_imprecise_dtypes=True).then_inc(ev["iota_ready"], 1)
            g.wait_ge(ev["wo_mm"], 1)
            nc.gpsimd.memset(view(acts, 0, 2 * D), 0.0)
            nc.gpsimd.memset(oh, 0.0).then_inc(ev["rows_zeroed"], 1)

        @block.scalar
        def _(a):
            act = nc.scalar.activation
            a.dma_start(x_tok[:, 1, :], I["x_prompt"][0, P:2 * P]).then_inc(ev["x_loaded"], 16)
            rows = lambda name, n: I[name][0].rearrange("(k c) -> k c", c=P)[0:n]
            for r0, ap, n in ((0, rows("g_mix", 8), 8), (8, rows("conv_ssd_b", 12), 12), (20, rows("g_ssd_norm", 8), 8),
                              (28, rows("conv_conf_b", 8), 8), (36, rows("ln_conf_g", 8), 8),
                              (44, rows("ln_conf_b", 8), 8), (52, rows("g_ffn", 8), 8),
                              (60, I["conv_ssd_w"][0].rearrange("k (m c) -> (k m) c", c=P), 48)):
                a.dma_start(vrow[r0:r0 + n, :], ap).then_inc(ev["vec_loaded"], 16)
            cw = I["conv_conf_w"][0].rearrange("k (m c) -> (k m) c", c=P)
            for j in range(2):
                a.dma_start(cwrow[0:124, j, :], cw[124 * j:124 * (j + 1)]).then_inc(ev["bias_loaded"], 16)
            a.dma_start(dtb, I["dt_bias"][0].partition_broadcast(P)).then_inc(ev["misc_loaded"], 16)
            a.dma_start(aneg, I["a_log"][0].partition_broadcast(P)).then_inc(ev["misc_loaded"], 16)
            a.dma_start(brt, I["b_router"][0].partition_broadcast(P)).then_inc(ev["misc_loaded"], 16)
            a.dma_start(wr, I["w_router"][0].rearrange("(k p) n -> p k n", p=P)).then_inc(ev["misc_loaded"], 16)
            dsv = I["d_skip"][0].rearrange("(m j) -> j m", j=2)
            for j in range(2):
                with nc.allow_non_contiguous_dma("sixteen scalars"):
                    a.dma_start(dsk[64 * j:64 * j + 64, :], dsv[j].partition_broadcast(64)).then_inc(ev["misc_loaded"], 16)

            a.wait_ge(ev["x_loaded"], 32)
            a.wait_ge(ev["zeroed"], 1)
            a.wait_ge(ev["x_tail"], 32)
            act(xs_tok[:, 0, :], x_tok[:, 0, :], ACT.Square, accum_out=stat[:, 0, 0:1])
            act(xs_tok[:, 1, :], x_tok[:, 1, :], ACT.Square, accum_out=stat[:, 0, 1:2])
            act(xs_tok[0:48, 2, :], x_tok[0:48, 2, :], ACT.Square, accum_out=stat[0:48, 0, 2:3])
            a.drain()
            act(stat[:, 3, 0:3], stat[:, 0, 0:3], ACT.Copy).then_inc(ev["ssq_ready"], 1)
            a.wait_ge(ev["rms_ready"], 1)
            act(stat[:, 2, 0:3], stat[:, 1, 0:3], ACT.Sqrt).then_inc(ev["std_ready"], 1)
            a.wait_ge(ev["rms_ready"], 2)
            act(xs_tok[:, 0, :], x_tok[:, 0, :], ACT.Copy, scale=stat[:, 1, 0:1]).then_inc(ev["xs_ready"], 1)
            act(xs_tok[:, 1, :], x_tok[:, 1, :], ACT.Copy, scale=stat[:, 1, 1:2]).then_inc(ev["xs_ready"], 1)
            act(xs_tok[0:48, 2, :], x_tok[0:48, 2, :], ACT.Copy, scale=stat[0:48, 1, 2:3]).then_inc(ev["xs_ready"], 1)
            a.dma_start(O["conf_s"][0, :, 0:CW - 2, :], I["state_conf_conv"][0, :, 1:CW - 1, :]).then_inc(ev["kept_out"], 16)
            a.dma_start(O["ssd_s"][0, :, 0:SW - 2, :], I["state_ssd_conv"][0, :, 1:SW - 1, :]).then_inc(ev["kept_out"], 16)

            def tiles_out(first, last):
                for j in range(first, last):
                    _, kind, m0_ = CHUNKS[j // 4]
                    mm = m0_ + j % 4
                    a.wait_ge(ev["win_done"], j + 1)
                    src = ps[:, tile_bank(j), 0:T]
                    if kind == "val":
                        h = act(cbuf[:, mm, 30:30 + T], src, ACT.Copy)
                    elif kind == "gate":
                        n = GATE_TILES[j]
                        if n >= 2:
                            a.wait_ge(ev["glu_done"], n - 1)
                        h = act(sgt[:, n % 2, :], src, ACT.Sigmoid)
                    elif kind == "xbc":
                        h = act(xraw[:, mm, 3:3 + T], src, ACT.Copy)
                    else:
                        h = act(zT[:, mm, :], src[:, 0:TN], ACT.Copy)
                    h.then_inc(ev["evac_done"], 1)

            tiles_out(0, 4)
            a.wait_ge(ev["htr_done"], 1)
            act(xsmp[:, :, :, 0:3], ps[:, 6, 0:288].rearrange("p (m b k) -> p m b k", m=12, b=8), ACT.Copy
                ).then_inc(ev["hist_ready"], 1)
            a.wait_ge(ev["dt_v"], 1)
            act(dte, dta, ACT.Exp, scale=-1.0).then_inc(ev["dt_exp"], 1)
            a.wait_ge(ev["dt_v"], 2)
            act(dta, dtw, ACT.Ln).then_inc(ev["dt_exp"], 1)
            a.wait_ge(ev["misc_loaded"], 96)
            act(aneg, aneg, ACT.Exp).then_inc(ev["dt_exp"], 1)

            tiles_out(4, 8)
            for k in range(4):
                j, h_ = k // 2, k % 2
                a.wait_ge(ev["htr_done"], k + 2)
                act(csmp[:, 4 * h_:4 * h_ + 4, 4 * j:4 * j + 4, 0:30],
                    ps[:, 4 + k, 0:480].rearrange("p (m b k) -> p m b k", m=4, b=4), ACT.Copy).then_inc(ev["hist_ready"], 1)
            tiles_out(8, X_TILES)
            a.wait_ge(ev["xst_tr"], 1)
            act(xstage[0:11, :], ps[0:11, 5:8, :].rearrange("p a b -> p (a b)"), ACT.Copy).then_inc(ev["xst_ready"], 1)
            a.wait_ge(ev["xst_ready"], 1)
            a.dma_start(O["ssd_p"][0, 0], xstage[0:SW - 1, :]).then_inc(ev["xst_out"], 16)
            a.dma_start(O["ssd_s"][0, :, SW - 2, :], xstage[SW - 1:SW - 1 + NB, :]).then_inc(ev["xst_out"], 16)
            tiles_out(X_TILES, X_TILES + 2)

            for h in range(2):
                a.wait_ge(ev["xpre_ready"], 1)
                if h:
                    tiles_out(X_TILES + 2, X_TILES + 3)
                    a.wait_ge(ev["xa_ready"], 1)
                act(flat(xsig), flat(xa[:, 6 * h:6 * h + 6, :]), ACT.Sigmoid).then_inc(ev["xsig_ready"], 1)
            tiles_out(X_TILES + 3, X_TILES + 5)

            a.wait_ge(ev["meta_v"], 1)
            act(dec[0:META, :], dec[0:META, :], ACT.Exp).then_inc(ev["meta_exp"], 1)
            tiles_out(X_TILES + 5, UNIT_TILES[0])
            for u in range(4):
                a.wait_ge(ev["d_ready"], u + 1)
                act(flat(Mh), flat(Mh), ACT.Exp).then_inc(ev["e_ready"], 1)
                if u:
                    a.wait_ge(ev["y_mm"], u)
                act(flat(Ce), ps[:, 4:6, :].rearrange("p a b -> p (a b)"), ACT.Exp).then_inc(ev["ce_ready"], 1)
                tiles_out(UNIT_TILES[u], UNIT_TILES[u + 1] if u < 3 else TILES)
            a.wait_ge(ev["cst_tr"], 1)
            act(cstage[0:38, :], ps[0:38, 6:8, :].rearrange("p a b -> p (a b)"), ACT.Copy).then_inc(ev["cst_ready"], 1)
            a.wait_ge(ev["cst_ready"], 1)
            a.dma_start(O["conf_p"][0, 0], cstage[0:CW - 1, :]).then_inc(ev["kept_out"], 16)
            a.dma_start(O["conf_s"][0, :, CW - 2, :], cstage[CW - 1:CW - 1 + NB, :]).then_inc(ev["kept_out"], 16)
            a.wait_ge(ev["sexp_mm"], 1)
            act(flat(sdec), ps[:, 2, 0:64], ACT.Exp).then_inc(ev["sdec_ready"], 1)
            for b in range(NB):
                a.wait_ge((ev["st_in0"], ev["st_in1"])[b % 2], 16 * (b // 2 + 1))
                if b == 0:
                    a.wait_ge(ev["sdec_ready"], 1)
                for m in range(KT):
                    h = act(state_in[:, b % 2, m, :], state_in[:, b % 2, m, :], ACT.Copy, scale=sdec[:, m, b:b + 1])
                h.then_inc(ev["sh_dec"], 1)
            a.wait_ge(ev["y_mm"], 4)
            a.wait_ge(ev["m_ready"], 4)
            act(flat(zsig), flat(zT), ACT.Sigmoid).then_inc(ev["z_sig"], 1)
            a.wait_ge(ev["yg_ready"], 1)
            act(flat(ysq), flat(yT), ACT.Square).then_inc(ev["ysq_ready"], 1)
            a.wait_ge(ev["yvar_ready"], 1)
            act(rstd, rstd, ACT.Sqrt)
            act(rstd2, rstd2, ACT.Sqrt).then_inc(ev["ystd_ready"], 1)
            a.wait_ge(ev["mean_mm"], 1)
            act(mu, ps[:, 6, 0:TN], ACT.Copy, scale=1.0 / D).then_inc(ev["mu_ready"], 1)
            a.wait_ge(ev["cent_ready"], 1)
            act(flat(csq), flat(conv), ACT.Square).then_inc(ev["csq_ready"], 1)
            a.wait_ge(ev["var_ready"], 1)
            act(rstd2, rstd, ACT.Sqrt).then_inc(ev["std_ready"], 1)
            a.wait_ge(ev["norm_ready"], 1)
            a.wait_ge(ev["var_mm"], 1)
            for m in range(KT):
                act(csq[:, m, :], conv[:, m, :], ACT.Sigmoid, scale=glg[:, m:m + 1], bias=glb[:, m:m + 1]
                    ).then_inc(ev["csig_ready"], 1)

            for j, (c, r) in enumerate(tok):
                a.wait_ge(ev["h_tr"], j + 1)
                act(hsq[0:r, :], ps[0:r, 2 * j:2 * j + 2, :].rearrange("p a b -> p (a b)"), ACT.Square,
                    accum_out=stat[0:r, 0, j:j + 1])
                a.drain()
            act(stat[:, 3, 0:3], stat[:, 0, 0:3], ACT.Copy).then_inc(ev["hsq_ready"], 1)
            a.wait_ge(ev["hr_v"], 1)
            act(stat[:, 2, 0:3], stat[:, 1, 0:3], ACT.Sqrt).then_inc(ev["hstd_ready"], 1)
            a.wait_ge(ev["hr_v"], 2)
            for j, (c, r) in enumerate(tok):
                act(xn[0:r, j, :], ps[0:r, 2 * j:2 * j + 2, :].rearrange("p a b -> p (a b)"), ACT.Copy,
                    scale=stat[0:r, 1, j:j + 1]).then_inc(ev["xn_ready"], 1)
            a.wait_ge(ev["nm_ready"], 1)
            for j, (c, r) in enumerate(tok):
                act(topw[0:r, j, :], top8[0:r, j, 0:TOPK], ACT.Exp, bias=nmax[0:r, j:j + 1],
                    accum_out=rsum[0:r, j:j + 1])
                a.drain()
            act(stat[:, 3, 0:3], stat[:, 0, 0:3], ACT.Copy).then_inc(ev["topexp"], 1)

            def back(dst, bank):
                return act(dst, ps[:, bank:bank + 2, :].rearrange("p a b -> p (a b)"), ACT.Copy)

            def inputs_out(i):
                a.wait_ge(ev["xg_done"], i + 2)
                back(xg, 4).then_inc(ev["xg_out"], 1)

            def places_out(i):
                a.wait_ge(ev["pt_done"], i + 2)
                act(Pm, ps[:, 6:8, 0:TN], ACT.Copy).then_inc(ev["p_ready"], 1)

            def sigmoid(i):
                a.wait_ge(ev["g_ready"], i + 1)
                act(sig, ge, ACT.Sigmoid, scale=ALPHA).then_inc(ev["sig_ready"], 1)

            def hidden_out(i):
                a.wait_ge(ev["ht_done"], i + 1)
                back(flat(hT_e), 0).then_inc(ev["ht_ready"], 1)

            def output_out(i):
                a.wait_ge(ev["piece_used"], i * NP + NP)
                back(ys, 4).then_inc(ev["y_back"], 1)

            inputs_out(-1)
            with a.Fori(0, NE) as i:
                sigmoid(i)
                inputs_out(i)
                places_out(i)
                hidden_out(i)
                output_out(i)
            places_out(NE)

            a.wait_ge(ev["o_tab"], 1)
            n_over = a.value_load(otab[0:1, OVER:OVER + 1], min_val=0, max_val=OVER)
            with a.Fori(0, OVER) as j:
                with a.If(j < n_over):
                    inputs_out(j + NE)
                    sigmoid(j + NE)
                    hidden_out(j + NE)
                    output_out(j + NE)
                    places_out(j + NE + 1)

            for j, (c, r) in enumerate(tok):
                a.wait_ge(ev["h_tr"], j + 4)
                act(hsq[0:r, :], ps[0:r, 2 * j:2 * j + 2, :].rearrange("p a b -> p (a b)"), ACT.Square,
                    accum_out=stat[0:r, 0, j:j + 1])
                a.drain()
            act(stat[:, 3, 0:3], stat[:, 0, 0:3], ACT.Copy).then_inc(ev["hsq_ready"], 1)
            a.wait_ge(ev["hr_v"], 3)
            act(stat[:, 2, 0:3], stat[:, 1, 0:3], ACT.Sqrt).then_inc(ev["hstd_ready"], 1)

        @block.vector
        def _(v):
            V = nc.vector
            TT, TS, STT = V.tensor_tensor, V.tensor_scalar, V.scalar_tensor_tensor

            V.memset(dtt, 0.0)
            v.wait_ge(ev["ssq_ready"], 1)
            TS(stat[:, 1, 0:3], stat[:, 0, 0:3], 1.0 / D, EPS, ALU.mult, ALU.add).then_inc(ev["rms_ready"], 1)
            v.wait_ge(ev["vt_done"], 1)
            V.tensor_copy(vcol, ps[:, 0, 0:108]).then_inc(ev["vcol_ready"], 1)
            v.wait_ge(ev["std_ready"], 1)
            V.reciprocal(stat[:, 1, 0:3], stat[:, 2, 0:3]).then_inc(ev["rms_ready"], 1)
            v.drain()
            for k in range(4):
                j, h = k // 2, k % 2
                v.wait_ge(ev["xtr_done"], k + 1)
                TT(uT[:, 4 * h:4 * h + 4, META + P * j:META + P * (j + 1)], ps[:, 4 + k, :].rearrange("p (m t) -> p m t", m=4),
                   bc(gmx[:, 4 * h:4 * h + 4], 2, P), ALU.mult).then_inc(ev["uT_ready"], 1)
            v.wait_ge(ev["xtr_done"], 5)
            tail = ps[:, 4, 0:384].rearrange("p (m t) -> p m t", m=8)
            TT(uT[:, :, TP:T], tail[:, :, 0:NB], bc(gmx, 2, NB), ALU.mult).then_inc(ev["uT_ready"], 1)
            TT(uT[:, :, 0:META], tail[:, :, 32:48], bc(gmx, 2, META), ALU.mult).then_inc(ev["uT_ready"], 1)

            xw = gxw.rearrange("p (k m) -> p k m", k=SW)
            v.wait_ge(ev["consts"], 1)

            def narrow_conv(m3):
                v.wait_ge(ev["evac_done"], m3 + 4)
                for k in range(SW):
                    for m in range(m3, m3 + 4):
                        src = xraw[:, m, k:k + TP]
                        if k == 0:
                            TS(xa[:, m, 0:TP], src, xw[:, k, m:m + 1], gxb[:, m:m + 1], ALU.mult, ALU.add)
                        else:
                            STT(xa[:, m, 0:TP], src, xw[:, k, m:m + 1], xa[:, m, 0:TP], ALU.mult, ALU.add)
                    v.drain()

            v.wait_ge(ev["dt_mm"], 1)
            v.drain()
            dp = ps[:, 5, 0:64].rearrange("p (g h) -> p g h", g=4)
            for g_, r in ((0, P), (1, P), (2, NB), (3, META)):
                V.tensor_copy(dtt[0:r, g_, :], dp[0:r, g_, :])
            v.wait_ge(ev["misc_loaded"], 96)
            v.drain()
            TT(dtt, dtt, bc(dtb, 1, 4), ALU.add)
            v.drain()
            TS(dtd, dtt, -1.0, None, ALU.mult)
            v.drain()
            TT(dta, dtt, dtd, ALU.max)
            v.drain()
            TS(dtd, dtt, 0.0, None, ALU.max).then_inc(ev["dt_v"], 1)
            v.wait_ge(ev["dt_exp"], 1)
            TS(dtw, dte, 1.0, None, ALU.add).then_inc(ev["dt_v"], 1)
            v.wait_ge(ev["dt_exp"], 2)
            v.drain()
            TS(dtw, dtw, -1.0, None, ALU.add)
            v.drain()
            TS(dtt, dtw, 0.0, None, ALU.is_equal)
            v.drain()
            TT(dtw, dtw, dtt, ALU.add)
            TT(dtt, dtt, dte, ALU.mult)
            v.drain()
            V.reciprocal(dtw, dtw)
            TT(dta, dta, dte, ALU.mult)
            TT(dtt, dtt, dtd, ALU.add)
            v.drain()
            TT(dta, dta, dtw, ALU.mult)
            v.drain()
            TT(dtt, dtt, dta, ALU.add)
            v.wait_ge(ev["dt_exp"], 3)
            v.drain()
            STT(dta, dtt, -1.0, bc(aneg, 1, 4), ALU.mult, ALU.mult)
            v.drain()
            TT(wr, wr, bc(gff, 2, NE), ALU.mult).then_inc(ev["dt_ready"], 1)

            v.wait_ge(ev["cw_tr"], 1)
            V.tensor_copy(flat(cwcol), ps[:, 7, 0:248]).then_inc(ev["vcol_ready"], 1)
            v.wait_ge(ev["hist_ready"], 1)
            for m3 in range(0, XT_, 4):
                narrow_conv(m3)
            v.wait_ge(ev["xpad_ready"], 1)
            TT(xsmp, xsmp, bc(xw.rearrange("p k m -> p m k"), 2, NB), ALU.mult)
            v.drain()
            V.tensor_reduce(xa[:, :, TP:T], xsmp, AX, ALU.add)
            v.drain()
            TT(xa[:, :, TP:T], xa[:, :, TP:T], bc(gxb, 2, NB), ALU.add).then_inc(ev["xpre_ready"], 1)
            for h in range(2):
                v.wait_ge(ev["xsig_ready"], h + 1)
                TT(flat(xa[:, 6 * h:6 * h + 6, :]), flat(xa[:, 6 * h:6 * h + 6, :]), flat(xsig), ALU.mult
                   ).then_inc(ev["xa_ready"], 1)

            def wide_conv(first, last):
                for q in range(first, last):
                    h, k = q // CW, q % CW
                    if k == 0:
                        v.wait_ge(ev["glu_done"], 4 * h + 4)
                    for m in range(4 * h, 4 * h + 4):
                        src = cbuf[:, m, META + k:META + k + SEQ]
                        w = cwcol[:, k, m:m + 1]
                        if k == 0:
                            TS(conv[:, m, 0:SEQ], src, w, gcb[:, m:m + 1], ALU.mult, ALU.add)
                        else:
                            STT(conv[:, m, 0:SEQ], src, w, conv[:, m, 0:SEQ], ALU.mult, ALU.add)
                    v.drain()

            v.wait_ge(ev["acum_mm"], 1)
            am = ps[:, 6, 0:64].rearrange("p (g h) -> p g h", g=4)
            V.tensor_copy(acum, am[:, 0:2, :])
            V.tensor_copy(dec[0:META, :], am[0:META, 2, :])
            v.drain()
            TT(dec[0:META, :], am[0:META, 3, :], dec[0:META, :], ALU.subtract).then_inc(ev["meta_v"], 1)

            def rows_of_chunk(n, r, g_):
                v.wait_ge(ev["xtok_mm"], n + 1)
                for h in range(2):
                    TT(xdt[0:r, 8 * h:8 * h + 8, :], ps[0:r, 1 + h, :].rearrange("p (h d) -> p h d", h=HPG),
                       bc(dtt[0:r, g_, 8 * h:8 * h + 8], 2, HD), ALU.mult)
                V.tensor_copy(flat(btok[0:r]), ps[0:r, 7, 0:256]).then_inc(ev["xdt_ready"], 1)

            v.wait_ge(ev["xst_out"], 32)
            rows_of_chunk(0, META, 3)
            v.wait_ge(ev["meta_exp"], 1)
            v.drain()
            TT(xdec[0:META], xdt[0:META], bc(dec[0:META, :], 2, HD), ALU.mult).then_inc(ev["hT_ready"], 1)
            for g_ in range(GROUPS):
                v.wait_ge(ev["st_mm"], g_ + 1)
                V.tensor_copy(hT[:, 8 * g_:8 * g_ + 8, :], ps[:, 7, :].rearrange("p (h d) -> p h d", h=HPG)
                              ).then_inc(ev["hT_ready"], 1)
            for c in range(2):
                if c:
                    v.wait_ge(ev["st_mm"], 6 - 2)
                rows_of_chunk(1 + c, P, c)
                for g_ in range(GROUPS):
                    u = 2 * c + g_
                    v.wait_ge(ev["cb_mm"], u + 1)
                    if u:
                        v.wait_ge(ev["m_ready"], u)
                    V.tensor_copy(cbm, ps[:, 7, 384:512]).then_inc(ev["cb_raw"], 1)
                    v.wait_ge(ev["acb_mm"], u + 1)
                    if u:
                        v.wait_ge(ev["y_mm"], u)
                    for h in range(2):
                        TT(Mh[:, 4 * h:4 * h + 4, :], ps[:, 4 + h, :].rearrange("p (h d) -> p h d", h=4),
                           bc(acum[:, c, 8 * g_ + 4 * h:8 * g_ + 4 * h + 4], 2, P), ALU.subtract)
                    v.drain()
                    TS(flat(Mh), flat(Mh), 0.0, None, ALU.min).then_inc(ev["d_ready"], 1)
                    wide_conv(TAPS[u][0], TAPS[u][1])
                    v.wait_ge(ev["e_ready"], u + 1)
                    V.tensor_copy(dec[:, 0:8], Mh[:, :, P - 1])
                    v.wait_ge(ev["ce_ready"], u + 1)
                    V.tensor_copy(cdec[:, 0:8], Ce[:, :, P - 1])
                    v.drain()
                    TT(xdec[:, 8 * g_:8 * g_ + 8, :], xdt[:, 8 * g_:8 * g_ + 8, :], bc(dec[:, 0:8], 2, HD), ALU.mult
                       ).then_inc(ev["xdec_ready"], 1)
                    wide_conv(TAPS[u][1], TAPS[u][2])
                    v.wait_ge(ev["y_mm"], u + 1)
                    for k in range(4):
                        m = 4 * g_ + k
                        h = STT(yT[:, m, c * P:(c + 1) * P], xa[:, m, META + c * P:META + (c + 1) * P], dsk[:, m:m + 1],
                                ps[:, 6, k * P:(k + 1) * P], ALU.mult, ALU.add)
                    h.then_inc(ev["y_ready"], 1)
                    TT(hT[:, 8 * g_:8 * g_ + 8, :], hT[:, 8 * g_:8 * g_ + 8, :], bc(cdec[:, 0:8], 2, HD), ALU.mult)
                    v.drain()
                    v.wait_ge(ev["st_mm"], 3 + u)
                    TT(hT[:, 8 * g_:8 * g_ + 8, :], hT[:, 8 * g_:8 * g_ + 8, :],
                       ps[:, 7, :].rearrange("p (h d) -> p h d", h=HPG), ALU.add).then_inc(ev["hT_ready"], 1)
                    wide_conv(TAPS[u][2], TAPS[u][3])
            v.wait_ge(ev["hT_tr"], 1)
            V.tensor_copy(view(ring, s0 + 3136, D), ps[:, 0:2, :].rearrange("p a b -> p (a b)")).then_inc(ev["hT_st"], 1)

            v.wait_ge(ev["sexp_mm"], 1)
            V.tensor_copy(flat(sdt), ps[:, 3, 0:64])
            v.drain()
            TT(sdt, sdt, xa[:, 0:KT, TP:T], ALU.mult)
            v.drain()
            for b in range(NB):
                v.wait_ge(ev["sbc_mm"], b + 1)
                sbc = ps[:, 4 + b % 2, :].rearrange("p (j n) -> p j n", j=4)
                if b:
                    v.drain()
                for g_ in range(GROUPS):
                    h = TT(sprod[:, 4 * g_:4 * g_ + 4, :], bc(sbc[:, g_, :], 1, 4), bc(sdt[:, 4 * g_:4 * g_ + 4, b], 2, P),
                           ALU.mult)
                h.then_inc(ev["sh_bx"], 1)
                wide_conv(DEC_TAPS[b], DEC_TAPS[b + 1])
                v.wait_ge(ev["sh_new"], b + 1)
                for g_ in range(GROUPS):
                    h = TT(sprod[:, 4 * g_:4 * g_ + 4, :], bc(sbc[:, 2 + g_, :], 1, 4),
                           state_in[:, b % 2, 4 * g_:4 * g_ + 4, :], ALU.mult)
                h.then_inc(ev["sh_prod"], 1)
                v.drain()
                V.tensor_reduce(yT[:, :, SEQ + b], sprod, AX, ALU.add)
            v.drain()
            TT(sdt, xa[:, 0:KT, TP:T], bc(dsk, 2, NB), ALU.mult)
            v.drain()
            TT(yT[:, :, SEQ:TN], yT[:, :, SEQ:TN], sdt, ALU.add).then_inc(ev["sy_ready"], 1)
            v.wait_ge(ev["z_sig"], 1)
            TT(flat(zT), flat(zT), flat(zsig), ALU.mult)
            v.drain()
            TT(flat(yT), flat(yT), flat(zT), ALU.mult).then_inc(ev["yg_ready"], 1)
            v.wait_ge(ev["pad_ready"], 1)
            v.wait_ge(ev["hist_ready"], 5)
            v.drain()
            for m in range(KT):
                TT(csmp[:, m], csmp[:, m], bc(cwcol[:, :, m], 1, NB), ALU.mult)
            v.drain()
            V.tensor_reduce(conv[:, :, SEQ:TN], csmp, AX, ALU.add)
            v.drain()
            TT(conv[:, :, SEQ:TN], conv[:, :, SEQ:TN], bc(gcb, 2, NB), ALU.add).then_inc(ev["conv_done"], 1)
            v.wait_ge(ev["yvar_mm"], 1)
            TS(rstd, ps[:, 4, 0:TN], 2.0 / D, EPS, ALU.mult, ALU.add)
            TS(rstd2, ps[:, 5, 0:TN], 2.0 / D, EPS, ALU.mult, ALU.add).then_inc(ev["yvar_ready"], 1)
            v.wait_ge(ev["ystd_ready"], 1)
            V.reciprocal(rstd, rstd)
            V.reciprocal(rstd2, rstd2)
            v.drain()
            for m in range(KT):
                h = STT(yT[:, m, :], yT[:, m, :], gsn[:, m:m + 1], rstd if m < 4 else rstd2, ALU.mult, ALU.mult)
            h.then_inc(ev["yn_ready"], 1)
            v.wait_ge(ev["mu_ready"], 1)
            TT(conv, conv, bc(mu, 1, KT), ALU.subtract).then_inc(ev["cent_ready"], 1)
            v.wait_ge(ev["var_mm"], 1)
            v.drain()
            TS(rstd, ps[:, 7, 0:TN], 1.0 / D, EPS, ALU.mult, ALU.add).then_inc(ev["var_ready"], 1)
            v.wait_ge(ev["std_ready"], 2)
            V.reciprocal(rstd, rstd2)
            v.drain()
            TT(conv, conv, bc(rstd, 1, KT), ALU.mult).then_inc(ev["norm_ready"], 1)
            for m in range(KT):
                v.wait_ge(ev["csig_ready"], m + 1)
                TS(conv[:, m, :], conv[:, m, :], glg[:, m:m + 1], glb[:, m:m + 1], ALU.mult, ALU.add)
            v.drain()
            TT(flat(conv), flat(conv), flat(csq), ALU.mult).then_inc(ev["conf_ready"], 1)

            v.wait_ge(ev["wo_mm"], 1)
            v.drain()
            for m in range(KT):
                V.tensor_copy(accT[:, m, :], ps[:, m, 0:TN]).then_inc(ev["acc_ready"], 1)
            V.memset(slotp, -FAR)
            V.memset(gates, 0.0)
            V.memset(ys, 0.0).then_inc(ev["y_back"], 1)
            V.memset(zero32, 0.0).then_inc(ev["ht_ready"], 1)
            V.memset(nbo, 0.0).then_inc(ev["u_read"], 1)
            v.wait_ge(ev["hsq_ready"], 1)
            TS(stat[:, 1, 0:3], stat[:, 0, 0:3], 1.0 / D, EPS, ALU.mult, ALU.add).then_inc(ev["hr_v"], 1)
            v.wait_ge(ev["hstd_ready"], 1)
            V.reciprocal(stat[:, 1, 0:3], stat[:, 2, 0:3]).then_inc(ev["hr_v"], 1)
            v.drain()
            v.wait_ge(ev["lg_mm"], 1)
            lg = ps[:, 6, 0:96].rearrange("p (j e) -> p j e", j=3)
            for j, (c, r) in enumerate(tok):
                STT(logit[0:r, j, :], lg[0:r, j, :], stat[0:r, 1, j:j + 1], brt[0:r, :], ALU.mult, ALU.add)
            v.drain()
            for j, (c, r) in enumerate(tok):
                V.max(top8[0:r, j, :], logit[0:r, j, :])
            v.drain()
            for j, (c, r) in enumerate(tok):
                V.max_index(topi[0:r, j, :], top8[0:r, j, :], logit[0:r, j, :])
                h = TS(nmax[0:r, j:j + 1], top8[0:r, j, 0:1], -1.0, None, ALU.mult)
            h.then_inc(ev["nm_ready"], 1)
            v.drain()
            for j, (c, r) in enumerate(tok):
                V.tensor_copy(topf[0:r, j, :], topi[0:r, j, 0:TOPK])
            v.wait_ge(ev["iota_ready"], 1)
            v.drain()
            for j, (c, r) in enumerate(tok):
                TT(eq[0:r], bc(iota_f[0:r, 0:NE], 1, TOPK), bc(topf[0:r, j, :], 2, NE), ALU.is_equal)
                v.drain()
                V.tensor_reduce(mask[0:r, j, :], eq[0:r].rearrange("p k e -> p e k"), AX, ALU.add)
                if j == 0:
                    v.wait_ge(ev["topexp"], 1)
                    V.reciprocal(rsum[:, 0:2], rsum[:, 0:2])
                    V.reciprocal(rsum[0:NB, 2:3], rsum[0:NB, 2:3])
                    v.drain()
                TS(topw[0:r, j, :], topw[0:r, j, :], rsum[0:r, j:j + 1], None, ALU.mult)
                v.drain()
                TT(eq[0:r], eq[0:r], bc(topw[0:r, j, :], 2, NE), ALU.mult)
                v.drain()
                h = V.tensor_reduce(gates[0:r, j, 1:NE + 1], eq[0:r].rearrange("p k e -> p e k"), AX, ALU.add)
                h.then_inc(ev["gates_ready"], 1)
                TS(tmp96[0:r, j, :], mask[0:r, j, :], FAR, -FAR, ALU.mult, ALU.add)
                v.drain()
            v.wait_ge(ev["pos_mm"], 1)
            pm = ps[:, 7, 0:128].rearrange("p (j e) -> p j e", j=4)
            for j, (c, r) in enumerate(tok):
                TT(slotp[0:r, j, 1:NE + 1], pm[0:r, j, :], tmp96[0:r, j, :], ALU.add)
            V.tensor_copy(cntf, pm[:, 3, :])
            V.memset(cnti[0:1, :], 0)
            v.drain()
            V.tensor_copy(cnti[0:1, 1:NE + 1], pm[0:1, 3, :])
            v.drain()
            V.memset(nbo, 0.0).then_inc(ev["cnt_ready"], 1)
            v.drain()

            def choose_slots(col):
                for j, (c, r) in enumerate(tok):
                    h = TS(S[0:r, j, :], iota_f[0:r, :], slotp[0:r, j, bass.ds(col, 1)], None, ALU.is_equal)
                return h

            def choose_gates(col):
                for k, io in enumerate((iota_f, iota_h)):
                    for j, (c, r) in enumerate(tok):
                        h = TS(Sg[0:r, 3 * k + j, :], io[0:r, :], slotp[0:r, j, bass.ds(col, 1)],
                               gates[0:r, j, bass.ds(col, 1)], ALU.is_equal, ALU.mult)
                return h

            def choose_bias(e):
                return V.tensor_copy(oh[0:NE, :], ident[0:NE, bass.ds(e, 1)].to_broadcast([NE, P]))

            v.wait_ge(ev["kept_out"], 64)
            choose_slots(1).then_inc(ev["s_ready"], 1)
            v.wait_ge(ev["rows_zeroed"], 1)
            choose_bias(0).then_inc(ev["oh_ready"], 1)
            TS(nbo, cntf, float(CAP), None, ALU.is_gt)
            TS(cum, cntf, float(2 * CAP), None, ALU.is_gt)
            V.memset(zero32, 0.0)
            v.drain()
            TT(nbo, nbo, cum, ALU.add)
            v.drain()
            V.tensor_tensor_scan(cum, nbo, zero32, 0.0, ALU.add, ALU.add)
            v.drain()
            for k in range(OVER):
                TS(ole[:, k, :], cum, float(k), None, ALU.is_le)
            v.drain()
            V.tensor_reduce(oe[:, 0:OVER], ole, AX, ALU.add)
            V.tensor_copy(oe[:, OVER:OVER + 1], cum[:, NE - 1:NE])
            v.drain()
            TT(ole, ole, bc(nbo, 1, OVER), ALU.mult)
            v.drain()
            V.tensor_reduce(ob, ole, AX, ALU.add)
            TS(oe[:, 0:OVER], oe[:, 0:OVER], float(NE - 1), None, ALU.min)
            v.drain()
            V.tensor_copy(otab, oe).then_inc(ev["o_tab"], 1)
            TS(ob, ob, -float(CAP), None, ALU.mult)
            for k in range(OVER):
                v.drain()
                TS(ob[:, k:k + 1], ob[:, k:k + 1], float(CAP * (k + 1)), None, ALU.add)
            v.wait_ge(ev["pt_done"], 1)
            V.tensor_copy(gT[0:NE, :], ps[0:NE, 6, 0:TN]).then_inc(ev["gt_ready"], 1)

            def take_inputs(n):
                src = ps[:, 6:8, :].rearrange("p a b -> p (a b)")
                if n == HALF:
                    return TT(xT[:, 0:4, :].rearrange("p c (h s) -> p c h s", h=2),
                              src[:, 0:512].rearrange("p (c h s) -> p c h s", c=4, h=2),
                              bc(gff.rearrange("p (h c) -> p c h", h=2), 3, HALF), ALU.mult)
                return TT(xT, src.rearrange("p (k s) -> p k s", k=KT), bc(gff, 2, CAP), ALU.mult)

            def by_width(count, what):
                with v.If(count < HALF + 1):
                    what(HALF)
                with v.Else():
                    what(CAP)

            def add_back(n):
                for m in range(KT):
                    v.wait_ge(ev["sc_done"], n + m + 1)
                    TT(accT[:, m, :], ps[:, 7 - m % 2, 0:TN], accT[:, m, :], ALU.add).then_inc(ev["acc_done"], 1)

            def swiglu(n):
                gate, up = (ps[:, b:b + 2, :].rearrange("p a b -> p (a b)") for b in (0, 2))
                v.wait_ge(ev["piece_used"], n * NP + 4)
                TS(ge, gate, LIMIT, None, ALU.min).then_inc(ev["g_ready"], 1)
                v.wait_ge(ev["piece_used"], n * NP + 8)
                TS(ue, up, LIMIT, -LIMIT, ALU.min, ALU.max).then_inc(ev["u_read"], 1)
                v.drain()
                STT(ue, ue, 1.0, ge, ALU.add, ALU.mult)
                v.drain()
                v.wait_ge(ev["sig_ready"], n + 1)
                TT(hdn, ue, sig, ALU.mult).then_inc(ev["hdn_ready"], 1)

            add_back(0)
            v.wait_ge(ev["xt_done"], 1)
            by_width(v.value_load(cnti[0:1, 1:2], min_val=0, max_val=TN),
                     lambda n: take_inputs(n).then_inc(ev["xt_ready"], 1))
            with v.Fori(0, NE) as i:
                following = v.value_load(cnti[0:1, bass.ds(i + 2, 1)], min_val=0, max_val=TN)
                v.wait_ge(ev["pt_done"], i + 1)
                choose_gates(i).then_inc(ev["sg_ready"], 1)
                v.wait_ge(ev["xg_done"], i + 1)
                choose_slots(i + 2).then_inc(ev["s_ready"], 1)
                swiglu(i)
                choose_bias(i + 1).then_inc(ev["oh_ready"], 1)
                add_back(i * 8 + 8)

                def following_inputs(n):
                    v.wait_ge(ev["xt_done"], i + 2)
                    take_inputs(n).then_inc(ev["xt_ready"], 1)

                by_width(following, following_inputs)
            v.wait_ge(ev["pt_done"], NE + 1)
            choose_gates(NE).then_inc(ev["sg_ready"], 1)
            add_back(NE * 8 + 8)

            n_over = v.value_load(otab[0:1, OVER:OVER + 1], min_val=0, max_val=OVER)
            with v.Fori(0, OVER) as j:
                with v.If(j < n_over):
                    e = v.value_load(otab[0:1, bass.ds(j, 1)], min_val=0, max_val=NE - 1)
                    v.drain()
                    TS(oslot, slotp[:, :, bass.ds(e + 1, 1)].rearrange("p j o -> p (j o)"), ob[:, bass.ds(j, 1)], None,
                       ALU.subtract)
                    v.drain()
                    for t, (c, r) in enumerate(tok):
                        TS(S[0:r, t, :], iota_f[0:r, :], oslot[0:r, t:t + 1], None, ALU.is_equal)
                        TS(Sg[0:r, t, :], iota_f[0:r, :], oslot[0:r, t:t + 1], gates[0:r, t, bass.ds(e + 1, 1)],
                           ALU.is_equal, ALU.mult)
                    choose_bias(e)
                    v.drain()
                    V.memset(zero32, 0.0).then_inc(ev["s_ready"], 1)
                    v.wait_ge(ev["xt_done"], j + NE + 2)
                    take_inputs(CAP).then_inc(ev["xt_ready"], 1)
                    swiglu(j + NE)
                    add_back(j * 8 + 8 * (NE + 2))

            v.drain()
            V.memset(zero32, 0.0).then_inc(ev["f_rd"], 1)
            v.wait_ge(ev["hsq_ready"], 2)
            TS(stat[:, 1, 0:3], stat[:, 0, 0:3], 1.0 / D, EPS, ALU.mult, ALU.add).then_inc(ev["hr_v"], 1)
            v.wait_ge(ev["hstd_ready"], 2)
            V.reciprocal(stat[:, 1, 0:3], stat[:, 2, 0:3])
            v.wait_ge(ev["late_loaded"], 32)
            v.drain()
            for j, (c, r) in enumerate(tok):
                STT(hout[0:r, j, :], ps[0:r, 2 * j:2 * j + 2, :].rearrange("p a b -> p (a b)"), stat[0:r, 1, j:j + 1],
                    gfin[0:r, :], ALU.mult, ALU.mult).then_inc(ev["f_ready"], 1)

        @block.tensor
        def _(pe):
            MM = nc.tensor.matmul

            def TR(out, in_):
                r = in_.shape[0]
                return nc.tensor.transpose(out, in_, ident[0:r, 0:r])

            def ident_at(r0, n):
                return ident[r0:r0 + n, r0:r0 + n]

            pe.wait_ge(ev["consts"], 1)
            pe.wait_ge(ev["vec_loaded"], 16 * 8)
            TR(ps[:, 0, 0:108], vrow[0:108, :]).then_inc(ev["vt_done"], 1)
            for k in range(4):
                j, h_ = k // 2, k % 2
                pe.wait_ge(ev["xs_ready"], j + 1)
                for m in range(4):
                    h = TR(ps[:, 4 + k, P * m:P * (m + 1)], xs_tok[:, j, P * (4 * h_ + m):P * (4 * h_ + m + 1)])
                h.then_inc(ev["xtr_done"], 1)
            pe.wait_ge(ev["xs_ready"], 3)
            pe.wait_ge(ev["uT_ready"], 1)
            for m in range(KT):
                h = TR(ps[:, 4, 48 * m:48 * (m + 1)], xs_tok[0:48, 2, P * m:P * (m + 1)])
            h.then_inc(ev["xtr_done"], 1)
            pe.wait_ge(ev["uT_ready"], 6)

            def w_in_tiles(first, last):
                for j in range(first, last):
                    c, m = j // 4, j % 4
                    if m == 0:
                        pe.wait_ge(win_landed[c % 6], 16 * (c // 6 + 1))
                    if j >= X_TILES:
                        pe.wait_ge(ev["evac_done"], j - 1)
                    elif j >= 4:
                        pe.wait_ge(ev["evac_done"], j - 3)
                    lo = META if CHUNKS[c][1] == "z" else 0
                    for k in range(KT):
                        h = MM(ps[:, tile_bank(j), 0:T - lo], win(c)[:, k, P * m:P * (m + 1)], uT[:, k, lo:T],
                               start=(k == 0), stop=(k == KT - 1))
                    h.then_inc(ev["win_done"], 1)
                    if m == 3:
                        pe.drain().then_inc(ev["win_used"], 1)

            pe.wait_ge(ev["vcol_ready"], 1)
            w_in_tiles(0, 4)
            pe.wait_ge(ev["wdt_loaded"], 16)
            for g_, (c, r) in enumerate(((META, P), (META + P, P), (TP, NB), (0, META))):
                for k in range(KT):
                    h = MM(ps[0:r, 5, HEADS * g_:HEADS * (g_ + 1)], uT[:, k, c:c + r], wdt[:, k, :],
                           start=(k == 0), stop=(k == KT - 1))
            h.then_inc(ev["dt_mm"], 1)
            pe.wait_ge(ev["bias_loaded"], 32)
            for j in range(2):
                h = TR(ps[:, 7, 124 * j:124 * (j + 1)], cwrow[0:124, j, :])
            h.then_inc(ev["cw_tr"], 1)
            pe.wait_ge(ev["histx_loaded"], 16)
            for m in range(XT_):
                h = TR(ps[:, 6, 24 * m:24 * (m + 1)], hist_x[0:24, P * m:P * (m + 1)])
            h.then_inc(ev["htr_done"], 1)
            w_in_tiles(4, 8)
            pe.wait_ge(ev["hist_loaded"], 32)
            pe.wait_ge(ev["dt_v"], 1)
            pe.wait_ge(ev["hist_ready"], 1)
            pe.wait_ge(ev["vcol_ready"], 2)
            for k in range(4):
                j, h_ = k // 2, k % 2
                for m in range(4):
                    h = TR(ps[:, 4 + k, 120 * m:120 * (m + 1)], hist_c[0:120, j, P * (4 * h_ + m):P * (4 * h_ + m + 1)])
                h.then_inc(ev["htr_done"], 1)
            w_in_tiles(8, X_TILES)
            pe.wait_ge(ev["hist_ready"], 5)
            pe.wait_ge(ev["evac_done"], X_TILES)
            for m in range(XT_):
                h = TR(ps[0:11, 5 + m // 4, P * (m % 4):P * (m % 4 + 1)], xraw[:, m, 3 + T - 11:3 + T])
            h.then_inc(ev["xst_tr"], 1)

            pe.wait_ge(ev["dt_ready"], 1)
            pe.wait_ge(ev["xst_ready"], 1)
            for c in range(2):
                MM(ps[:, 6, HEADS * c:HEADS * (c + 1)], tri, dta[:, c, :], start=True, stop=True)
            MM(ps[0:META, 6, 32:48], tri[0:META, 0:META], dta[0:META, 3, :], start=True, stop=True)
            MM(ps[0:META, 6, 48:64], ones[0:META, 0:META], dta[0:META, 3, :], start=True, stop=True
               ).then_inc(ev["acum_mm"], 1)

            def chunk_rows(n, c, r):
                pe.wait_ge(ev["xa_ready"], 2)
                if n:
                    pe.wait_ge(ev["xdt_ready"], n)
                if n:
                    pe.wait_ge(ev["hT_ready"], 3 if n == 1 else 5)
                for m in range(KT):
                    TR(ps[0:r, 1 + m // 4, P * (m % 4):P * (m % 4 + 1)], xa[:, m, c:c + r])
                for g_ in range(GROUPS):
                    h = TR(ps[0:r, 7, P * g_:P * (g_ + 1)], xa[:, KT + g_, c:c + r])
                h.then_inc(ev["xtok_mm"], 1)

            w_in_tiles(X_TILES, X_TILES + 4)
            chunk_rows(0, 0, META)
            w_in_tiles(X_TILES + 4, X_TILES + 5)
            pe.wait_ge(ev["xdt_ready"], 1)
            for g_ in range(GROUPS):
                pe.wait_ge(ev["hT_ready"], 1 + g_)
                MM(ps[:, 7, :], btok[0:META, g_, :], xdec[0:META, 8 * g_:8 * g_ + 8, :].rearrange("p h d -> p (h d)"),
                   start=True, stop=True).then_inc(ev["st_mm"], 1)
            w_in_tiles(X_TILES + 5, UNIT_TILES[0])
            for c in range(2):
                cs = META + c * P
                chunk_rows(1 + c, cs, P)
                for g_ in range(GROUPS):
                    u = 2 * c + g_
                    pe.wait_ge(ev["xdt_ready"], 2 + c)
                    pe.wait_ge(ev["hT_ready"], 3 + u)
                    MM(ps[:, 7, 384:512], xa[:, KT + g_, cs:cs + P], xa[:, KT + 2 + g_, cs:cs + P], start=True, stop=True
                       ).then_inc(ev["cb_mm"], 1)
                    if u:
                        pe.wait_ge(ev["ce_ready"], u)
                    for k in range(HPG):
                        h = MM(ps[:, 4 + k // 4, P * (k % 4):P * (k % 4 + 1)],
                               dta[:, c, 8 * g_ + k:8 * g_ + k + 1].to_broadcast([P, P]), tri, start=True, stop=True)
                    h.then_inc(ev["acb_mm"], 1)
                    w_in_tiles(UNIT_TILES[u], UNIT_END[u])
                    pe.wait_ge(ev["m_ready"], u + 1)
                    pe.wait_ge(ev["hT_ready"], 3 + u)
                    pe.wait_ge(ev["meta_v"], 1)
                    if u:
                        pe.wait_ge(ev["y_ready"], u)
                    for k in range(HPG):
                        r0 = 64 * (k % 2)
                        dst = ps[r0:r0 + 64, 6, P * (k // 2):P * (k // 2 + 1)]
                        MM(dst, xdt[:, 8 * g_ + k, :], Mh[:, k, :], start=True, stop=False)
                        h = MM(dst, hT[:, 8 * g_ + k, :], Ce[:, k, :], start=False, stop=True)
                    h.then_inc(ev["y_mm"], 1)
                    pe.wait_ge(ev["xdec_ready"], u + 1)
                    MM(ps[:, 7, :], btok[:, g_, :], xdec[:, 8 * g_:8 * g_ + 8, :].rearrange("p h d -> p (h d)"),
                       start=True, stop=True).then_inc(ev["st_mm"], 1)
                    w_in_tiles(UNIT_END[u], UNIT_TILES[u + 1] if u < 3 else TILES)
            pe.wait_ge(ev["hT_ready"], 6)
            pe.wait_ge(ev["evac_done"], TILES)
            pe.wait_ge(ev["hT_ready"], 7)
            for m in range(KT):
                h = TR(ps[:, m // 4, P * (m % 4):P * (m % 4 + 1)], hT[:, 2 * m:2 * m + 2, :].rearrange("p h d -> p (h d)"))
            h.then_inc(ev["hT_tr"], 1)

            pe.wait_ge(ev["glu_done"], 8)
            pe.wait_ge(ev["y_ready"], 4)
            for m in range(KT):
                h = TR(ps[0:38, 6 + m // 4, P * (m % 4):P * (m % 4 + 1)], cbuf[:, m, 30 + T - 38:30 + T])
            h.then_inc(ev["cst_tr"], 1)
            for which, src in enumerate((dtt, dta)):
                for hd in range(HEADS):
                    r0, m = 64 * (hd % 2), hd // 2
                    h = MM(ps[r0:r0 + 64, 3 - which, NB * m:NB * (m + 1)],
                           src[0:NB, 2, hd:hd + 1].to_broadcast([NB, HD]), ident[0:NB, 0:NB], start=True, stop=True)
            h.then_inc(ev["sexp_mm"], 1)
            pe.wait_ge(ev["ce_ready"], 4)
            for b in range(NB):
                if b >= 2:
                    pe.wait_ge(ev["sh_prod"], b - 1)
                for j in range(4):
                    h = MM(ps[:, 4 + b % 2, P * j:P * (j + 1)], xa[:, KT + j, TP + b:TP + b + 1].to_broadcast([P, P]),
                           ident, start=True, stop=True)
                h.then_inc(ev["sbc_mm"], 1)
            pe.wait_ge(ev["ysq_ready"], 1)
            pe.wait_ge(ev["sh_prod"], NB)
            for g_ in range(GROUPS):
                for m in range(4):
                    h = MM(ps[:, 4 + g_, 0:TN], ones, ysq[:, 4 * g_ + m, :], start=(m == 0), stop=(m == 3))
            h.then_inc(ev["yvar_mm"], 1)

            pe.wait_ge(ev["conv_done"], 1)
            pe.wait_ge(ev["cst_ready"], 1)
            for m in range(KT):
                h = MM(ps[:, 6, 0:TN], ones, conv[:, m, :], start=(m == 0), stop=(m == KT - 1))
            h.then_inc(ev["mean_mm"], 1)

            def w_out_tiles(first, last):
                for m in range(first, last):
                    for k in range(KT):
                        MM(ps[:, m, 0:TN], wout(k // 2)[:, k % 2, P * m:P * (m + 1)], yT[:, k, :],
                           start=(k == 0), stop=False, skip_group_check=True)

            pe.wait_ge(ev["hT_st"], 1)
            pe.wait_ge(ev["sdec_ready"], 1)
            pe.wait_ge(ev["yvar_ready"], 1)
            pe.wait_ge(ev["yn_ready"], 1)
            pe.wait_ge(ev["wo_y_landed"], 64)
            w_out_tiles(0, 4)
            pe.wait_ge(ev["csq_ready"], 1)
            for m in range(KT):
                h = MM(ps[:, 7, 0:TN], ones, csq[:, m, :], start=(m == 0), stop=(m == KT - 1))
            h.then_inc(ev["var_mm"], 1)
            w_out_tiles(4, 6)
            pe.wait_ge(ev["mu_ready"], 1)
            pe.wait_ge(ev["var_ready"], 1)
            w_out_tiles(6, 8)
            pe.drain().then_inc(ev["wo_used"], 1)
            pe.wait_ge(ev["conf_ready"], 1)
            pe.wait_ge(ev["wo_conf_landed"], 64)
            for k in range(KT):
                for m in range(KT):
                    MM(ps[:, m, 0:TN], wout(4 + k // 2)[:, k % 2, P * m:P * (m + 1)], conv[:, k, :],
                       start=False, stop=False, skip_group_check=True)
            pe.drain().then_inc(ev["wo_used"], 1)
            for m in range(KT):
                for j, (c, r) in enumerate(tok):
                    h = MM(ps[:, m, c:c + r], x_tok[0:r, j, P * m:P * (m + 1)], ident[0:r, 0:r],
                           start=False, stop=(j == 2), skip_group_check=True)
            h.then_inc(ev["wo_mm"], 1)

            pe.wait_ge(ev["acc_ready"], 8)
            for j, (c, r) in enumerate(tok):
                for k in range(KT):
                    h = MM(ps[0:r, 6, NE * j:NE * (j + 1)], accT[:, k, c:c + r], wr[:, k, :],
                           start=(k == 0), stop=(k == KT - 1))
            h.then_inc(ev["lg_mm"], 1)
            for j, (c, r) in enumerate(tok):
                for m in range(KT):
                    h = TR(ps[0:r, 2 * j + m // 4, P * (m % 4):P * (m % 4 + 1)], accT[:, m, c:c + r])
                h.then_inc(ev["h_tr"], 1)
            pe.wait_ge(ev["gates_ready"], 3)
            for j, (c, r) in enumerate(tok):
                for i_ in range(j):
                    MM(ps[0:r, 7, NE * j:NE * (j + 1)], ones[:, 0:r], mask[:, i_, :], start=(i_ == 0), stop=False)
                MM(ps[0:r, 7, NE * j:NE * (j + 1)], tri_s[0:r, 0:r], mask[0:r, j, :], start=(j == 0), stop=True)
            for j, (c, r) in enumerate(tok):
                h = MM(ps[:, 7, 96:128], ones[0:r, :], mask[0:r, j, :], start=(j == 0), stop=(j == 2))
            h.then_inc(ev["pos_mm"], 1)
            for j, (c, r) in enumerate(tok):
                h = TR(ps[0:NE, 6, c:c + r], gates[0:r, j, 1:NE + 1])
            h.then_inc(ev["pt_done"], 1)

            def halves(n, bank):
                if n == HALF:
                    return [ps[HALF * h:HALF * (h + 1), bank, :] for h in range(2)]
                return [ps[:, bank + h, :] for h in range(2)]

            def gather(n):
                for j, (c, r) in enumerate(tok):
                    for h_, dst in enumerate(halves(n, 4)):
                        h = MM(dst, S[0:r, j, 0:n], xn[0:r, j, 512 * h_:512 * (h_ + 1)], start=(j == 0), stop=(j == 2))
                h.then_inc(ev["xg_done"], 1)

            def turn(src, n, bank, done):
                for c in range(4 if n == HALF else 8):
                    h = TR(ps[:, bank + c // 4, P * (c % 4):P * (c % 4 + 1)], src[:, P * c:P * (c + 1)])
                h.then_inc(done, 1)

            def bias(n, rows, bank):
                for h_, dst in enumerate(halves(n, bank)):
                    MM(dst, oh[:, 0:n], rows[:, 512 * h_:512 * (h_ + 1)], start=True, stop=False, skip_group_check=True)

            def products(n, first, src, bank, i16, fresh=False):
                for p in range(first, first + 4):
                    pe.wait_ge(landed[p], i16)
                    for k in range(2):
                        kk = 2 * (p - first) + k
                        x = src[:, kk % 4, HALF * (kk // 4):HALF * (kk // 4 + 1)] if n == HALF else src[:, kk, :]
                        for h_, dst in enumerate(halves(n, bank)):
                            h = MM(dst, x, piece(p)[:, k, 512 * h_:512 * (h_ + 1)], start=(fresh and kk == 0),
                                   stop=(kk == KT - 1), skip_group_check=True)
                    h.then_inc(ev["piece_used"], 1)

            def scatter(lhs, rhs, n):
                for m in range(KT):
                    if m >= 2:
                        pe.wait_ge(ev["acc_done"], n + m - 1)
                    MM(ps[:, 7 - m % 2, 0:TN], lhs(m), rhs(m), start=True, stop=True).then_inc(ev["sc_done"], 1)

            def turn_slots():
                for k in range(2):
                    for j, (c, r) in enumerate(tok):
                        h = TR(ps[:, 6 + k, c:c + r], Sg[0:r, 3 * k + j, :])
                h.then_inc(ev["pt_done"], 1)

            def scatter_rows(n, i8):
                if n == HALF:
                    scatter(lambda m: ys[:, P * (m % 4):P * (m % 4 + 1)], lambda m: Pm[:, m // 4, :], i8)
                else:
                    scatter(lambda m: ys[:, P * m:P * (m + 1)], lambda m: Pm[:, 0, :], i8)

            def by_width(count, what):
                with pe.If(count < HALF + 1):
                    what(HALF)
                with pe.Else():
                    what(CAP)

            def count_of(i):
                return pe.value_load(cnti[0:1, bass.ds(i, 1)], min_val=0, max_val=TN)

            pe.wait_ge(ev["cnt_ready"], 1)
            pe.wait_ge(ev["s_ready"], 1)
            pe.wait_ge(ev["xn_ready"], 3)
            first = count_of(1)
            by_width(first, gather)
            pe.wait_ge(ev["gt_ready"], 1)
            pe.wait_ge(ev["late_loaded"], 16)
            scatter(lambda m: bdn[0:NE, P * m:P * (m + 1)], lambda m: gT[0:NE, :], 0)
            pe.wait_ge(ev["xg_out"], 1)
            pe.wait_ge(ev["acc_done"], 8)
            by_width(first, lambda n: turn(xg, n, 6, ev["xt_done"]))
            pe.wait_ge(ev["rows_loaded"], 32)
            with pe.Fori(0, NE) as i:
                former, count, following = count_of(i), count_of(i + 1), count_of(i + 2)
                pe.wait_ge(ev["xt_ready"], i + 1)
                pe.wait_ge(ev["oh_ready"], i + 1)
                pe.wait_ge(ev["ht_ready"], i + 1)
                pe.wait_ge(ev["u_read"], i + 1)

                def gate_up(n):
                    bias(n, bg_rows, 0)
                    products(n, 0, xT, 0, i * 16 + 16)
                    bias(n, bu_rows, 2)
                    products(n, 4, xT, 2, i * 16 + 16)

                by_width(count, gate_up)
                pe.wait_ge(ev["s_ready"], i + 2)
                pe.wait_ge(ev["y_back"], i + 1)
                by_width(following, gather)
                pe.wait_ge(ev["sg_ready"], i + 1)
                pe.wait_ge(ev["acc_done"], i * 8 + 8)
                turn_slots()
                pe.wait_ge(ev["p_ready"], i + 1)
                by_width(former, lambda n: scatter_rows(n, i * 8 + 8))
                pe.wait_ge(ev["hdn_ready"], i + 1)
                by_width(count, lambda n: turn(hdn, n, 0, ev["ht_done"]))
                pe.wait_ge(ev["xg_out"], i + 2)
                pe.wait_ge(ev["acc_done"], i * 8 + 16)
                by_width(following, lambda n: turn(xg, n, 6, ev["xt_done"]))
                pe.wait_ge(ev["ht_ready"], i + 2)
                by_width(count, lambda n: products(n, 8, hT_e, 4, i * 16 + 16, fresh=True))
            pe.wait_ge(ev["y_back"], NE + 1)
            pe.wait_ge(ev["sg_ready"], NE + 1)
            pe.wait_ge(ev["xt_ready"], NE + 1)
            turn_slots()
            pe.wait_ge(ev["p_ready"], NE + 1)
            by_width(count_of(NE), lambda n: scatter_rows(n, NE * 8 + 8))

            pe.wait_ge(ev["o_tab"], 1)
            pe.wait_ge(ev["acc_done"], NE * 8 + 16)
            n_over = pe.value_load(otab[0:1, OVER:OVER + 1], min_val=0, max_val=OVER)
            with pe.Fori(0, OVER) as j:
                with pe.If(j < n_over):
                    pe.wait_ge(ev["s_ready"], j + NE + 2)
                    gather(CAP)
                    pe.wait_ge(ev["xg_out"], j + NE + 2)
                    turn(xg, CAP, 6, ev["xt_done"])
                    pe.wait_ge(ev["xt_ready"], j + NE + 2)
                    bias(CAP, bg_rows, 0)
                    products(CAP, 0, xT, 0, j * 16 + 16 * (NE + 1))
                    pe.wait_ge(ev["u_read"], j + NE + 1)
                    bias(CAP, bu_rows, 2)
                    products(CAP, 4, xT, 2, j * 16 + 16 * (NE + 1))
                    pe.wait_ge(ev["hdn_ready"], j + NE + 1)
                    turn(hdn, CAP, 0, ev["ht_done"])
                    pe.wait_ge(ev["ht_ready"], j + NE + 2)
                    products(CAP, 8, hT_e, 4, j * 16 + 16 * (NE + 1), fresh=True)
                    turn_slots()
                    pe.wait_ge(ev["y_back"], j + NE + 2)
                    pe.wait_ge(ev["p_ready"], j + NE + 2)
                    scatter_rows(CAP, j * 8 + 8 * (NE + 2))
                    pe.wait_ge(ev["acc_done"], j * 8 + 8 * (NE + 3))

            pe.wait_ge(ev["f_rd"], 1)
            for j, (c, r) in enumerate(tok):
                for m in range(KT):
                    h = TR(ps[0:r, 2 * j + m // 4, P * (m % 4):P * (m % 4 + 1)], accT[:, m, c:c + r])
                h.then_inc(ev["h_tr"], 1)


_INS = ["x_prompt", "x_sample", "state_ssm", "state_ssd_conv", "state_conf_conv", "meta_tokens", "g_mix", "w_in",
        "conv_ssd_w", "conv_ssd_b", "dt_bias", "a_log", "d_skip", "g_ssd_norm", "conv_conf_w", "conv_conf_b",
        "ln_conf_g", "ln_conf_b", "w_out", "g_ffn", "w_router", "b_router", "w_gate", "b_gate", "w_up", "b_up",
        "w_down", "b_down", "g_final"]
_OUTS = {"y_p": (1, SEQ, D), "y_s": (NB, 1, D), "ssm_p": (1, 1, HEADS, HD, NST), "ssd_p": (1, 1, SW - 1, XBC),
         "conf_p": (1, 1, CW - 1, D), "ssm_s": (1, NB, HEADS, HD, NST), "ssd_s": (1, NB, SW - 1, XBC),
         "conf_s": (1, NB, CW - 1, D)}


def kernel(**inputs):
    import numpy as _np
    import concourse.bacc as _bacc
    from concourse import mybir as _mybir
    from concourse.bass_utils import run_bass_kernel_spmd as _run

    nc = _bacc.Bacc("TRN2", target_bir_lowering=False, num_devices=1)
    arrays, ins, outs = {}, {}, {}
    for name in _INS:
        a = _np.ascontiguousarray(inputs[name])
        arrays[f"in_{name}"] = a
        ins[name] = nc.dram_tensor(f"in_{name}", a.shape, _mybir.dt.from_np(a.dtype), kind="ExternalInput").ap()
    for name, shape in _OUTS.items():
        outs[name] = nc.dram_tensor(f"out_{name}", shape, F32, kind="ExternalOutput").ap()
    build(nc, ins, outs)
    r = _run(nc, [arrays], core_ids=[0])
    return tuple(r.results[0][f"out_{name}"] for name in _OUTS)
```
